# Optimizing a Trainium2 kernel written in Bass

```python
import jax, jax.numpy as jnp
from jax import lax
import numpy as np

D_MODEL = 1024
BATCH = 1
SEQ = 256
DEPTH = 2
DEC_BATCH = 1
DEC_SEQ = 64
PAST_LEN = 128

CHUNK = 64
WINDOW = 128
HEAD_DIM = 64
SWA_HEADS = 8
SWA_KV_HEADS = 2
FOX_HEADS = 8
D_FF = 2816
CONV_W = 3
ROPE_THETA = 10000.0
Q_BLOCK = 128
LN_EPS = 1e-5
NEG = -1e30
ALPHA = (2.0 * DEPTH) ** 0.25
BETA = (8.0 * DEPTH) ** -0.25
SWA_Q = SWA_HEADS * HEAD_DIM
SWA_KV = SWA_KV_HEADS * HEAD_DIM
FOX_W = FOX_HEADS * HEAD_DIM
SIZES = [SWA_Q, SWA_KV, SWA_KV, FOX_W, FOX_W, FOX_W, FOX_HEADS, D_MODEL, D_MODEL]
SPLIT_AT = [int(v) for v in np.cumsum(SIZES)[:-1]]
D_IN = int(sum(SIZES))
V_COLS = [(SWA_Q + SWA_KV, SWA_Q + 2 * SWA_KV), (SWA_Q + 2 * SWA_KV + 2 * FOX_W, SWA_Q + 2 * SWA_KV + 3 * FOX_W)]
SCALE = HEAD_DIM ** -0.5

kernel_name = 'hybrid_swa_sink_fox_convffn_stream_step'

def layer_norm(x, g, b):
    xf = x.astype(jnp.float32)
    mu = xf.mean(-1, keepdims=True)
    var = jnp.square(xf - mu).mean(-1, keepdims=True)
    return ((xf - mu) * lax.rsqrt(var + LN_EPS) * g.astype(jnp.float32) + b.astype(jnp.float32)).astype(x.dtype)

def rope(x, pos):
    half = HEAD_DIM // 2
    inv = 1.0 / (ROPE_THETA ** (jnp.arange(half, dtype=jnp.float32) / half))
    ang = pos.astype(jnp.float32)[:, None] * inv[None, :]
    cos = jnp.cos(ang)[None, :, None, :]
    sin = jnp.sin(ang)[None, :, None, :]
    xf = x.astype(jnp.float32)
    x1, x2 = xf[..., :half], xf[..., half:]
    return jnp.concatenate([x1 * cos - x2 * sin, x1 * sin + x2 * cos], -1).astype(x.dtype)

def sink_softmax(s, sink_b):
    sink_b = sink_b.astype(jnp.float32)
    m = jnp.maximum(s.max(-1, keepdims=True), sink_b)
    e = jnp.exp(s - m)
    return e / (e.sum(-1, keepdims=True) + jnp.exp(sink_b - m))

def project_in(x, w_in, b_f):
    B, T = x.shape[:2]
    z = jnp.einsum('btd,de->bte', x, w_in)
    qa, ka, va, qb, kb, vb, fz, ga, gb = jnp.split(z, SPLIT_AT, axis=-1)
    hd = lambda a, h: a.reshape(B, T, h, HEAD_DIM)
    logf = jax.nn.log_sigmoid((fz + b_f).astype(jnp.float32))
    return (hd(qa, SWA_HEADS), hd(ka, SWA_KV_HEADS), hd(va, SWA_KV_HEADS),
            hd(qb, FOX_HEADS), hd(kb, FOX_HEADS), hd(vb, FOX_HEADS), logf, ga, gb)

def swa_prompt(q, k, v, sink):
    B, T = q.shape[:2]
    nc = T // CHUNK
    g = SWA_HEADS // SWA_KV_HEADS
    nb = WINDOW // CHUNK
    qc = q.reshape(B, nc, CHUNK, SWA_KV_HEADS, g, HEAD_DIM)

    def band(a):
        ac = a.reshape(B, nc, CHUNK, SWA_KV_HEADS, HEAD_DIM)
        pad = jnp.pad(ac, ((0, 0), (nb, 0), (0, 0), (0, 0), (0, 0)))
        return jnp.concatenate([pad[:, j:j + nc] for j in range(nb + 1)], axis=2)

    kb, vb = band(k), band(v)
    s = jnp.einsum('bcqkgd,bcskd->bckgqs', qc, kb).astype(jnp.float32) * SCALE
    blk = jnp.arange(nc)[:, None] - nb + jnp.arange(nb + 1)[None, :]
    valid = jnp.repeat(blk >= 0, CHUNK, axis=1)
    s = jnp.where(valid[None, :, None, None, None, :], s, NEG)
    p = sink_softmax(s, sink.reshape(SWA_KV_HEADS, g)[None, None, :, :, None, None])
    o = jnp.einsum('bckgqs,bcskd->bcqkgd', p.astype(v.dtype), vb)
    return o.reshape(B, T, SWA_Q)

def swa_sample(q, k_all, v_all, sink):
    B, T = q.shape[:2]
    g = SWA_HEADS // SWA_KV_HEADS
    qg = q.reshape(B, T, SWA_KV_HEADS, g, HEAD_DIM)
    s = jnp.einsum('bqkgd,bskd->bkgqs', qg, k_all).astype(jnp.float32) * SCALE
    p = sink_softmax(s, sink.reshape(SWA_KV_HEADS, g)[None, :, :, None, None])
    o = jnp.einsum('bkgqs,bskd->bqkgd', p.astype(v_all.dtype), v_all)
    return o.reshape(B, T, SWA_Q)

def fox_prompt(q, k, v, logf):
    B, T = q.shape[:2]
    Ft = jnp.cumsum(logf, axis=1).transpose(0, 2, 1)
    kpos = jnp.arange(T)

    def block(i):
        qs = lax.dynamic_slice_in_dim(q, i * Q_BLOCK, Q_BLOCK, axis=1)
        Fq = lax.dynamic_slice_in_dim(Ft, i * Q_BLOCK, Q_BLOCK, axis=2)
        s = jnp.einsum('bqhd,bshd->bhqs', qs, k).astype(jnp.float32) * SCALE
        s = s + Fq[..., :, None] - Ft[..., None, :]
        qpos = i * Q_BLOCK + jnp.arange(Q_BLOCK)
        s = jnp.where(kpos[None, :] <= qpos[:, None], s, NEG)
        p = jax.nn.softmax(s, axis=-1)
        return jnp.einsum('bhqs,bshd->bqhd', p.astype(v.dtype), v)

    o = lax.map(block, jnp.arange(T // Q_BLOCK))
    return o.transpose(1, 0, 2, 3, 4).reshape(B, T, FOX_W)

def fox_sample(q, k_all, v_all, logf_all, past):
    B, T = q.shape[:2]
    Ft = jnp.cumsum(logf_all, axis=1).transpose(0, 2, 1)
    s = jnp.einsum('bqhd,bshd->bhqs', q, k_all).astype(jnp.float32) * SCALE
    s = s + Ft[..., past:, None] - Ft[..., None, :]
    kpos = jnp.arange(k_all.shape[1])
    qpos = past + jnp.arange(T)
    s = jnp.where(kpos[None, :] <= qpos[:, None], s, NEG)
    p = jax.nn.softmax(s, axis=-1)
    o = jnp.einsum('bhqs,bshd->bqhd', p.astype(v_all.dtype), v_all)
    return o.reshape(B, T, FOX_W)

def merge_out(oa, ob, ga, gb, w_pa, w_pb, w_o):
    ya = jnp.einsum('bte,ed->btd', oa, w_pa)
    yb = jnp.einsum('bte,ed->btd', ob, w_pb)
    m = jax.nn.sigmoid(ga) * ya + jax.nn.sigmoid(gb) * yb
    return jnp.einsum('btd,de->bte', m, w_o)

def conv_ffn(x, a_prev, w_gate, w_up, conv_w, conv_b, w_down):
    T = x.shape[1]
    a = jnp.einsum('btd,df->btf', x, w_gate)
    u = jnp.einsum('btd,df->btf', x, w_up)
    ap = jnp.concatenate([a_prev.astype(a.dtype), a], axis=1)
    c = conv_b + sum(ap[:, j:j + T] * conv_w[j] for j in range(CONV_W))
    h = jax.nn.gelu(c) * u
    return jnp.einsum('btf,fd->btd', h, w_down), ap[:, -(CONV_W - 1):]

def setup_inputs(seed: int = 0) -> dict:
    key = jax.random.key(seed)
    ks = jax.random.split(key, 32)
    f32 = jnp.float32
    nrm = lambda k, shape, s: jax.random.normal(k, shape, f32) * s
    swa_rows = min(WINDOW, PAST_LEN)
    col_scale = jnp.ones((D_IN,), f32)
    for lo, hi in V_COLS:
        col_scale = col_scale.at[lo:hi].set(BETA)
    return {
        'x_prompt': nrm(ks[0], (BATCH, SEQ, D_MODEL), 1.0),
        'x_sample': nrm(ks[1], (DEC_BATCH, DEC_SEQ, D_MODEL), 1.0),
        'cache_swa_k': nrm(ks[2], (DEPTH, DEC_BATCH, swa_rows, SWA_KV_HEADS, HEAD_DIM), 1.0),
        'cache_swa_v': nrm(ks[3], (DEPTH, DEC_BATCH, swa_rows, SWA_KV_HEADS, HEAD_DIM), 1.0),
        'cache_fox_k': nrm(ks[4], (DEPTH, DEC_BATCH, PAST_LEN, FOX_HEADS, HEAD_DIM), 1.0),
        'cache_fox_v': nrm(ks[5], (DEPTH, DEC_BATCH, PAST_LEN, FOX_HEADS, HEAD_DIM), 1.0),
        'cache_fox_logf': jax.nn.log_sigmoid(1.0 + nrm(ks[6], (DEPTH, DEC_BATCH, PAST_LEN, FOX_HEADS), 1.0)),
        'state_conv': nrm(ks[7], (DEPTH, DEC_BATCH, CONV_W - 1, D_FF), 1.0),
        'w_in': nrm(ks[8], (DEPTH, D_MODEL, D_IN), D_MODEL ** -0.5) * col_scale,
        'b_f': 1.0 + nrm(ks[9], (DEPTH, FOX_HEADS), 0.1),
        'attn_sink': nrm(ks[10], (DEPTH, SWA_HEADS), 0.1),
        'w_pa': nrm(ks[11], (DEPTH, SWA_Q, D_MODEL), SWA_Q ** -0.5),
        'w_pb': nrm(ks[12], (DEPTH, FOX_W, D_MODEL), FOX_W ** -0.5),
        'w_o': nrm(ks[13], (DEPTH, D_MODEL, D_MODEL), D_MODEL ** -0.5) * BETA,
        'ln1_g': 1.0 + nrm(ks[14], (DEPTH, D_MODEL), 0.02),
        'ln1_b': nrm(ks[15], (DEPTH, D_MODEL), 0.02),
        'w_gate': nrm(ks[16], (DEPTH, D_MODEL, D_FF), D_MODEL ** -0.5),
        'w_up': nrm(ks[17], (DEPTH, D_MODEL, D_FF), D_MODEL ** -0.5) * BETA,
        'conv_w': nrm(ks[18], (DEPTH, CONV_W, D_FF), CONV_W ** -0.5),
        'conv_b': nrm(ks[19], (DEPTH, D_FF), 0.01),
        'w_down': nrm(ks[20], (DEPTH, D_FF, D_MODEL), D_FF ** -0.5) * BETA,
        'ln2_g': 1.0 + nrm(ks[21], (DEPTH, D_MODEL), 0.02),
        'ln2_b': nrm(ks[22], (DEPTH, D_MODEL), 0.02),
    }

def reference(x_prompt, x_sample, cache_swa_k, cache_swa_v, cache_fox_k, cache_fox_v, cache_fox_logf, state_conv,
              w_in, b_f, attn_sink, w_pa, w_pb, w_o, ln1_g, ln1_b, w_gate, w_up, conv_w, conv_b, w_down, ln2_g, ln2_b):
    xp, xs = x_prompt, x_sample
    Bp, Tp = xp.shape[:2]
    Ts = xs.shape[1]
    past = cache_fox_k.shape[2]
    swa_rows_p = min(WINDOW, Tp)
    swa_rows_s = cache_swa_k.shape[2]
    pos_p = jnp.arange(Tp)
    pos_s = past + jnp.arange(Ts)
    p_sk, p_sv, p_fk, p_fv, p_fl, p_cv = [], [], [], [], [], []
    s_sk, s_sv, s_fk, s_fv, s_fl, s_cv = [], [], [], [], [], []
    for l in range(DEPTH):
        qa, ka, va, qb, kb, vb, lf, ga, gb = project_in(xp, w_in[l], b_f[l])
        qa, ka = rope(qa, pos_p), rope(ka, pos_p)
        oa = swa_prompt(qa, ka, va, attn_sink[l])
        ob = fox_prompt(qb, kb, vb, lf)
        y = merge_out(oa, ob, ga, gb, w_pa[l], w_pb[l], w_o[l])
        xp = layer_norm(ALPHA * xp + y, ln1_g[l], ln1_b[l])
        f, cst = conv_ffn(xp, jnp.zeros((Bp, CONV_W - 1, D_FF), xp.dtype), w_gate[l], w_up[l], conv_w[l], conv_b[l], w_down[l])
        xp = layer_norm(ALPHA * xp + f, ln2_g[l], ln2_b[l])
        p_sk.append(ka[:, Tp - swa_rows_p:])
        p_sv.append(va[:, Tp - swa_rows_p:])
        p_fk.append(kb)
        p_fv.append(vb)
        p_fl.append(lf)
        p_cv.append(cst)
        qa, ka, va, qb, kb, vb, lf, ga, gb = project_in(xs, w_in[l], b_f[l])
        qa, ka = rope(qa, pos_s), rope(ka, pos_s)
        ka_all = jnp.concatenate([cache_swa_k[l].astype(ka.dtype), ka], axis=1)
        va_all = jnp.concatenate([cache_swa_v[l].astype(va.dtype), va], axis=1)
        oa = swa_sample(qa, ka_all, va_all, attn_sink[l])
        kb_all = jnp.concatenate([cache_fox_k[l].astype(kb.dtype), kb], axis=1)
        vb_all = jnp.concatenate([cache_fox_v[l].astype(vb.dtype), vb], axis=1)
        lf_all = jnp.concatenate([cache_fox_logf[l].astype(jnp.float32), lf], axis=1)
        ob = fox_sample(qb, kb_all, vb_all, lf_all, past)
        y = merge_out(oa, ob, ga, gb, w_pa[l], w_pb[l], w_o[l])
        xs = layer_norm(ALPHA * xs + y, ln1_g[l], ln1_b[l])
        f, cst = conv_ffn(xs, state_conv[l], w_gate[l], w_up[l], conv_w[l], conv_b[l], w_down[l])
        xs = layer_norm(ALPHA * xs + f, ln2_g[l], ln2_b[l])
        s_sk.append(ka_all[:, ka_all.shape[1] - swa_rows_s:])
        s_sv.append(va_all[:, va_all.shape[1] - swa_rows_s:])
        s_fk.append(kb)
        s_fv.append(vb)
        s_fl.append(lf)
        s_cv.append(cst)
    st = jnp.stack
    return (xp, xs,
            st(p_sk), st(p_sv), st(p_fk), st(p_fv), st(p_fl), st(p_cv),
            st(s_sk), st(s_sv), st(s_fk), st(s_fv), st(s_fl), st(s_cv))


_drawn_inputs = setup_inputs


def setup_inputs(seed=0):
    import zlib

    import numpy as np

    out = dict(_drawn_inputs(seed))
    spreads = {}
    factors = {'cache_fox_k': 4.098,
     'cache_fox_v': 2.743,
     'cache_fox_logf': 8.0,
     'state_conv': 3.173,
     'attn_sink': 64.0,
     'conv_b': 35.562}
    for name, (base, spread) in spreads.items():
        noise = np.random.default_rng([zlib.crc32(name.encode()), seed]).standard_normal(out[name].shape)
        drawn = base * np.exp(spread * noise) if base else spread * noise
        out[name] = __import__('jax').numpy.asarray(drawn.astype(out[name].dtype))
    for name, factor in factors.items():
        out[name] = (out[name] * factor).astype(out[name].dtype)
    return out
```

```python
from contextlib import ExitStack

import numpy as np

import concourse.bass as bass
from concourse import mybir

P = 128
F32, F32R, BF16 = mybir.dt.float32, mybir.dt.float32r, mybir.dt.bfloat16
ALU = mybir.AluOpType
ACT = mybir.ActivationFunctionType
AX = mybir.AxisListType

DM, TP, TS, DEPTH, PAST = 1024, 256, 64, 2, 128
HD, DFF, CONV = 64, 2816, 3
CHUNK = 64
ALPHA = (2.0 * DEPTH) ** 0.25
SCALE = HD ** -0.5
EPS = 1e-5
NEG = -1e30
THETA = 10000.0
TOK = TP + TS
KC = DM // P
FT = DFF // P
KEYS = TOK + PAST
KV = 10
NH = 8
PAIRS = 8

C_QA, C_KA, C_VA, C_QB, C_KB, C_VB, C_F, C_GA, C_GB = 0, 512, 640, 768, 1280, 1792, 2304, 2312, 3336

P_STATE, P_CW, P_CB = 0, 2 * FT, 5 * FT
P_LN1G = 6 * FT
P_LN1B, P_LN2G, P_LN2B = P_LN1G + KC, P_LN1G + 2 * KC, P_LN1G + 3 * KC
P_ALL = P_LN1G + 4 * KC
ROWS_A = 5 * FT
ROWS_B = P_ALL - ROWS_A

CF_ID, CF_ROT, CF_MEAN, CF_COS, CF_SIN = 0, 128, 256, 384, 384 + TOK
CF_ALL = CF_SIN + TOK
CB_ID, CB_FOX, CB_SWA, CB_SMP, CB_SEL, CB_SELS = 0, 128, 512, 896, 1088, 1088 + NH * P
CB_ALL = CB_SELS + 4 * P

SLOTS = 4


def unit_list():
    units = [("forget", 0, KC), ("ka", 0, KC), ("va", 0, KC)]
    units += [("qa", t, KC) for t in range(4)]
    units += [("kb", t, KC) for t in range(4)] + [("vb", t, KC) for t in range(4)] + [("qb", t, KC) for t in range(4)]
    for o in range(KC):
        units += [("ga", o, KC), ("gb", o, KC)]
    units += [("pab", o, KC) for o in range(KC)] + [("wo", o, KC) for o in range(KC)]
    while len(units) % SLOTS:
        units.append(None)
    for j in range(FT):
        units += [("gate", j, KC), ("up", j, KC)]
    for o in range(KC):
        units += [("down", o, 0), ("down", o, 1), ("down", o, 2)]
    while len(units) % SLOTS:
        units.append(None)
    return units


UNITS = unit_list()
NU = len(UNITS)
DOWN_CHUNKS = [(0, 8), (8, 15), (15, FT)]
AT = {u[:2] + ((u[2],) if u[0] == "down" else ()): n for n, u in enumerate(UNITS) if u}


def unit_dmas(u):
    return {"qa": 2, "pab": 3}.get(UNITS[u][0], 1)


def credit(u):
    n = 1
    while u + n < NU and UNITS[u + n] is None:
        n += 1
    return n


TILES = []
for _u in UNITS:
    if _u is None:
        continue
    if _u[0] == "pab":
        TILES += [("pa", _u[1]), ("pb", _u[1])]
    elif _u[0] != "down" or _u[2] == 0:
        TILES.append(_u[:2])
NT = len(TILES)
TILE = {t: n for n, t in enumerate(TILES)}
BY_SCALAR = ("forget", "ka", "va", "qa", "kb", "vb", "qb", "ga", "gb", "gate")
COPIED = {t: n + 1 for n, t in enumerate([t for t in TILES if t[0] in BY_SCALAR])}
N_COPIED = len(COPIED)


def last_unit(tile):
    kind, i = tile
    return AT[("pab", i)] if kind in ("pa", "pb") else AT[("down", i, 2)] if kind == "down" else AT[tile]


SCHEDULE = {}


def at_unit(u, *step):
    SCHEDULE.setdefault(u, []).append(step)


at_unit(0, "params", 0)
at_unit(0, "cache", 0)
at_unit(0, "cache", 1)
at_unit(1, "logf", 0)
at_unit(3, "rope", 0)
at_unit(4, "rope", 1)
at_unit(5, "rope", 2)
at_unit(5, "logft", 0)
at_unit(5, "kv", 0)
at_unit(5, "kv", 1)
at_unit(6, "rope", 3)
at_unit(7, "rope", 4)
for _t in range(8):
    at_unit(9 + _t, "kv", 2 + _t)
for _p in range(PAIRS):
    _a = 8 + 3 * _p
    at_unit(_a, "scores", _p)
    at_unit(_a + 1, "soften", _p)
    at_unit(_a + 2, "turn", _p)
    at_unit(_a + 4, "values", _p)
at_unit(AT[("wo", KC - 1)], "norm", 0)
at_unit(AT[("down", 7, 2)], "norm", 1)
at_unit(AT[("down", 0, 1)], "tails", 0)

USES = []
for _u in range(NU):
    for _s, _i in SCHEDULE.get(_u, []):
        USES += [(k, _i) for k in {"logf": (), "soften": (), "scores": ("s0", "s1", "s2"), "turn": ("t0", "t1", "t2"),
                                   "values": ("o",), "norm": ("mean", "var")}.get(_s, (_s,))]
N_USES = len(USES)
FIRST = KC
LAST = 6
while len(USES) % 4:
    USES.append(None)
USE = {u: n for n, u in enumerate(USES) if u}

KV_TILES = [("ka", 0), ("va", 0)] + [("kb", t) for t in range(4)] + [("vb", t) for t in range(4)]
LANDED_INPUTS = 14
STORES_KV = 8


def constants():
    f = np.zeros((P, CF_ALL), np.float32)
    f[:, CF_ID:CF_ID + P] = np.eye(P)
    for m in range(P):
        f[m + 32 if m % 64 < 32 else m - 32, CF_ROT + m] = -1.0 if m % 64 < 32 else 1.0
    f[:, CF_MEAN:CF_MEAN + P] = 1.0 / DM
    half = HD // 2
    inv = (1.0 / (np.float32(THETA) ** (np.arange(half, dtype=np.float32) / np.float32(half)))).astype(np.float32)
    pos = np.concatenate([np.arange(TP), PAST + np.arange(TS)]).astype(np.float32)
    ang = (pos[None, :] * inv[np.arange(P) % half][:, None]).astype(np.float32)
    f[:, CF_COS:CF_COS + TOK] = np.cos(ang)
    f[:, CF_SIN:CF_SIN + TOK] = np.sin(ang)

    b = np.zeros((P, CB_ALL), np.float32)
    b[:, CB_ID:CB_ID + P] = np.eye(P)
    t, s = np.arange(P)[:, None], np.arange(2 * P)[None, :]
    b[:, CB_FOX:CB_FOX + P] = np.where(s[:, :P] <= t, 0, NEG)
    b[:, CB_FOX + P:CB_FOX + 3 * P] = np.where(s <= P + t, 0, NEG)
    back = 2 * CHUNK

    def window(q, k):
        c = q // CHUNK
        return (k // CHUNK <= c) & (k // CHUNK >= c - back // CHUNK)

    b[:, CB_SWA:CB_SWA + P] = np.where(window(t, s[:, :P]), 0, NEG)
    b[:, CB_SWA + P:CB_SWA + 3 * P] = np.where(window(t + P, s), 0, NEG)
    b[:, CB_SMP:CB_SMP + TS] = np.where(s[:, :TS] <= t % TS, 0, NEG)
    for part in range(3):
        for h in range(NH):
            b[32 * part + h, CB_SEL + h * P:CB_SEL + (h + 1) * P] = 1
        for j in range(4):
            b[32 * part + 2 * j, CB_SELS + j * P:CB_SELS + j * P + 64] = 1
            b[32 * part + 2 * j + 1, CB_SELS + j * P + 64:CB_SELS + (j + 1) * P] = 1
    return f, b


def build(nc, A, O):
    (y_prompt, y_sample, p_swa_k, p_swa_v, p_fox_k, p_fox_v, p_logf, p_conv,
     s_swa_k, s_swa_v, s_fox_k, s_fox_v, s_logf, s_conv) = O
    with ExitStack() as ctx:
        def sb(name, shape, dt=F32):
            return ctx.enter_context(nc.sbuf_tensor(name, shape, dt))

        def sem(name):
            return ctx.enter_context(nc.semaphore(name))

        raw = sb("raw", [P, SLOTS, KC * P])
        w_hi = sb("w_hi", [P, SLOTS, KC, P], F32R)
        w_lo = sb("w_lo", [P, SLOTS, KC, P], F32R)
        xT = sb("xT", [P, KC, TOK])
        act_hi = sb("act_hi", [P, KC, TOK], F32R)
        act_lo = sb("act_lo", [P, KC, TOK], F32R)
        arena0 = (nc.sbuf_base + 31) // 32 * 32
        sb("arena", [P, 2 * FT * TOK])

        def within(name, first, shape, dt=F32):
            return nc.alloc_sbuf_tensor_at(name, shape, dt, offset=arena0 + 4 * first)

        h_hi = within("h_hi", 0, [P, FT, TOK], F32R)
        h_lo = within("h_lo", FT * TOK, [P, FT, TOK], F32R)
        o_hi = within("o_hi", 0, [P, PAIRS, TOK], F32R)
        o_lo = within("o_lo", PAIRS * TOK, [P, PAIRS, TOK], F32R)
        qT = within("qT", 2 * PAIRS * TOK, [P, PAIRS, TOK])
        kT = within("kT", 3 * PAIRS * TOK, [P, 5, KEYS])
        kv = within("kv", 3 * PAIRS * TOK + 5 * KEYS, [P, 3, KV * P])
        assert 3 * PAIRS * TOK + 5 * KEYS + 3 * KV * P <= 2 * FT * TOK
        gates = sb("gates", [P, 2 * KC, TOK])
        kcache = sb("kcache", [P, 5 * P])
        vcache = sb("vcache", [P, 5 * P])
        cf = sb("cf", [P, CF_ALL])
        cb = sb("cb", [P, CB_ALL], BF16)
        rows_a = sb("rows_a", [ROWS_A, P])
        rows_b = sb("rows_b", [ROWS_B, P])
        par = sb("par", [P, P_ALL])
        lf_cache = sb("lf_cache", [P, NH])
        b_f = sb("b_f", [NH, 1])
        sinks = sb("sinks", [P, NH])
        sink5 = sb("sink5", [P, 4, 5])
        fz = sb("fz", [NH, TOK])
        fe = sb("fe", [NH, TOK])
        logf = sb("logf", [NH, TOK])
        logf_c = sb("logf_c", [NH, PAST])
        ones8 = sb("ones8", [NH, TP])
        NF = P + KEYS
        fsum = sb("fsum", [NH, NF])
        fres = sb("fres", [NH, NF])
        fmid = sb("fmid", [NH, NF], BF16)
        fparts = sb("fparts", [72, NF], BF16)
        logf_t = sb("logf_t", [P, 3, NH])
        stage = sb("stage", [P, 2, TOK])
        roped_a = sb("roped_a", [P, TOK])
        roped_b = sb("roped_b", [P, TOK])
        probs = sb("probs", [P, 2, 960])
        probs_t = sb("probs_t", [P, 3, 3 * P])
        nmax = sb("nmax", [P, PAIRS, 5])
        den = sb("den", [P, PAIRS, 5])
        sink_e = sb("sink_e", [P, 4, 5])
        rden = sb("rden", [P, PAIRS, 5])
        EXT = TOK + 4
        a_ext = sb("a_ext", [P, 2, EXT])
        conv = sb("conv", [P, 2, EXT - 2])
        hf = stage
        tails = sb("tails", [P, 4 * FT])
        tails_t = sb("tails_t", [4 * FT, P])
        merged_a = probs_t[:].rearrange("p a b -> p (a b)")[:, 0:2 * TOK].rearrange("p (a b) -> p a b", a=2)
        spread, rstd = roped_a, roped_b
        eps_t = sb("eps_t", [P, 1])

        xin = gates[:].rearrange("p a b -> p (a b)")[:, 0:3 * DM].rearrange("p (t d) -> p t d", t=3)
        bank = [ctx.enter_context(nc.psum_tensor(f"bank{i}", [P, 512], F32)) for i in range(8)]

        id32, rot = cf[:, CF_ID:CF_ID + P], cf[:, CF_ROT:CF_ROT + P]
        mean_w = cf[:, CF_MEAN:CF_MEAN + P]
        cos, sin = cf[:, CF_COS:CF_COS + TOK], cf[:, CF_SIN:CF_SIN + TOK]
        id16 = cb[:, CB_ID:CB_ID + P]

        cb_wide = kv[:].rearrange("p a b -> p (a b)")[:, 0:CB_ALL]
        masks_in = sem("masks_in")
        constants_in = sem("constants_in")
        landed = [sem(f"landed{i}") for i in range(SLOTS)]
        inputs_in = sem("inputs_in")
        hi_made, lo_made = sem("hi_made"), sem("lo_made")
        unit_used = sem("unit_used")
        copied = sem("copied")
        a_gated, b_gated = sem("a_gated"), sem("b_gated")
        spare_done = sem("spare_done")
        cache_turned, logf_turned = sem("cache_turned"), sem("logf_turned")
        params_ready = sem("params_ready")
        x_copied = sem("x_copied")
        x_hi_made, x_split = sem("x_hi_made"), sem("x_split")
        z_ready, log_ready, logf_ready, f_ready = sem("z_ready"), sem("log_ready"), sem("logf_ready"), sem("f_ready")
        roped = sem("roped")
        kv_turned = sem("kv_turned")
        max_ready, exp_done, sink_done, probs_ready = (sem("max_ready"), sem("exp_done"), sem("sink_done"),
                                                       sem("probs_ready"))
        turned_act, turned_dve = sem("turned_act"), sem("turned_dve")
        o_hi_made, o_split = sem("o_hi_made"), sem("o_split")
        m_ready, m_hi_made, m_split = sem("m_ready"), sem("m_hi_made"), sem("m_split")
        r_ready, centred, squared = sem("r_ready"), sem("centred"), sem("squared")
        spread_ready, scaled = sem("spread_ready"), sem("scaled")
        history_set, gate_copied, conv_begun, conv_done = (sem("history_set"), sem("gate_copied"), sem("conv_begun"),
                                                           sem("conv_done"))
        gelu_done, h_ready, h_hi_made, h_split = sem("gelu_done"), sem("h_ready"), sem("h_hi_made"), sem("h_split")
        tail_copied, tails_turned = sem("tail_copied"), sem("tails_turned")
        y_copied = sem("y_copied")
        rows_free = sem("rows_free")
        kv_stored, logf_stored, conv_stored, stored = (sem("kv_stored"), sem("logf_stored"), sem("conv_stored"),
                                                       sem("stored"))
        set_once = sem("set_once")
        act_chain, dve_chain = sem("act_chain"), sem("dve_chain")
        gate_pass = sem("gate_pass")

        def n(l, k, per):
            return l * per + k

        def unit_n(l, u):
            return l * NU + u

        def released(l, key):
            kind, i = key
            return {"params": (params_ready, n(l, 1, 1)), "cache": (cache_turned, n(l, i + 1, 2)),
                    "rope": (roped, n(l, i + 1, 5)), "logft": (logf_turned, n(l, 1, 1)),
                    "kv": (kv_turned, n(l, i + 1, KV)), "tails": (tails_turned, n(l, 1, 1)),
                    "s0": (exp_done, n(l, 3 * i + 1, 3 * PAIRS)), "s1": (exp_done, n(l, 3 * i + 2, 3 * PAIRS)),
                    "s2": (exp_done, n(l, 3 * i + 3, 3 * PAIRS)), "t0": (turned_act, n(l, 2 * i + 1, 2 * PAIRS)),
                    "t1": (turned_dve, n(l, i + 1, PAIRS)), "t2": (turned_act, n(l, 2 * i + 2, 2 * PAIRS)),
                    "o": (o_split, n(l, i + 1, PAIRS) + 1), "mean": (centred, n(l, KC * i + KC, 2 * KC)),
                    "var": (spread_ready, n(l, i + 1, 2))}[kind]

        def tile_released(l, tile):
            kind, i = tile
            if kind in BY_SCALAR:
                return copied, n(l, COPIED[tile], N_COPIED)
            return {"pa": (a_gated, n(l, i + 1, KC)), "pb": (b_gated, n(l, i + 1, KC)),
                    "wo": (r_ready, n(l, i + 1, 2 * KC)), "down": (r_ready, n(l, KC + i + 1, 2 * KC)),
                    "up": (h_ready, n(l, i + 1, FT))}[kind]

        per_slot = [0] * SLOTS
        landed_at = []
        for u in range(NU):
            if UNITS[u]:
                per_slot[u % SLOTS] += 16 * unit_dmas(u)
            landed_at.append(per_slot[u % SLOTS])

        block = ctx.enter_context(nc.Block())

        def value_stage(i):
            return 1 if i == 1 else i % 2

        def spare(l, key):
            return bank[4 + USE[key] % 4], FIRST + n(l, USE[key] + 1, N_USES)

        def width(u):
            kind, _, c = UNITS[u]
            return (DOWN_CHUNKS[c][1] - DOWN_CHUNKS[c][0] if kind == "down" else KC) * P

        GROUPS = [(0, 0, P), (0, P, TP), (1, 0, P), (1, P, TP), (2, 0, TS + PAST)]

        @block.sync
        def _(sp):
            sp.dma_start(xin[:, 0:2, :], A["x_prompt"][0].rearrange("(t p) d -> p t d", p=P)).then_inc(constants_in, 16)
            sp.dma_start(xin[0:TS, 2, :], A["x_sample"][0]).then_inc(constants_in, 16)
            sp.dma_start(cf[:], A["const_f"]).then_inc(constants_in, 16)
            sp.dma_start(cb_wide, A["const_b"]).then_inc(masks_in, 16)

            def columns(w, l, c0, width=P):
                return w[l].rearrange("(c p) e -> p c e", p=P)[:, :, c0:c0 + width]

            with sp.Fori(0, DEPTH) as l:
                for u in range(NU):
                    if UNITS[u] is None:
                        continue
                    kind, i, c = UNITS[u]
                    slot = u % SLOTS
                    sp.wait_ge(lo_made, unit_n(l, u + 1))
                    sp.sem_inc(gate_pass, 1)
                    flat = raw[:, slot, :]
                    dst = flat.rearrange("p (c e) -> p c e", e=P)
                    if kind == "qa":
                        for g in range(2):
                            sp.dma_start(dst[:, :, g * HD:(g + 1) * HD],
                                         columns(A["w_in"], l, C_QA + (i + 4 * g) * HD, HD)).then_inc(landed[slot], 16)
                    elif kind == "pab":
                        wa = A["w_pa"][l].rearrange("(g t p) e -> g p t e", g=2, p=HD)
                        for g in range(2):
                            sp.dma_start(dst[g * HD:(g + 1) * HD, 0:4, :],
                                         wa[g, :, :, i * P:(i + 1) * P]).then_inc(landed[slot], 16)
                        sp.dma_start(dst[:, 4:8, :], columns(A["w_pb"], l, i * P)).then_inc(landed[slot], 16)
                    elif kind == "down":
                        k0, k1 = DOWN_CHUNKS[c]
                        sp.dma_start(dst[:, 0:k1 - k0, :],
                                     columns(A["w_down"], l, i * P)[:, k0:k1, :]).then_inc(landed[slot], 16)
                    else:
                        w, c0 = {"ka": ("w_in", C_KA), "va": ("w_in", C_VA), "kb": ("w_in", C_KB),
                                 "vb": ("w_in", C_VB), "qb": ("w_in", C_QB), "ga": ("w_in", C_GA), "forget": ("w_in", C_F),
                                 "gb": ("w_in", C_GB), "wo": ("w_o", 0), "gate": ("w_gate", 0),
                                 "up": ("w_up", 0)}[kind]
                        sp.dma_start(dst, columns(A[w], l, c0 + i * P)).then_inc(landed[slot], 16)

        @block.gpsimd
        def _(pool):
            def passed(wait_sem, value):
                pool.wait_ge(wait_sem, value)
                pool.sem_inc(gate_pass, 1)

            with pool.Fori(0, DEPTH) as l:
                def load(dst, src):
                    pool.dma_start(dst, src).then_inc(inputs_in, 16)

                passed(o_split, n(l, 1, PAIRS))
                load(rows_a[0:2 * FT, :], A["state_conv"][l, 0].rearrange("r (j p) -> (r j) p", p=P))
                load(rows_a[2 * FT:5 * FT, :], A["conv_w"][l].rearrange("r (j p) -> (r j) p", p=P))
                load(rows_b[0:FT, :], A["conv_b"][l].rearrange("(j p) -> j p", p=P))
                for k, name in enumerate(("ln1_g", "ln1_b", "ln2_g", "ln2_b")):
                    load(rows_b[FT + k * KC:FT + (k + 1) * KC, :], A[name][l].rearrange("(j p) -> j p", p=P))
                load(lf_cache[:], A["cache_fox_logf"][l, 0])
                load(b_f[:], A["b_f"][l].rearrange("(h a) -> h a", a=1))
                load(sinks[:], A["attn_sink"][l].rearrange("(a h) -> a h", a=1).to_broadcast([P, NH]))
                for tile, s, f in ((kcache, "cache_swa_k", "cache_fox_k"), (vcache, "cache_swa_v", "cache_fox_v")):
                    load(tile[:, 0:P], A[s][l, 0].rearrange("t h d -> t (h d)"))
                    load(tile[:, P:5 * P], A[f][l, 0].rearrange("t h d -> t (h d)"))
                keep = PAST - TS
                pool.dma_start(s_swa_k[l, 0, 0:keep], A["cache_swa_k"][l, 0, TS:PAST]).then_inc(stored, 16)
                pool.dma_start(s_swa_v[l, 0, 0:keep], A["cache_swa_v"][l, 0, TS:PAST]).then_inc(stored, 16)

                passed(logf_turned, n(l, 1, 1))
                pool.dma_start(p_logf[l, 0].rearrange("(t p) h -> p t h", p=P), logf_t[:, 0:2, :]).then_inc(logf_stored, 16)
                pool.dma_start(s_logf[l, 0], logf_t[0:TS, 2, :]).then_inc(logf_stored, 16)

                def store_kv(dst_p, dst_s, f0, nf, window_only):
                    cols = slice(f0 * P, (f0 + nf) * P)
                    if window_only:
                        pool.dma_start(dst_p[l, 0].rearrange("t h d -> t (h d)"), kv[:, 1, cols]).then_inc(kv_stored, 16)
                        pool.dma_start(dst_s[l, 0, keep:PAST].rearrange("t h d -> t (h d)"),
                                       kv[0:TS, 2, cols]).then_inc(kv_stored, 16)
                    else:
                        pool.dma_start(dst_p[l, 0].rearrange("(t p) h d -> p t (h d)", p=P),
                                       kv[:, 0:2, cols]).then_inc(kv_stored, 16)
                        pool.dma_start(dst_s[l, 0].rearrange("t h d -> t (h d)"),
                                       kv[0:TS, 2, cols]).then_inc(kv_stored, 16)

                passed(kv_turned, n(l, KV, KV))
                store_kv(p_swa_k, s_swa_k, 0, 1, True)
                store_kv(p_swa_v, s_swa_v, 1, 1, True)
                store_kv(p_fox_k, s_fox_k, 2, 4, False)
                store_kv(p_fox_v, s_fox_v, 6, 4, False)

                passed(tails_turned, n(l, 1, 1))
                pool.dma_start(p_conv[l, 0].rearrange("r (j p) -> (r j) p", p=P), tails_t[0:2 * FT, :]).then_inc(conv_stored, 16)
                pool.dma_start(s_conv[l, 0].rearrange("r (j p) -> (r j) p", p=P),
                               tails_t[2 * FT:4 * FT, :]).then_inc(conv_stored, 16)
                passed(logf_stored, 32 * n(l, 1, 1))
                passed(conv_stored, 32 * n(l, 1, 1))
                pool.sem_inc(rows_free, 1)

            pool.wait_ge(y_copied, LAST)
            pool.dma_start(y_prompt[0].rearrange("(t p) d -> p t d", p=P), xin[:, 0:2, :]).then_inc(stored, 16)
            pool.dma_start(y_sample[0], xin[0:TS, 2, :]).then_inc(stored, 16)
            pool.wait_ge(kv_stored, 16 * STORES_KV * DEPTH)
            pool.wait_ge(logf_stored, 32 * DEPTH)
            pool.wait_ge(conv_stored, 32 * DEPTH)
            pool.wait_ge(stored, 16 * (2 * DEPTH + 2))

        @block.tensor
        def _(pe):
            def claim(l, key):
                at = USE[key]
                if at >= 4:
                    pe.wait_ge(*released(l, USES[at - 4]))
                return bank[4 + at % 4]

            def claim_tile(l, tile):
                at = TILE[tile]
                if at >= 4:
                    pe.wait_ge(*tile_released(l, TILES[at - 4]))
                return bank[at % 4]

            def products(out, slot, n_chunks, hi, lo, k0, begin, end, ready=None, c0=0):
                for c in range(n_chunks):
                    if ready:
                        ready(k0 + c)
                    wh, wl = w_hi[:, slot, c0 + c, :], w_lo[:, slot, c0 + c, :]
                    pe.matmul(out, wh, hi[:, k0 + c, :], start=begin and c == 0, stop=False)
                    pe.matmul(out, wh, lo[:, k0 + c, :], start=False, stop=False)
                    mm = pe.matmul(out, wl, hi[:, k0 + c, :], start=False, stop=end and c == n_chunks - 1)
                return mm

            def unit(l, u):
                kind, i, c = UNITS[u]
                slot = u % SLOTS
                pe.wait_ge(lo_made, unit_n(l, u + 1) + SLOTS)
                fresh = {("forget", 0): (x_split, lambda k: n(l, k + 1, 2 * KC)),
                         ("pab", 0): (o_split, lambda k: n(l, k + 1, PAIRS) + 1),
                         ("wo", 0): (m_split, lambda k: n(l, k + 1, KC)),
                         ("gate", 0): (x_split, lambda k: n(l, KC + k + 1, 2 * KC)),
                         ("down", 0): (h_split, lambda k: n(l, k + 1, FT))}.get((kind, i))

                def ready(k):
                    if fresh:
                        pe.wait_ge(fresh[0], fresh[1](k))

                if kind == "pab":
                    for part, k0 in (("pa", 0), ("pb", 4)):
                        out = claim_tile(l, (part, i))
                        mm = products(out[:, 0:TOK], slot, 4, o_hi, o_lo, k0, True, True, ready, c0=k0)
                elif kind == "down":
                    k0, k1 = DOWN_CHUNKS[c]
                    out = claim_tile(l, ("down", i)) if c == 0 else bank[TILE[("down", i)] % 4]
                    mm = products(out[:, 0:TOK], slot, k1 - k0, h_hi, h_lo, k0, c == 0, c == 2, ready)
                else:
                    out = claim_tile(l, (kind, i))
                    mm = products(out[:, 0:TOK], slot, KC, act_hi, act_lo, 0, True, True, ready)
                mm.then_inc(unit_used, credit(u))

            def done(mm):
                mm.then_inc(spare_done, 1)

            def turned(out, src):
                rows, cols = src.shape
                if cols == P:
                    return pe.transpose(out, src, id32[0:rows, 0:rows])
                return pe.matmul(out, src, id32[0:rows, 0:rows], start=True, stop=True)

            def settled():
                pe.sem_inc(gate_pass, 1)

            def step(l, kind, i):
                if kind == "params":
                    pe.wait_ge(inputs_in, 16 * n(l, LANDED_INPUTS, LANDED_INPUTS))
                    b = claim(l, ("params", 0))
                    turned(b[:, 0:ROWS_A], rows_a[:])
                    done(turned(b[:, ROWS_A:P_ALL], rows_b[:]))
                elif kind == "cache" and i == 0:
                    b = claim(l, ("cache", 0))
                    for t in range(4):
                        mm = turned(b[:, t * P:(t + 1) * P], kcache[:, (t + 1) * P:(t + 2) * P])
                    done(mm)
                elif kind == "cache":
                    b = claim(l, ("cache", 1))
                    turned(b[:, 0:P], kcache[:, 0:P])
                    done(turned(b[0:NH, P:2 * P], lf_cache[:]))
                elif kind == "rope":
                    b = claim(l, ("rope", i))
                    src = ("ka", 0) if i == 0 else ("qa", i - 1)
                    pe.wait_ge(copied, n(l, COPIED[src], N_COPIED))
                    x = stage[:, 0, :] if i == 0 else qT[:, i - 1, :]
                    done(pe.matmul(b[:, 0:TOK], rot, x, start=True, stop=True))
                elif kind == "logft":
                    pe.wait_ge(logf_ready, n(l, 1, 1))
                    b = claim(l, ("logft", 0))
                    settled()
                    for t in range(3):
                        w = P if t < 2 else TS
                        mm = turned(b[0:w, t * NH:(t + 1) * NH], logf[:, t * P:t * P + w])
                    done(mm)
                elif kind == "kv":
                    b = claim(l, ("kv", i))
                    if i == 0:
                        pe.wait_ge(roped, n(l, 1, 5))
                        src = kT[:, 0, :]
                    else:
                        pe.wait_ge(copied, n(l, COPIED[KV_TILES[i]], N_COPIED))
                        src = kT[:, i - 1, :] if 2 <= i < 6 else stage[:, value_stage(i), :]
                    for t in range(3):
                        w = P if t < 2 else TS
                        mm = turned(b[0:w, t * P:(t + 1) * P], src[:, t * P:t * P + w])
                    done(mm)
                elif kind == "scores":
                    scores(l, i)
                elif kind == "turn":
                    pe.wait_ge(probs_ready, n(l, i + 1, PAIRS))
                    pr = probs[:, i % 2, :]
                    for hd in range(2):
                        b = claim(l, (f"t{hd}", i))
                        for k in range(3):
                            c0 = 3 * P * hd + k * P
                            mm = turned(b[:, k * P:(k + 1) * P], pr[:, c0:c0 + P])
                        done(mm)
                    b = claim(l, ("t2", i))
                    turned(b[:, 0:P], pr[:, 6 * P + TS:6 * P + TS + PAST])
                    done(turned(b[0:TS, P:2 * P], pr[:, 6 * P:6 * P + TS]))
                elif kind == "values":
                    values(l, i)
                elif kind == "norm":
                    b = claim(l, ("mean", i))
                    for o in range(KC):
                        pe.wait_ge(r_ready, n(l, KC * i + o + 1, 2 * KC))
                        mm = pe.matmul(b[:, 0:TOK], mean_w, gates[:, o, :], start=(o == 0), stop=(o == KC - 1))
                    done(mm)
                    b = claim(l, ("var", i))
                    for o in range(KC):
                        pe.wait_ge(squared, n(l, KC * i + o + 1, 2 * KC))
                        mm = pe.matmul(b[:, 0:TOK], mean_w, gates[:, KC + o, :], start=(o == 0), stop=(o == KC - 1))
                    done(mm)
                elif kind == "tails":
                    pe.wait_ge(tail_copied, n(l, 2 * FT, 2 * FT))
                    b = claim(l, ("tails", 0))
                    done(turned(b[0:4 * FT, 0:P], tails[:]))

            def scores(l, p):
                fox = p >= 4
                if fox:
                    pe.wait_ge(f_ready, n(l, 1, 1))
                    pe.wait_ge(copied, n(l, COPIED[("qb", p - 4)], N_COPIED))
                else:
                    pe.wait_ge(roped, n(l, p + 2, 5))
                k = kT[:, p - 3, :] if fox else kT[:, 0, :]
                mask = CB_FOX if fox else CB_SWA
                for hd in range(2):
                    b = claim(l, (f"s{hd}", p))
                    rows = slice(hd * HD, (hd + 1) * HD)
                    settled()
                    pe.matmul(b[:, 0:P], qT[rows, p, 0:P], k[rows, 0:P], start=True, stop=False)
                    pe.matmul(b[:, P:3 * P], qT[rows, p, P:TP], k[rows, 0:TP], start=False, stop=False)
                    if fox:
                        h = 2 * (p - 4) + hd
                        pe.matmul(b[:, 0:3 * P], cb[0:72, CB_SEL + h * P:CB_SEL + (h + 1) * P], fparts[:, 0:3 * P],
                                  start=False, stop=False)
                    done(pe.matmul(b[:, 0:3 * P], id16, cb[:, mask:mask + 3 * P], start=False, stop=True))
                b = claim(l, ("s2", p))
                settled()
                for hd in range(2):
                    rows = slice(hd * HD, (hd + 1) * HD)
                    mm = pe.matmul(b[rows, 0:TS + PAST], qT[rows, p, TP:TOK], k[rows, TP:KEYS],
                                   start=True, stop=not fox)
                if fox:
                    pe.matmul(b[:, 0:TS + PAST], cb[0:72, CB_SELS + (p - 4) * P:CB_SELS + (p - 3) * P],
                              fparts[:, 3 * P:3 * P + TS + PAST], start=False, stop=False)
                    mm = pe.matmul(b[:, 0:TS + PAST], id16, cb[:, CB_SMP:CB_SMP + TS + PAST], start=False, stop=True)
                done(mm)

            def values(l, p):
                fox = p >= 4
                pe.wait_ge(kv_turned, n(l, (p - 4 + 7) if fox else 2, KV))
                pe.wait_ge(turned_act, n(l, 2 * p + 2, 2 * PAIRS))
                pe.wait_ge(turned_dve, n(l, p + 1, PAIRS))
                b = claim(l, ("o", p))
                settled()
                f = 6 + p - 4 if fox else 1
                for hd in range(2):
                    rows = slice(hd * HD, (hd + 1) * HD)
                    v = slice(f * P + hd * HD, f * P + (hd + 1) * HD)
                    vc = slice((p - 3) * P + hd * HD, (p - 3) * P + (hd + 1) * HD) if fox else rows
                    pt = probs_t[:, hd, :]
                    sample = slice(hd * TS, (hd + 1) * TS)
                    pe.matmul(b[rows, 0:P], kv[:, 0, v], pt[:, 0:P], start=True, stop=True, skip_group_check=True)
                    pe.matmul(b[rows, P:TP], kv[:, 0, v], pt[:, P:2 * P], start=False, stop=False,
                              skip_group_check=True)
                    pe.matmul(b[rows, P:TP], kv[:, 1, v], pt[:, 2 * P:3 * P], start=False, stop=True,
                              skip_group_check=True)
                    pe.matmul(b[rows, TP:TOK], vcache[:, vc], probs_t[:, 2, sample], start=False, stop=False,
                              skip_group_check=True)
                    mm = pe.matmul(b[rows, TP:TOK], kv[0:TS, 2, v],
                                   probs_t[0:TS, 2, P + hd * TS:P + (hd + 1) * TS], start=False, stop=True,
                                   skip_group_check=True)
                done(mm)

            pe.wait_ge(constants_in, 48)
            for o in range(KC):
                if o >= 4:
                    pe.wait_ge(x_copied, o - 3)
                for t in range(3):
                    w = P if t < 2 else TS
                    mm = turned(bank[4 + o % 4][:, t * P:t * P + w], xin[0:w, t, o * P:(o + 1) * P])
                done(mm)

            with pe.Fori(0, DEPTH) as l:
                for u in range(NU):
                    if UNITS[u]:
                        unit(l, u)
                    for kind, i in SCHEDULE.get(u, []):
                        step(l, kind, i)

            pe.wait_ge(x_split, DEPTH * 2 * KC + KC)
            for k in range(6):
                t, half = k // 2, k % 2
                w = P if t < 2 else TS
                if k >= 4:
                    pe.wait_ge(y_copied, k - 3)
                for c in range(4):
                    mm = turned(bank[4 + k % 4][0:w, c * P:(c + 1) * P], xT[:, 4 * half + c, t * P:t * P + w])
                done(mm)

        @block.scalar
        def _(act):
            sc = nc.scalar
            chain = [0]

            def link(ins):
                chain[0] += 1
                ins.then_inc(act_chain, 1)
                act.wait_ge(act_chain, chain[0])

            def hi_part(l, u):
                kind, _, c = UNITS[u]
                slot = u % SLOTS
                act.wait_ge(landed[slot], n(l, landed_at[u], per_slot[slot]))
                act.wait_ge(unit_used, unit_n(l, u + 1))
                w = width(u)
                sc.copy(w_hi[:, slot, :, :].rearrange("p c e -> p (c e)")[:, 0:w],
                        raw[:, slot, 0:w]).then_inc(hi_made, credit(u))

            def tile_wait(l, tile):
                act.wait_ge(unit_used, SLOTS + unit_n(l, last_unit(tile) + 1))
                return bank[TILE[tile] % 4]

            def after(l, u):
                kind, i, c = UNITS[u]
                if kind == "forget":
                    b = tile_wait(l, ("forget", 0))
                    act.wait_ge(inputs_in, 16 * n(l, LANDED_INPUTS, LANDED_INPUTS))
                    sc.activation(fz[:], b[0:NH, 0:TOK], ACT.Identity, bias=b_f[:]).then_inc(copied, 1)
                elif kind in ("qa", "qb"):
                    b = tile_wait(l, (kind, i))
                    sc.activation(qT[:, i + (4 if kind == "qb" else 0), :], b[:, 0:TOK], ACT.Copy,
                                  scale=SCALE).then_inc(copied, 1)
                elif kind == "kb":
                    b = tile_wait(l, (kind, i))
                    sc.copy(kT[:, 1 + i, 0:TOK], b[:, 0:TOK]).then_inc(copied, 1)
                elif kind in ("ka", "va", "vb"):
                    b = tile_wait(l, (kind, i))
                    k = 0 if kind == "ka" else value_stage(1 if kind == "va" else 6 + i)
                    if kind == "vb":
                        back = ("kv", 6 + i - 2) if i >= 2 else ("kv", 1)
                        act.wait_ge(spare_done, spare(l, back)[1])
                        act.wait_ge(roped, n(l, 1, 5))
                    sc.copy(stage[:, k, :], b[:, 0:TOK]).then_inc(copied, 1)
                elif kind in ("ga", "gb"):
                    b = tile_wait(l, (kind, i))
                    sc.activation(gates[:, i + (KC if kind == "gb" else 0), :], b[:, 0:TOK], ACT.Tanh,
                                  scale=0.5).then_inc(copied, 1)
                elif kind == "pab":
                    act.wait_ge(m_ready, n(l, i + 1, KC))
                    sc.activation(act_hi[:, i, :], merged_a[:, i % 2, :], ACT.Copy, scale=0.5).then_inc(m_hi_made, 1)
                elif kind == "gate":
                    b = tile_wait(l, ("gate", i))
                    e = a_ext[:, i % 2, :]
                    if i >= 2:
                        act.wait_ge(conv_done, n(l, i - 1, FT))
                    sc.copy(e[:, 2:2 + TP], b[:, 0:TP])
                    sc.copy(e[:, 4 + TP:4 + TOK], b[:, TP:TOK]).then_inc(copied, 1)
                    act.wait_ge(copied, n(l, COPIED[("gate", i)], N_COPIED))
                    act.wait_ge(history_set, n(l, i + 1, FT))
                    act.wait_ge(params_ready, n(l, 1, 1))
                    sc.activation(conv[:, i % 2, :], e[:, 2:4 + TOK], ACT.Identity,
                                  bias=par[:, P_CB + i:P_CB + i + 1],
                                  scale=par[:, P_CW + 2 * FT + i:P_CW + 2 * FT + i + 1]).then_inc(conv_begun, 1)
                    if i > 0:
                        h_part(l, i - 1)
                elif kind == "up":
                    act.wait_ge(conv_done, n(l, i + 1, FT))
                    sc.activation(conv[:, i % 2, :], conv[:, i % 2, :], ACT.Gelu_apprx_tanh).then_inc(gelu_done, 1)
                elif kind == "down" and i == 0 and c == 0:
                    h_part(l, FT - 1)

            def h_part(l, j):
                act.wait_ge(h_ready, n(l, j + 1, FT))
                if j == 0:
                    act.wait_ge(kv_stored, 16 * n(l, STORES_KV, STORES_KV))
                sc.copy(h_hi[:, j, :], hf[:, j % 2, :]).then_inc(h_hi_made, 1)

            def step(l, kind, i):
                if kind == "logf":
                    act.wait_ge(copied, n(l, COPIED[("forget", 0)], N_COPIED))
                    link(sc.activation(fe[:], fz[:], ACT.Abs))
                    link(sc.activation(fe[:], fe[:], ACT.Exp, scale=-1.0))
                    sc.activation(fe[:], fe[:], ACT.Ln, bias=1.0).then_inc(log_ready, 1)
                elif kind == "scores":
                    pr = probs[:, i % 2, :]
                    for g, (key, c0, w) in enumerate(GROUPS):
                        b, v = spare(l, (f"s{key}", i))
                        src = b[:, c0:c0 + w]
                        if g == 0:
                            act.wait_ge(max_ready, n(l, i + 1, PAIRS))
                            if i >= 2:
                                act.wait_ge(spare_done, spare(l, ("t2", i - 2))[1])
                        at = 3 * P * key + c0
                        ins = sc.activation(pr[:, at:at + w], src, ACT.Exp, bias=nmax[:, i, g:g + 1],
                                            accum_out=den[:, i, g:g + 1])
                        if g in (1, 3, 4):
                            ins.then_inc(exp_done, 1)
                    if i < 4:
                        sc.activation(sink_e[:, i, :], sink_e[:, i, :], ACT.Exp).then_inc(sink_done, 1)
                elif kind == "turn":
                    if i > 0:
                        act.wait_ge(spare_done, spare(l, ("o", i - 1))[1])
                    b, v = spare(l, ("t0", i))
                    act.wait_ge(spare_done, v)
                    sc.copy(probs_t[:, 0, :], b[:, 0:3 * P]).then_inc(turned_act, 1)
                    b, v = spare(l, ("t2", i))
                    act.wait_ge(spare_done, v)
                    sc.copy(probs_t[:, 2, 0:P], b[:, 0:P])
                    sc.copy(probs_t[0:TS, 2, P:2 * P], b[0:TS, P:2 * P]).then_inc(turned_act, 1)
                elif kind == "values":
                    b, v = spare(l, ("o", i))
                    act.wait_ge(spare_done, v)
                    sc.copy(o_hi[:, i, :], b[:, 0:TOK]).then_inc(o_hi_made, 1)
                elif kind == "norm":
                    for o in range(KC):
                        act.wait_ge(centred, n(l, KC * i + o + 1, 2 * KC))
                        sc.activation(gates[:, KC + o, :], gates[:, o, :], ACT.Square).then_inc(squared, 1)
                    b, v = spare(l, ("var", i))
                    act.wait_ge(spare_done, v)
                    sc.activation(spread[:], b[:, 0:TOK], ACT.Sqrt, bias=eps_t[:]).then_inc(spread_ready, 1)
                    g0, b0 = (P_LN1G, P_LN1B) if i == 0 else (P_LN2G, P_LN2B)
                    for o in range(KC):
                        act.wait_ge(scaled, n(l, KC * i + o + 1, 2 * KC))
                        sc.activation(act_hi[:, o, :], gates[:, KC + o, :], ACT.Identity,
                                      bias=par[:, b0 + o:b0 + o + 1],
                                      scale=par[:, g0 + o:g0 + o + 1]).then_inc(x_hi_made, 1)

            act.wait_ge(set_once, 4)
            for o in range(KC):
                act.wait_ge(x_copied, o + 1)
                sc.copy(act_hi[:, o, :], xT[:, o, :]).then_inc(x_hi_made, 1)
            with act.Fori(0, DEPTH) as l:
                act.wait_ge(x_hi_made, KC * (2 * l + 1))
                act.sem_inc(gate_pass, 1)
                act.sem_clear(act_chain)
                chain[0] = 0
                hi_part(l, 0)
                hi_part(l, 1)
                for u in range(NU):
                    if u + 2 < NU and UNITS[u + 2]:
                        hi_part(l, u + 2)
                    if UNITS[u]:
                        after(l, u)
                    for kind, i in SCHEDULE.get(u, []):
                        step(l, kind, i)

        @block.vector
        def _(dve):
            ve = nc.vector
            chain = [0]

            def link(ins):
                chain[0] += 1
                ins.then_inc(dve_chain, 1)
                dve.wait_ge(dve_chain, chain[0])

            def lo_part(l, u):
                slot = u % SLOTS
                dve.wait_ge(hi_made, unit_n(l, u + credit(u)))
                w = width(u)
                hi = w_hi[:, slot, :, :].rearrange("p c e -> p (c e)")[:, 0:w]
                ve.tensor_tensor(w_lo[:, slot, :, :].rearrange("p c e -> p (c e)")[:, 0:w], raw[:, slot, 0:w],
                                 hi.bitcast(F32), ALU.subtract).then_inc(lo_made, credit(u))

            def tile_wait(l, tile):
                dve.wait_ge(unit_used, SLOTS + unit_n(l, last_unit(tile) + 1))
                return bank[TILE[tile] % 4]

            def after(l, u):
                kind, i, c = UNITS[u]
                if kind == "pab":
                    b = tile_wait(l, ("pa", i))
                    dve.wait_ge(copied, n(l, COPIED[("gb", i)], N_COPIED))
                    ma, g = merged_a[:, i % 2, :], gates[:, i, :]
                    if i >= 2:
                        dve.wait_ge(m_split, n(l, i - 1, KC))
                    ve.scalar_tensor_tensor(ma, g, 1.0, b[:, 0:TOK], ALU.add, ALU.mult).then_inc(a_gated, 1)
                    b = tile_wait(l, ("pb", i))
                    gb = gates[:, KC + i, :]
                    ve.scalar_tensor_tensor(gb, gb, 1.0, b[:, 0:TOK], ALU.add, ALU.mult).then_inc(b_gated, 1)
                    dve.wait_ge(b_gated, n(l, i + 1, KC))
                    ve.tensor_tensor(ma, ma, gb, ALU.add).then_inc(m_ready, 1)
                    dve.wait_ge(m_hi_made, n(l, i + 1, KC))
                    ve.scalar_tensor_tensor(act_lo[:, i, :], ma, 0.5, act_hi[:, i, :].bitcast(F32), ALU.mult,
                                            ALU.subtract).then_inc(m_split, 1)
                elif kind == "wo" or (kind == "down" and c == 2):
                    b = tile_wait(l, (kind, i))
                    ve.scalar_tensor_tensor(gates[:, i, :], xT[:, i, :], ALPHA, b[:, 0:TOK], ALU.mult,
                                            ALU.add).then_inc(r_ready, 1)
                elif kind == "gate":
                    e, cv = a_ext[:, i % 2, :], conv[:, i % 2, :]
                    if i == 0:
                        history(l, 0)
                    if i + 1 < FT:
                        history(l, i + 1)
                    dve.wait_ge(conv_begun, n(l, i + 1, FT))
                    for s, last in ((0, TP), (1, TOK + 2)):
                        ve.tensor_copy(tails[:].rearrange("p (s r j) -> p s r j", s=2, r=2)[:, s, :, i],
                                       e[:, last:last + 2]).then_inc(tail_copied, 1)
                    link(ve.scalar_tensor_tensor(cv, e[:, 1:3 + TOK], par[:, P_CW + FT + i:P_CW + FT + i + 1], cv,
                                                 ALU.mult, ALU.add))
                    ve.scalar_tensor_tensor(cv, e[:, 0:2 + TOK], par[:, P_CW + i:P_CW + i + 1], cv, ALU.mult,
                                            ALU.add).then_inc(conv_done, 1)
                    if i > 0:
                        h_part(l, i - 1)
                elif kind == "up":
                    b = tile_wait(l, ("up", i))
                    dve.wait_ge(gelu_done, n(l, i + 1, FT))
                    cv, h = conv[:, i % 2, :], hf[:, i % 2, :]
                    if i >= 2:
                        dve.wait_ge(h_split, n(l, i - 1, FT))
                    ve.tensor_tensor(h[:, 0:TP], cv[:, 0:TP], b[:, 0:TP], ALU.mult)
                    ve.tensor_tensor(h[:, TP:TOK], cv[:, TP + 2:TOK + 2], b[:, TP:TOK],
                                     ALU.mult).then_inc(h_ready, 1)
                elif kind == "down" and i == 0 and c == 0:
                    h_part(l, FT - 1)

            def history(l, j):
                if j >= 2:
                    dve.wait_ge(conv_done, n(l, j - 1, FT))
                ve.tensor_copy(a_ext[:, j % 2, TP + 2:TP + 4],
                               par[:, P_STATE:P_STATE + 2 * FT].rearrange("p (r j) -> p r j", r=2)[:, :, j])\
                    .then_inc(history_set, 1)

            def h_part(l, j):
                dve.wait_ge(h_hi_made, n(l, j + 1, FT))
                ve.tensor_tensor(h_lo[:, j, :], hf[:, j % 2, :], h_hi[:, j, :].bitcast(F32),
                                 ALU.subtract).then_inc(h_split, 1)

            def step(l, kind, i):
                if kind == "params":
                    b, v = spare(l, ("params", 0))
                    dve.wait_ge(spare_done, v)
                    ve.tensor_copy(par[:], b[:, 0:P_ALL]).then_inc(params_ready, 1)
                    for g in range(4):
                        ve.tensor_copy(sink5[:, :, g], sinks[:, 4 * (g // 2):4 * (g // 2) + 4])
                    ve.tensor_copy(sink5[0:64, :, 4], sinks[0:64, 0:4])
                    link(ve.tensor_copy(sink5[64:P, :, 4], sinks[64:P, 4:8]))
                    dve.wait_ge(params_ready, n(l, 1, 1))
                elif kind == "cache" and i == 0:
                    b, v = spare(l, ("cache", 0))
                    dve.wait_ge(spare_done, v)
                    ve.tensor_copy(kT[:, 1:5, TOK:KEYS],
                                   b[:, 0:4 * P].rearrange("p (t c) -> p t c", t=4)).then_inc(cache_turned, 1)
                elif kind == "cache":
                    b, v = spare(l, ("cache", 1))
                    dve.wait_ge(spare_done, v)
                    ve.tensor_copy(kT[:, 0, TOK:KEYS], b[:, 0:P])
                    ve.tensor_copy(logf_c[:], b[0:NH, P:2 * P]).then_inc(cache_turned, 1)
                    dve.wait_ge(cache_turned, n(l, 2, 2))
                elif kind == "logf":
                    dve.wait_ge(log_ready, n(l, 1, 1))
                    ve.scalar_tensor_tensor(logf[:], fz[:], 0.0, fe[:], ALU.min, ALU.subtract).then_inc(logf_ready, 1)
                    dve.wait_ge(logf_ready, n(l, 1, 1))
                    cache0 = P + TOK
                    link(ve.tensor_tensor_scan(fsum[:, P:P + TP], ones8[:], logf[:, 0:TP], 0.0, ALU.mult, ALU.add))
                    link(ve.tensor_tensor_scan(fsum[:, cache0:NF], ones8[:, 0:PAST], logf_c[:], 0.0, ALU.mult,
                                               ALU.add))
                    link(ve.tensor_tensor_scan(fsum[:, P + TP:cache0], ones8[:, 0:TS], logf[:, TP:TOK],
                                               fsum[:, NF - 1:NF], ALU.mult, ALU.add))
                    link(ve.tensor_copy(fsum[:, 0:P], fsum[:, P:2 * P]))
                    link(ve.tensor_scalar(fparts[0:NH, :], fsum[:], -1.0, None, ALU.mult))
                    link(ve.scalar_tensor_tensor(fres[:], fsum[:], -1.0, fparts[0:NH, :], ALU.mult, ALU.subtract))
                    link(ve.tensor_copy(fmid[:], fres[:]))
                    ve.tensor_copy(fparts[32:32 + NH, :], fmid[:])
                    link(ve.tensor_tensor(fres[:], fres[:], fmid[:], ALU.subtract))
                    ve.tensor_copy(fparts[64:64 + NH, :], fres[:]).then_inc(f_ready, 1)
                elif kind == "logft":
                    b, v = spare(l, ("logft", 0))
                    dve.wait_ge(spare_done, v)
                    dve.wait_ge(rows_free, n(l, 1, 1))
                    ve.tensor_copy(logf_t[:, 0:2, :], b[:, 0:2 * NH].rearrange("p (t h) -> p t h", t=2))
                    ve.tensor_copy(logf_t[0:TS, 2, :], b[0:TS, 2 * NH:3 * NH]).then_inc(logf_turned, 1)
                elif kind == "rope":
                    x = stage[:, 0, :] if i == 0 else qT[:, i - 1, :]
                    out = kT[:, 0, 0:TOK] if i == 0 else qT[:, i - 1, :]
                    b, v = spare(l, ("rope", i))
                    dve.wait_ge(spare_done, v)
                    if i > 0:
                        dve.wait_ge(roped, n(l, i, 5))
                    ve.tensor_tensor(roped_b[:], sin, b[:, 0:TOK], ALU.mult)
                    link(ve.tensor_tensor(roped_a[:], x, cos, ALU.mult))
                    ve.tensor_tensor(out, roped_a[:], roped_b[:], ALU.add).then_inc(roped, 1)
                elif kind == "kv":
                    b, v = spare(l, ("kv", i))
                    dve.wait_ge(spare_done, v)
                    ve.tensor_copy(kv[:, 0:2, i * P:(i + 1) * P], b[:, 0:2 * P].rearrange("p (t c) -> p t c", t=2))
                    ve.tensor_copy(kv[0:TS, 2, i * P:(i + 1) * P], b[0:TS, 2 * P:3 * P]).then_inc(kv_turned, 1)
                elif kind == "scores":
                    for g, (key, c0, w) in enumerate(GROUPS):
                        b, v = spare(l, (f"s{key}", i))
                        if g in (0, 2, 4):
                            dve.wait_ge(spare_done, v)
                        ins = ve.tensor_reduce(nmax[:, i, g:g + 1], b[:, c0:c0 + w], AX.X, ALU.max, negate=True)
                    if i < 4:
                        link(ins)
                        link(ve.scalar_tensor_tensor(nmax[:, i, :], sink5[:, i, :], -1.0, nmax[:, i, :], ALU.mult,
                                                     ALU.min))
                        ins = ve.tensor_tensor(sink_e[:, i, :], sink5[:, i, :], nmax[:, i, :], ALU.add)
                    ins.then_inc(max_ready, 1)
                elif kind == "soften":
                    dve.wait_ge(exp_done, n(l, 3 * i + 3, 3 * PAIRS))
                    if i < 4:
                        dve.wait_ge(sink_done, n(l, i + 1, 4))
                        link(ve.tensor_tensor(den[:, i, :], den[:, i, :], sink_e[:, i, :], ALU.add))
                    link(ve.reciprocal(rden[:, i, :], den[:, i, :]))
                    for g, (key, c0, w) in enumerate(GROUPS):
                        pr = probs[:, i % 2, 3 * P * key + c0:3 * P * key + c0 + w]
                        ins = ve.tensor_scalar(pr, pr, rden[:, i, g:g + 1], None, ALU.mult)
                    ins.then_inc(probs_ready, 1)
                elif kind == "turn":
                    if i > 0:
                        dve.wait_ge(spare_done, spare(l, ("o", i - 1))[1])
                    b, v = spare(l, ("t1", i))
                    dve.wait_ge(spare_done, v)
                    ve.tensor_copy(probs_t[:, 1, :], b[:, 0:3 * P]).then_inc(turned_dve, 1)
                elif kind == "values":
                    b, v = spare(l, ("o", i))
                    dve.wait_ge(o_hi_made, n(l, i + 1, PAIRS))
                    ve.tensor_tensor(o_lo[:, i, :], b[:, 0:TOK], o_hi[:, i, :].bitcast(F32),
                                     ALU.subtract).then_inc(o_split, 1)
                elif kind == "norm":
                    b, v = spare(l, ("mean", i))
                    dve.wait_ge(spare_done, v)
                    for o in range(KC):
                        ve.tensor_tensor(gates[:, o, :], gates[:, o, :], b[:, 0:TOK],
                                         ALU.subtract).then_inc(centred, 1)
                    dve.wait_ge(spread_ready, n(l, i + 1, 2))
                    link(ve.reciprocal(rstd[:], spread[:]))
                    g0, b0 = (P_LN1G, P_LN1B) if i == 0 else (P_LN2G, P_LN2B)

                    def lo(o):
                        dve.wait_ge(x_hi_made, KC + n(l, KC * i + o + 1, 2 * KC))
                        ve.tensor_tensor(act_lo[:, o, :], xT[:, o, :], act_hi[:, o, :].bitcast(F32),
                                         ALU.subtract).then_inc(x_split, 1)

                    for o in range(KC):
                        t = gates[:, KC + o, :]
                        ve.tensor_tensor(t, gates[:, o, :], rstd[:], ALU.mult).then_inc(scaled, 1)
                        dve.wait_ge(scaled, n(l, KC * i + o + 1, 2 * KC))
                        link(ve.tensor_scalar(xT[:, o, :], t, par[:, g0 + o:g0 + o + 1], par[:, b0 + o:b0 + o + 1],
                                              ALU.mult, ALU.add))
                        if o > 0:
                            lo(o - 1)
                    lo(KC - 1)
                elif kind == "tails":
                    b, v = spare(l, ("tails", 0))
                    dve.wait_ge(spare_done, v)
                    dve.wait_ge(rows_free, n(l, 1, 1))
                    ve.tensor_copy(tails_t[:], b[0:4 * FT, 0:P]).then_inc(tails_turned, 1)

            dve.sem_inc(lo_made, SLOTS)
            dve.sem_inc(unit_used, SLOTS)
            dve.sem_inc(o_split, 1)
            dve.sem_inc(rows_free, 1)
            ve.memset(a_ext[:, :, 0:2], 0.0).then_inc(set_once, 1)
            ve.memset(ones8[:], 1.0).then_inc(set_once, 1)
            ve.memset(fparts[:], 0.0).then_inc(set_once, 1)
            ve.memset(eps_t[:], EPS).then_inc(set_once, 1)
            dve.wait_ge(masks_in, 16)
            ve.tensor_copy(cb[:], cb_wide).then_inc(set_once, 1)
            for o in range(KC):
                dve.wait_ge(spare_done, o + 1)
                ve.tensor_copy(xT[:, o, :], bank[4 + o % 4][:, 0:TOK]).then_inc(x_copied, 1)
            for o in range(KC):
                dve.wait_ge(x_hi_made, o + 1)
                ve.tensor_tensor(act_lo[:, o, :], xT[:, o, :], act_hi[:, o, :].bitcast(F32),
                                 ALU.subtract).then_inc(x_split, 1)

            with dve.Fori(0, DEPTH) as l:
                dve.wait_ge(x_split, KC * (2 * l + 1))
                dve.sem_inc(gate_pass, 1)
                dve.sem_clear(dve_chain)
                chain[0] = 0
                lo_part(l, 0)
                lo_part(l, 1)
                for u in range(NU):
                    if u + 2 < NU and UNITS[u + 2]:
                        lo_part(l, u + 2)
                    if UNITS[u]:
                        after(l, u)
                    for kind, i in SCHEDULE.get(u, []):
                        step(l, kind, i)

            for k in range(6):
                t, half = k // 2, k % 2
                w = P if t < 2 else TS
                dve.wait_ge(spare_done, FIRST + DEPTH * N_USES + k + 1)
                ve.tensor_copy(xin[0:w, t, half * 512:(half + 1) * 512], bank[4 + k % 4][0:w, :]).then_inc(y_copied, 1)


OUTS = [(1, TP, DM), (1, TS, DM),
        (DEPTH, 1, 128, 2, HD), (DEPTH, 1, 128, 2, HD), (DEPTH, 1, TP, NH, HD), (DEPTH, 1, TP, NH, HD),
        (DEPTH, 1, TP, NH), (DEPTH, 1, CONV - 1, DFF),
        (DEPTH, 1, PAST, 2, HD), (DEPTH, 1, PAST, 2, HD), (DEPTH, 1, TS, NH, HD), (DEPTH, 1, TS, NH, HD),
        (DEPTH, 1, TS, NH), (DEPTH, 1, CONV - 1, DFF)]


def kernel(**inputs):
    import concourse.bacc as bacc
    from concourse.bass_utils import run_bass_kernel_spmd

    nc = bacc.Bacc("TRN2", target_bir_lowering=False, num_devices=1)
    const_f, const_b = constants()
    arrays, A, O = {}, {}, []
    for name, value in {**inputs, "const_f": const_f, "const_b": const_b}.items():
        a = np.ascontiguousarray(value)
        arrays["in_" + name] = a
        A[name] = nc.dram_tensor("in_" + name, a.shape, mybir.dt.from_np(a.dtype), kind="ExternalInput").ap()
    for k, shape in enumerate(OUTS):
        O.append(nc.dram_tensor(f"out_{k}", shape, F32, kind="ExternalOutput").ap())
    build(nc, A, O)
    r = run_bass_kernel_spmd(nc, [arrays], core_ids=[0])
    return tuple(r.results[0][f"out_{k}"] for k in range(len(OUTS)))
```

```python
from contextlib import ExitStack

import numpy as np

import concourse.bass as bass
from concourse import mybir

P = 128
F32, F32R, BF16 = mybir.dt.float32, mybir.dt.float32r, mybir.dt.bfloat16
ALU = mybir.AluOpType
ACT = mybir.ActivationFunctionType
AX = mybir.AxisListType

DM, TP, TS, DEPTH, PAST = 1024, 256, 64, 2, 128
HD, DFF, CONV = 64, 2816, 3
CHUNK = 64
ALPHA = (2.0 * DEPTH) ** 0.25
SCALE = HD ** -0.5
EPS = 1e-5
NEG = -1e30
THETA = 10000.0
TOK = TP + TS
KC = DM // P
FT = DFF // P
KEYS = TOK + PAST
KV = 10
NH = 8
PAIRS = 8

C_QA, C_KA, C_VA, C_QB, C_KB, C_VB, C_F, C_GA, C_GB = 0, 512, 640, 768, 1280, 1792, 2304, 2312, 3336

P_STATE, P_CW, P_CB = 0, 2 * FT, 5 * FT
P_LN1G = 6 * FT
P_LN1B, P_LN2G, P_LN2B = P_LN1G + KC, P_LN1G + 2 * KC, P_LN1G + 3 * KC
P_ALL = P_LN1G + 4 * KC
ROWS_A = 5 * FT
ROWS_B = P_ALL - ROWS_A

CF_ID, CF_ROT, CF_MEAN, CF_COS, CF_SIN = 0, 128, 256, 384, 384 + TOK
CF_ALL = CF_SIN + TOK
CB_ID, CB_FOX, CB_SWA, CB_SMP, CB_SEL, CB_SELS = 0, 128, 512, 896, 1088, 1088 + NH * P
CB_ALL = CB_SELS + 4 * P

SLOTS = 4


def unit_list():
    units = [("forget", 0, KC), ("ka", 0, KC), ("va", 0, KC)]
    units += [("qa", t, KC) for t in range(4)]
    units += [("kb", t, KC) for t in range(4)] + [None]
    units += [("vb", t, KC) for t in range(4)] + [("qb", t, KC) for t in range(4)]
    for o in range(KC):
        units += [("ga", o, KC), ("gb", o, KC)]
    units += [("pab", o, KC) for o in range(KC)] + [("wo", o, KC) for o in range(KC)]
    for j in range(FT):
        units += [("gate", j, KC), ("up", j, KC)]
    for o in range(KC):
        units += [("down", o, 0), ("down", o, 1), ("down", o, 2)]
    assert len(units) % SLOTS == 0
    return units


UNITS = unit_list()
NU = len(UNITS)
AHEAD = 3
DOWN_CHUNKS = [(0, 8), (8, 15), (15, FT)]
AT = {u[:2] + ((u[2],) if u[0] == "down" else ()): n for n, u in enumerate(UNITS) if u}


GROUPED = {AT[("forget", 0)]: 3, AT[("gate", 0)]: 3}


def unit_dmas(u):
    return {"qa": 2, "pab": 3}.get(UNITS[u][0], 1)


def credit(u):
    n = 1
    while u + n < NU and UNITS[u + n] is None:
        n += 1
    return n


TILES = []
for _u in UNITS:
    if _u is None:
        continue
    if _u[0] == "pab":
        TILES += [("pa", _u[1]), ("pb", _u[1])]
    elif _u[0] != "down" or _u[2] == 0:
        TILES.append(_u[:2])
NT = len(TILES)
TILE = {t: n for n, t in enumerate(TILES)}
BY_SCALAR = ("forget", "ka", "va", "qa", "kb", "vb", "qb", "ga", "gb", "gate")
COPIED = {t: n + 1 for n, t in enumerate([t for t in TILES if t[0] in BY_SCALAR])}
N_COPIED = len(COPIED)


def last_unit(tile):
    kind, i = tile
    return AT[("pab", i)] if kind in ("pa", "pb") else AT[("down", i, 2)] if kind == "down" else AT[tile]


SCHEDULE = {}


def at_unit(u, *step):
    SCHEDULE.setdefault(u, []).append(step)


TOP = -1
at_unit(TOP, "cache", 0)
at_unit(TOP, "cache", 1)
at_unit(TOP, "params", 0)
at_unit(3, "logf", 0)
at_unit(3, "rope", 0)
at_unit(4, "rope", 1)
at_unit(5, "rope", 2)
at_unit(5, "logft", 0)
at_unit(5, "kv", 0)
at_unit(5, "kv", 1)
at_unit(6, "rope", 3)
at_unit(7, "rope", 4)
for _t in range(8):
    at_unit(9 + _t + (_t >= 4), "kv", 2 + _t)
for _p in range(PAIRS):
    _a = 8 + 3 * _p
    at_unit(_a, "scores", _p)
    at_unit(_a + 1, "soften", _p)
    at_unit(_a + 2, "turn", _p)
    at_unit(_a + 4, "values", _p)
for _k in range(4):
    at_unit(10 + 3 * _k, "sums", _k)
at_unit(AT[("pab", 2)], "root", 0)
at_unit(AT[("down", 0, 2)], "root", 1)
at_unit(AT[("wo", 1)], "shift", 0)
at_unit(AT[("down", 1, 2)], "shift", 1)
NORM_UNITS = [AT[("wo", KC - 1)], AT[("down", KC - 1, 2)]]
SQUARES_AT = {AT[("wo", o)] + 1: (0, o) for o in range(KC - 1)}
SQUARES_AT.update({AT[("down", o, 2)] + 1: (1, o) for o in range(KC - 1)})
at_unit(NORM_UNITS[0], "norm", 0)
at_unit(NORM_UNITS[1], "norm", 1)
at_unit(AT[("down", 0, 1)], "tails", 0)

USES = []
for _u in range(TOP, NU):
    for _s, _i in SCHEDULE.get(_u, []):
        if (_s, _i) == ("norm", 1):
            while len(USES) % 4 != 3:
                USES.append(None)
        USES += [(k, _i) for k in {"logf": (), "sums": (), "root": (), "soften": (), "scores": ("s0", "s1", "s2"), "turn": ("t0", "t1", "t2"),
                                   "values": ("o",), "norm": ("mean", "square")}.get(_s, (_s,))]
FROM_SHIFTED = 3
FIRST = KC
while len(USES) % 4:
    USES.append(None)
USE = {u: n for n, u in enumerate(USES) if u}
USED = {u: n + 1 for n, u in enumerate(USE)}
N_USES = len(USED)

KV_TILES = [("ka", 0), ("va", 0)] + [("kb", t) for t in range(4)] + [("vb", t) for t in range(4)]
LANDED_INPUTS = 14
STORES_KV = 8


def constants():
    f = np.zeros((P, CF_ALL), np.float32)
    f[:, CF_ID:CF_ID + P] = np.eye(P)
    for m in range(P):
        f[m + 32 if m % 64 < 32 else m - 32, CF_ROT + m] = -1.0 if m % 64 < 32 else 1.0
    f[:, CF_MEAN:CF_MEAN + P] = 1.0 / DM
    half = HD // 2
    inv = (1.0 / (np.float32(THETA) ** (np.arange(half, dtype=np.float32) / np.float32(half)))).astype(np.float32)
    pos = np.concatenate([np.arange(TP), PAST + np.arange(TS)]).astype(np.float32)
    ang = (pos[None, :] * inv[np.arange(P) % half][:, None]).astype(np.float32)
    f[:, CF_COS:CF_COS + TOK] = np.cos(ang)
    f[:, CF_SIN:CF_SIN + TOK] = np.sin(ang)

    b = np.zeros((P, CB_ALL), np.float32)
    b[:, CB_ID:CB_ID + P] = np.eye(P)
    t, s = np.arange(P)[:, None], np.arange(2 * P)[None, :]
    b[:, CB_FOX:CB_FOX + P] = np.where(s[:, :P] <= t, 0, NEG)
    b[:, CB_FOX + P:CB_FOX + 3 * P] = np.where(s <= P + t, 0, NEG)
    back = 2 * CHUNK

    def window(q, k):
        c = q // CHUNK
        return (k // CHUNK <= c) & (k // CHUNK >= c - back // CHUNK)

    b[:, CB_SWA:CB_SWA + P] = np.where(window(t, s[:, :P]), 0, NEG)
    b[:, CB_SWA + P:CB_SWA + 3 * P] = np.where(window(t + P, s), 0, NEG)
    b[:, CB_SMP:CB_SMP + TS] = np.where(s[:, :TS] <= t % TS, 0, NEG)
    for part in range(3):
        for h in range(NH):
            b[32 * part + h, CB_SEL + h * P:CB_SEL + (h + 1) * P] = 1
        for j in range(4):
            b[32 * part + 2 * j, CB_SELS + j * P:CB_SELS + j * P + 64] = 1
            b[32 * part + 2 * j + 1, CB_SELS + j * P + 64:CB_SELS + (j + 1) * P] = 1
    return f, b


def build(nc, A, O):
    (y_prompt, y_sample, p_swa_k, p_swa_v, p_fox_k, p_fox_v, p_logf, p_conv,
     s_swa_k, s_swa_v, s_fox_k, s_fox_v, s_logf, s_conv) = O
    with ExitStack() as ctx:
        def sb(name, shape, dt=F32):
            return ctx.enter_context(nc.sbuf_tensor(name, shape, dt))

        def sem(name):
            return ctx.enter_context(nc.semaphore(name))

        raw = sb("raw", [P, SLOTS, KC * P])
        w_hi = sb("w_hi", [P, SLOTS, KC, P], F32R)
        w_lo = sb("w_lo", [P, SLOTS, KC, P], F32R)
        xT = sb("xT", [P, KC, TOK])
        act_hi = sb("act_hi", [P, KC, TOK], F32R)
        act_lo = sb("act_lo", [P, KC, TOK], F32R)
        arena0 = (nc.sbuf_base + 31) // 32 * 32
        sb("arena", [P, 2 * FT * TOK])

        def within(name, first, shape, dt=F32):
            return nc.alloc_sbuf_tensor_at(name, shape, dt, offset=arena0 + 4 * first)

        h_hi = within("h_hi", 0, [P, FT, TOK], F32R)
        h_lo = within("h_lo", FT * TOK, [P, FT, TOK], F32R)
        o_hi = within("o_hi", 0, [P, PAIRS, TOK], F32R)
        o_lo = within("o_lo", PAIRS * TOK, [P, PAIRS, TOK], F32R)
        qT = within("qT", 2 * PAIRS * TOK, [P, PAIRS, TOK])
        kT = within("kT", 3 * PAIRS * TOK, [P, 5, KEYS])
        kv = within("kv", 3 * PAIRS * TOK + 5 * KEYS, [P, 3, KV * P])
        assert 3 * PAIRS * TOK + 5 * KEYS + 3 * KV * P <= 2 * FT * TOK
        gates = sb("gates", [P, 2 * KC, TOK])
        kcache = sb("kcache", [P, 5 * P])
        vcache = sb("vcache", [P, 5 * P])
        cf = sb("cf", [P, CF_ALL])
        cb = sb("cb", [P, CB_ALL], BF16)
        rows_a = sb("rows_a", [ROWS_A, P])
        rows_b = sb("rows_b", [ROWS_B, P])
        par = sb("par", [P, P_ALL])
        lf_cache = sb("lf_cache", [P, NH])
        b_f = sb("b_f", [NH, 1])
        sinks = sb("sinks", [P, NH])
        sink5 = sb("sink5", [P, 4, 5])
        fz = sb("fz", [NH, TOK])
        fe = sb("fe", [NH, TOK])
        logf = sb("logf", [NH, TOK])
        logf_c = sb("logf_c", [NH, PAST])
        ones8 = sb("ones8", [NH, TP])
        NF = P + KEYS
        fsum = sb("fsum", [NH, NF])
        fres = sb("fres", [NH, NF])
        fmid = sb("fmid", [NH, NF], BF16)
        fparts = sb("fparts", [72, NF], BF16)
        logf_t = sb("logf_t", [P, 3, NH])
        stage = sb("stage", [P, 2, TOK])
        roped_a = sb("roped_a", [P, TOK])
        roped_b = sb("roped_b", [P, TOK])
        probs = sb("probs", [P, 2, 960])
        probs_t = sb("probs_t", [P, 3, 3 * P])
        nmax = sb("nmax", [P, PAIRS, 5])
        den = sb("den", [P, PAIRS, 5])
        sink_e = sb("sink_e", [P, 4, 5])
        rden = sb("rden", [P, PAIRS, 5])
        EXT = TOK + 4
        a_ext = sb("a_ext", [P, 2, EXT])
        conv = sb("conv", [P, 2, EXT - 2])
        hf = stage
        tails = sb("tails", [P, 4 * FT])
        tails_t = sb("tails_t", [4 * FT, P])
        merged_a = probs_t[:].rearrange("p a b -> p (a b)")[:, 0:2 * TOK].rearrange("p (a b) -> p a b", a=2)
        vectors = probs[:].rearrange("p a b -> p (a b)").rearrange("p (k t) -> p k t", t=TOK)
        shift, sum_q, sum_sq, mean_q, mean_sq, spread = [vectors[:, k, :] for k in range(6)]
        rstd = roped_b
        eps_t, warm = sb("eps_t", [P, 1]), sb("warm", [P, 1])

        xin = gates[:].rearrange("p a b -> p (a b)")[:, 0:3 * DM].rearrange("p (t d) -> p t d", t=3)
        bank = [ctx.enter_context(nc.psum_tensor(f"bank{i}", [P, 512], F32)) for i in range(8)]

        id32, rot = cf[:, CF_ID:CF_ID + P], cf[:, CF_ROT:CF_ROT + P]
        mean_w = cf[:, CF_MEAN:CF_MEAN + P]
        cos, sin = cf[:, CF_COS:CF_COS + TOK], cf[:, CF_SIN:CF_SIN + TOK]
        id16 = cb[:, CB_ID:CB_ID + P]

        cb_wide = kv[:].rearrange("p a b -> p (a b)")[:, 0:CB_ALL]
        masks_in, masks_ready = sem("masks_in"), sem("masks_ready")
        tables_in = sem("tables_in")
        matrices_in = sem("matrices_in")
        x_in = [sem("x_in0"), sem("x_in1")]
        landed = [sem(f"landed{i}") for i in range(SLOTS)]
        inputs_in = sem("inputs_in")
        hi_made, lo_made = sem("hi_made"), sem("lo_made")
        unit_used = sem("unit_used")
        copied = sem("copied")
        a_gated, b_gated = sem("a_gated"), sem("b_gated")
        spare_done = sem("spare_done")
        cache_turned, logf_turned = sem("cache_turned"), sem("logf_turned")
        params_ready = sem("params_ready")
        x_copied = sem("x_copied")
        x_hi_made, x_split = sem("x_hi_made"), sem("x_split")
        z_ready, log_ready, logf_ready, f_ready = sem("z_ready"), sem("log_ready"), sem("logf_ready"), sem("f_ready")
        roped = sem("roped")
        kv_turned = sem("kv_turned")
        max_ready, exp_done, sink_done, probs_ready = (sem("max_ready"), sem("exp_done"), sem("sink_done"),
                                                       sem("probs_ready"))
        turned_act, turned_dve = sem("turned_act"), sem("turned_dve")
        o_hi_made, o_split = sem("o_hi_made"), sem("o_split")
        m_ready, m_hi_made, m_split = sem("m_ready"), sem("m_hi_made"), sem("m_split")
        r_ready, shift_ready, shifted, squared = sem("r_ready"), sem("shift_ready"), sem("shifted"), sem("squared")
        summed, mean_copied, var_ready = sem("summed"), sem("mean_copied"), sem("var_ready")
        mean_squared = sem("mean_squared")
        centred = sem("centred")
        spread_ready, scaled = sem("spread_ready"), sem("scaled")
        history_set, gate_copied, conv_begun, conv_done = (sem("history_set"), sem("gate_copied"), sem("conv_begun"),
                                                           sem("conv_done"))
        gelu_done, h_ready, h_hi_made, h_split = sem("gelu_done"), sem("h_ready"), sem("h_hi_made"), sem("h_split")
        tail_copied, tails_turned = sem("tail_copied"), sem("tails_turned")
        y_copied, y_stored = sem("y_copied"), sem("y_stored")
        rows_free = sem("rows_free")
        kv_stored, logf_stored, conv_stored, stored = (sem("kv_stored"), sem("logf_stored"), sem("conv_stored"),
                                                       sem("stored"))
        set_once = sem("set_once")
        act_chain, dve_chain = sem("act_chain"), sem("dve_chain")
        gate_pass = sem("gate_pass")

        def n(l, k, per):
            return l * per + k

        def unit_n(l, u):
            return l * NU + u

        def released(l, key):
            kind, i = key
            return {"params": (params_ready, n(l, 1, 1)), "cache": (cache_turned, n(l, i + 1, 2)),
                    "rope": (roped, n(l, i + 1, 5)), "logft": (logf_turned, n(l, 1, 1)),
                    "kv": (kv_turned, n(l, i + 1, KV)), "tails": (tails_turned, n(l, 1, 1)),
                    "s0": (exp_done, n(l, 3 * i + 1, 3 * PAIRS)), "s1": (exp_done, n(l, 3 * i + 2, 3 * PAIRS)),
                    "s2": (exp_done, n(l, 3 * i + 3, 3 * PAIRS)), "t0": (turned_act, n(l, 2 * i + 1, 2 * PAIRS)),
                    "t1": (turned_dve, n(l, i + 1, PAIRS)), "t2": (turned_act, n(l, 2 * i + 2, 2 * PAIRS)),
                    "o": (o_split, n(l, i + 1, PAIRS) + 1), "shift": (shift_ready, n(l, i + 1, 2)),
                    "mean": (mean_copied, n(l, i + 1, 2)), "square": (var_ready, n(l, i + 1, 2) + 2)}[kind]

        def tile_released(l, tile):
            kind, i = tile
            if kind in BY_SCALAR:
                return copied, n(l, COPIED[tile], N_COPIED)
            return {"pa": (a_gated, n(l, i + 1, KC)), "pb": (b_gated, n(l, i + 1, KC)),
                    "wo": (r_ready, n(l, i + 1, 2 * KC)), "down": (r_ready, n(l, KC + i + 1, 2 * KC)),
                    "up": (h_ready, n(l, i + 1, FT))}[kind]

        per_slot = [0] * SLOTS
        landed_at = []
        for u in range(NU):
            if UNITS[u]:
                per_slot[u % SLOTS] += 16 * unit_dmas(u)
            landed_at.append(per_slot[u % SLOTS])

        Y_BANKS = bank[4:7] + bank[0:3]

        block = ctx.enter_context(nc.Block())

        def value_stage(i):
            return 1 if i == 1 else i % 2

        def spare(l, key):
            return bank[4 + USE[key] % 4], FIRST + n(l, USED[key], N_USES)

        def width(u):
            kind, _, c = UNITS[u]
            return (DOWN_CHUNKS[c][1] - DOWN_CHUNKS[c][0] if kind == "down" else KC) * P

        GROUPS = [(0, 0, P), (0, P, TP), (1, 0, P), (1, P, TP), (2, 0, TS + PAST)]

        @block.sync
        def _(sp):
            sp.dma_start(cf[:, 0:CF_COS], A["const_f"][:, 0:CF_COS]).then_inc(matrices_in, 16)
            for half in range(2):
                cols = slice(half * DM // 2, (half + 1) * DM // 2)
                sp.dma_start(xin[:, 0:2, cols],
                             A["x_prompt"][0].rearrange("(t p) d -> p t d", p=P)[:, :, cols]).then_inc(x_in[half], 16)
                sp.dma_start(xin[0:TS, 2, cols], A["x_sample"][0][:, cols]).then_inc(x_in[half], 16)

            def columns(w, l, c0, width=P):
                return w[l].rearrange("(c p) e -> p c e", p=P)[:, :, c0:c0 + width]

            def small_inputs(l):
                def load(dst, src):
                    sp.dma_start(dst, src).then_inc(inputs_in, 16)

                sp.wait_ge(o_split, n(l, 1, PAIRS))
                sp.sem_inc(gate_pass, 1)
                load(rows_a[0:2 * FT, :], A["state_conv"][l, 0].rearrange("r (j p) -> (r j) p", p=P))
                load(rows_a[2 * FT:5 * FT, :], A["conv_w"][l].rearrange("r (j p) -> (r j) p", p=P))
                load(rows_b[0:FT, :], A["conv_b"][l].rearrange("(j p) -> j p", p=P))
                for k, name in enumerate(("ln1_g", "ln1_b", "ln2_g", "ln2_b")):
                    load(rows_b[FT + k * KC:FT + (k + 1) * KC, :], A[name][l].rearrange("(j p) -> j p", p=P))
                load(lf_cache[:], A["cache_fox_logf"][l, 0])
                load(b_f[:], A["b_f"][l].rearrange("(h a) -> h a", a=1))
                load(sinks[:], A["attn_sink"][l].rearrange("(a h) -> a h", a=1).to_broadcast([P, NH]))
                for tile, s, f in ((kcache, "cache_swa_k", "cache_fox_k"), (vcache, "cache_swa_v", "cache_fox_v")):
                    load(tile[:, 0:P], A[s][l, 0].rearrange("t h d -> t (h d)"))
                    load(tile[:, P:5 * P], A[f][l, 0].rearrange("t h d -> t (h d)"))

            with sp.Fori(0, DEPTH) as l:
                for u in range(NU):
                    if u == AHEAD:
                        small_inputs(l)
                    if UNITS[u] is None:
                        continue
                    kind, i, c = UNITS[u]
                    slot = u % SLOTS
                    sp.wait_ge(lo_made, unit_n(l, u + 1))
                    sp.sem_inc(gate_pass, 1)
                    flat = raw[:, slot, :]
                    dst = flat.rearrange("p (c e) -> p c e", e=P)
                    if kind == "qa":
                        for g in range(2):
                            sp.dma_start(dst[:, :, g * HD:(g + 1) * HD],
                                         columns(A["w_in"], l, C_QA + (i + 4 * g) * HD, HD)).then_inc(landed[slot], 16)
                    elif kind == "pab":
                        wa = A["w_pa"][l].rearrange("(g t p) e -> g p t e", g=2, p=HD)
                        for g in range(2):
                            sp.dma_start(dst[g * HD:(g + 1) * HD, 0:4, :],
                                         wa[g, :, :, i * P:(i + 1) * P]).then_inc(landed[slot], 16)
                        sp.dma_start(dst[:, 4:8, :], columns(A["w_pb"], l, i * P)).then_inc(landed[slot], 16)
                    elif kind == "down":
                        k0, k1 = DOWN_CHUNKS[c]
                        sp.dma_start(dst[:, 0:k1 - k0, :],
                                     columns(A["w_down"], l, i * P)[:, k0:k1, :]).then_inc(landed[slot], 16)
                    else:
                        w, c0 = {"ka": ("w_in", C_KA), "va": ("w_in", C_VA), "kb": ("w_in", C_KB),
                                 "vb": ("w_in", C_VB), "qb": ("w_in", C_QB), "ga": ("w_in", C_GA), "forget": ("w_in", C_F),
                                 "gb": ("w_in", C_GB), "wo": ("w_o", 0), "gate": ("w_gate", 0),
                                 "up": ("w_up", 0)}[kind]
                        sp.dma_start(dst, columns(A[w], l, c0 + i * P)).then_inc(landed[slot], 16)

            for half in range(2):
                cols = slice(half * DM // 2, (half + 1) * DM // 2)
                sp.wait_ge(y_copied, 3 * half + 2)
                sp.dma_start(y_prompt[0].rearrange("(t p) d -> p t d", p=P)[:, :, cols],
                             xin[:, 0:2, cols]).then_inc(y_stored, 16)
                sp.wait_ge(y_copied, 3 * half + 3)
                sp.dma_start(y_sample[0][:, cols], xin[0:TS, 2, cols]).then_inc(y_stored, 16)
            sp.wait_ge(y_stored, 64)

        @block.gpsimd
        def _(pool):
            def passed(wait_sem, value):
                pool.wait_ge(wait_sem, value)
                pool.sem_inc(gate_pass, 1)

            pool.wait_ge(x_in[1], 32)
            pool.dma_start(cf[:, CF_COS:CF_ALL], A["const_f"][:, CF_COS:CF_ALL]).then_inc(tables_in, 16)
            pool.dma_start(cb_wide, A["const_b"]).then_inc(masks_in, 16)
            pool.wait_ge(masks_in, 16)
            nc.gpsimd.tensor_copy(cb[:], cb_wide).then_inc(masks_ready, 1)

            with pool.Fori(0, DEPTH) as l:
                keep = PAST - TS
                pool.dma_start(s_swa_k[l, 0, 0:keep], A["cache_swa_k"][l, 0, TS:PAST]).then_inc(stored, 16)
                pool.dma_start(s_swa_v[l, 0, 0:keep], A["cache_swa_v"][l, 0, TS:PAST]).then_inc(stored, 16)

                passed(logf_turned, n(l, 1, 1))
                pool.dma_start(p_logf[l, 0].rearrange("(t p) h -> p t h", p=P), logf_t[:, 0:2, :]).then_inc(logf_stored, 16)
                pool.dma_start(s_logf[l, 0], logf_t[0:TS, 2, :]).then_inc(logf_stored, 16)

                def store_kv(dst_p, dst_s, f0, nf, window_only):
                    cols = slice(f0 * P, (f0 + nf) * P)
                    if window_only:
                        pool.dma_start(dst_p[l, 0].rearrange("t h d -> t (h d)"), kv[:, 1, cols]).then_inc(kv_stored, 16)
                        pool.dma_start(dst_s[l, 0, keep:PAST].rearrange("t h d -> t (h d)"),
                                       kv[0:TS, 2, cols]).then_inc(kv_stored, 16)
                    else:
                        pool.dma_start(dst_p[l, 0].rearrange("(t p) h d -> p t (h d)", p=P),
                                       kv[:, 0:2, cols]).then_inc(kv_stored, 16)
                        pool.dma_start(dst_s[l, 0].rearrange("t h d -> t (h d)"),
                                       kv[0:TS, 2, cols]).then_inc(kv_stored, 16)

                passed(kv_turned, n(l, KV, KV))
                store_kv(p_swa_k, s_swa_k, 0, 1, True)
                store_kv(p_swa_v, s_swa_v, 1, 1, True)
                store_kv(p_fox_k, s_fox_k, 2, 4, False)
                store_kv(p_fox_v, s_fox_v, 6, 4, False)

                passed(tails_turned, n(l, 1, 1))
                pool.dma_start(p_conv[l, 0].rearrange("r (j p) -> (r j) p", p=P), tails_t[0:2 * FT, :]).then_inc(conv_stored, 16)
                pool.dma_start(s_conv[l, 0].rearrange("r (j p) -> (r j) p", p=P),
                               tails_t[2 * FT:4 * FT, :]).then_inc(conv_stored, 16)
                passed(logf_stored, 32 * n(l, 1, 1))
                passed(conv_stored, 32 * n(l, 1, 1))
                pool.sem_inc(rows_free, 1)

            pool.wait_ge(kv_stored, 16 * STORES_KV * DEPTH)
            pool.wait_ge(logf_stored, 32 * DEPTH)
            pool.wait_ge(conv_stored, 32 * DEPTH)
            pool.wait_ge(stored, 32 * DEPTH)

        @block.tensor
        def _(pe):
            def claim(l, key):
                at = USE[key]
                back = at - 4
                while back >= 0 and USES[back] is None:
                    back -= 4
                if back >= 0:
                    pe.wait_ge(*released(l, USES[back]))
                elif at < 3:
                    pe.wait_ge(var_ready, n(l, 2, 2))
                return bank[4 + at % 4]

            def claim_tile(l, tile):
                at = TILE[tile]
                if at >= 4:
                    pe.wait_ge(*tile_released(l, TILES[at - 4]))
                return bank[at % 4]

            def products(out, slot, n_chunks, hi, lo, k0, begin, end, ready=None, c0=0):
                for c in range(n_chunks):
                    if ready:
                        ready(k0 + c)
                    wh, wl = w_hi[:, slot, c0 + c, :], w_lo[:, slot, c0 + c, :]
                    pe.matmul(out, wh, hi[:, k0 + c, :], start=begin and c == 0, stop=False)
                    pe.matmul(out, wh, lo[:, k0 + c, :], start=False, stop=False)
                    mm = pe.matmul(out, wl, hi[:, k0 + c, :], start=False, stop=end and c == n_chunks - 1)
                return mm

            def group(l, u0, count):
                pe.wait_ge(lo_made, unit_n(l, u0 + count) + SLOTS)
                split_n = KC if UNITS[u0][0] == "gate" else 0
                outs = [bank[TILE[UNITS[u][:2]] % 4][:, 0:TOK] for u in range(u0, u0 + count)]
                for c in range(KC):
                    pe.wait_ge(x_hi_made, n(l, split_n + c + 1, 2 * KC))
                    for k, out in enumerate(outs):
                        slot = (u0 + k) % SLOTS
                        pe.matmul(out, w_hi[:, slot, c, :], act_hi[:, c, :], start=c == 0, stop=False)
                        pe.matmul(out, w_lo[:, slot, c, :], act_hi[:, c, :], start=False, stop=False)
                    pe.wait_ge(x_split, n(l, split_n + c + 1, 2 * KC))
                    for k, out in enumerate(outs):
                        mm = pe.matmul(out, w_hi[:, (u0 + k) % SLOTS, c, :], act_lo[:, c, :], start=False,
                                       stop=c == KC - 1)
                        if c == KC - 1:
                            mm.then_inc(unit_used, 1)

            def unit(l, u):
                kind, i, c = UNITS[u]
                slot = u % SLOTS
                pe.wait_ge(lo_made, unit_n(l, u + 1) + SLOTS)
                fresh = {("pab", 0): (o_split, lambda k: n(l, k + 1, PAIRS) + 1),
                         ("wo", 0): (m_split, lambda k: n(l, k + 1, KC)),
                         ("down", 0): (h_split, lambda k: n(l, k + 1, FT))}.get((kind, i))

                def ready(k):
                    if fresh:
                        pe.wait_ge(fresh[0], fresh[1](k))

                if kind == "pab":
                    for part, k0 in (("pa", 0), ("pb", 4)):
                        out = claim_tile(l, (part, i))
                        mm = products(out[:, 0:TOK], slot, 4, o_hi, o_lo, k0, True, True, ready, c0=k0)
                elif kind == "down":
                    k0, k1 = DOWN_CHUNKS[c]
                    out = claim_tile(l, ("down", i)) if c == 0 else bank[TILE[("down", i)] % 4]
                    mm = products(out[:, 0:TOK], slot, k1 - k0, h_hi, h_lo, k0, c == 0, c == 2, ready)
                else:
                    out = claim_tile(l, (kind, i))
                    mm = products(out[:, 0:TOK], slot, KC, act_hi, act_lo, 0, True, True, ready)
                mm.then_inc(unit_used, credit(u))

            def done(mm):
                mm.then_inc(spare_done, 1)

            def turned(out, src):
                rows, cols = src.shape
                if cols == P:
                    return pe.transpose(out, src, id32[0:rows, 0:rows])
                return pe.matmul(out, src, id32[0:rows, 0:rows], start=True, stop=True)

            def settled():
                pe.sem_inc(gate_pass, 1)

            def step(l, kind, i):
                if kind == "params":
                    b = claim(l, ("params", 0))
                    turned(b[:, 0:ROWS_A], rows_a[:])
                    done(turned(b[:, ROWS_A:P_ALL], rows_b[:]))
                elif kind == "cache" and i == 0:
                    pe.wait_ge(inputs_in, 16 * n(l, LANDED_INPUTS, LANDED_INPUTS))
                    b = claim(l, ("cache", 0))
                    for t in range(4):
                        mm = turned(b[:, t * P:(t + 1) * P], kcache[:, (t + 1) * P:(t + 2) * P])
                    done(mm)
                elif kind == "cache":
                    b = claim(l, ("cache", 1))
                    turned(b[:, 0:P], kcache[:, 0:P])
                    done(turned(b[0:NH, P:2 * P], lf_cache[:]))
                elif kind == "rope":
                    b = claim(l, ("rope", i))
                    src = ("ka", 0) if i == 0 else ("qa", i - 1)
                    pe.wait_ge(copied, n(l, COPIED[src], N_COPIED))
                    x = stage[:, 0, :] if i == 0 else qT[:, i - 1, :]
                    done(pe.matmul(b[:, 0:TOK], rot, x, start=True, stop=True))
                elif kind == "logft":
                    pe.wait_ge(logf_ready, n(l, 1, 1))
                    b = claim(l, ("logft", 0))
                    settled()
                    for t in range(3):
                        w = P if t < 2 else TS
                        mm = turned(b[0:w, t * NH:(t + 1) * NH], logf[:, t * P:t * P + w])
                    done(mm)
                elif kind == "kv":
                    b = claim(l, ("kv", i))
                    if i == 0:
                        pe.wait_ge(roped, n(l, 1, 5))
                        src = kT[:, 0, :]
                    else:
                        pe.wait_ge(copied, n(l, COPIED[KV_TILES[i]], N_COPIED))
                        src = kT[:, i - 1, :] if 2 <= i < 6 else stage[:, value_stage(i), :]
                    for t in range(3):
                        w = P if t < 2 else TS
                        mm = turned(b[0:w, t * P:(t + 1) * P], src[:, t * P:t * P + w])
                    done(mm)
                elif kind == "scores":
                    scores(l, i)
                elif kind == "turn":
                    pe.wait_ge(probs_ready, n(l, i + 1, PAIRS))
                    pr = probs[:, i % 2, :]
                    for hd in range(2):
                        b = claim(l, (f"t{hd}", i))
                        for k in range(3):
                            c0 = 3 * P * hd + k * P
                            mm = turned(b[:, k * P:(k + 1) * P], pr[:, c0:c0 + P])
                        done(mm)
                    b = claim(l, ("t2", i))
                    turned(b[:, 0:P], pr[:, 6 * P + TS:6 * P + TS + PAST])
                    done(turned(b[0:TS, P:2 * P], pr[:, 6 * P:6 * P + TS]))
                elif kind == "values":
                    values(l, i)
                elif kind == "shift":
                    pe.wait_ge(r_ready, n(l, KC * i + 1, 2 * KC))
                    b = claim(l, ("shift", i))
                    done(pe.matmul(b[:, 0:TOK], mean_w, gates[:, 0, :], start=True, stop=True))
                elif kind == "norm":
                    pe.wait_ge(summed, n(l, i + 1, 2))
                    mean = claim(l, ("mean", i))[:, 0:TOK]
                    square = claim(l, ("square", i))[:, 0:TOK]
                    pe.matmul(mean, mean_w, sum_q, start=True, stop=False)
                    pe.matmul(square, mean_w, sum_sq, start=True, stop=False)
                    pe.wait_ge(r_ready, n(l, KC * i + KC, 2 * KC))
                    done(pe.matmul(mean, mean_w, gates[:, KC - 1, :], start=False, stop=True))
                    pe.wait_ge(squared, n(l, KC * i + KC, 2 * KC))
                    done(pe.matmul(square, mean_w, gates[:, 2 * KC - 1, :], start=False, stop=True))
                elif kind == "tails":
                    pe.wait_ge(tail_copied, n(l, 2 * FT, 2 * FT))
                    b = claim(l, ("tails", 0))
                    done(turned(b[0:4 * FT, 0:P], tails[:]))

            def scores(l, p):
                fox = p >= 4
                pe.wait_ge(masks_ready, 1)
                if fox:
                    pe.wait_ge(f_ready, n(l, 1, 1))
                    pe.wait_ge(copied, n(l, COPIED[("qb", p - 4)], N_COPIED))
                else:
                    pe.wait_ge(roped, n(l, p + 2, 5))
                k = kT[:, p - 3, :] if fox else kT[:, 0, :]
                mask = CB_FOX if fox else CB_SWA
                outs = []
                for hd in range(2):
                    outs.append(claim(l, (f"s{hd}", p)))
                    settled()
                for hd, b in enumerate(outs):
                    rows = slice(hd * HD, (hd + 1) * HD)
                    pe.matmul(b[:, 0:P], qT[rows, p, 0:P], k[rows, 0:P], start=True, stop=False)
                for hd, b in enumerate(outs):
                    rows = slice(hd * HD, (hd + 1) * HD)
                    pe.matmul(b[:, P:3 * P], qT[rows, p, P:TP], k[rows, 0:TP], start=False, stop=False)
                for hd, b in enumerate(outs):
                    if fox:
                        h = 2 * (p - 4) + hd
                        pe.matmul(b[:, 0:3 * P], cb[0:72, CB_SEL + h * P:CB_SEL + (h + 1) * P], fparts[:, 0:3 * P],
                                  start=False, stop=False)
                    done(pe.matmul(b[:, 0:3 * P], id16, cb[:, mask:mask + 3 * P], start=False, stop=True))
                b = claim(l, ("s2", p))
                settled()
                for hd in range(2):
                    rows = slice(hd * HD, (hd + 1) * HD)
                    mm = pe.matmul(b[rows, 0:TS + PAST], qT[rows, p, TP:TOK], k[rows, TP:KEYS],
                                   start=True, stop=not fox)
                if fox:
                    pe.matmul(b[:, 0:TS + PAST], cb[0:72, CB_SELS + (p - 4) * P:CB_SELS + (p - 3) * P],
                              fparts[:, 3 * P:3 * P + TS + PAST], start=False, stop=False)
                    mm = pe.matmul(b[:, 0:TS + PAST], id16, cb[:, CB_SMP:CB_SMP + TS + PAST], start=False, stop=True)
                done(mm)

            def values(l, p):
                fox = p >= 4
                pe.wait_ge(kv_turned, n(l, (p - 4 + 7) if fox else 2, KV))
                pe.wait_ge(turned_act, n(l, 2 * p + 2, 2 * PAIRS))
                pe.wait_ge(turned_dve, n(l, p + 1, PAIRS))
                b = claim(l, ("o", p))
                settled()
                f = 6 + p - 4 if fox else 1
                sample = P
                steps = [(lambda v, vc: kv[:, 0, v], lambda hd: probs_t[:, hd, 0:P], 0, P, True, True),
                         (lambda v, vc: kv[:, 0, v], lambda hd: probs_t[:, hd, P:2 * P], P, TP, False, False),
                         (lambda v, vc: kv[:, 1, v], lambda hd: probs_t[:, hd, 2 * P:3 * P], P, TP, False, True),
                         (lambda v, vc: vcache[:, vc], lambda hd: probs_t[:, 2, hd * TS:(hd + 1) * TS], TP, TOK, False,
                          False),
                         (lambda v, vc: kv[0:TS, 2, v],
                          lambda hd: probs_t[0:TS, 2, sample + hd * TS:sample + (hd + 1) * TS], TP, TOK, False, True)]
                for values_of, probs_of, c0, c1, start, stop in steps:
                    for hd in range(2):
                        v = slice(f * P + hd * HD, f * P + (hd + 1) * HD)
                        rows = slice(hd * HD, (hd + 1) * HD)
                        vc = slice((p - 3) * P + hd * HD, (p - 3) * P + (hd + 1) * HD) if fox else rows
                        mm = pe.matmul(b[rows, c0:c1], values_of(v, vc), probs_of(hd), start=start, stop=stop,
                                       skip_group_check=True)
                done(mm)

            pe.wait_ge(matrices_in, 16)
            for o in range(KC):
                if o % (KC // 2) == 0:
                    pe.wait_ge(x_in[2 * o // KC], 32)
                if o >= 4:
                    pe.wait_ge(x_copied, o - 3)
                for t in range(3):
                    w = P if t < 2 else TS
                    mm = turned(bank[4 + o % 4][:, t * P:t * P + w], xin[0:w, t, o * P:(o + 1) * P])
                done(mm)

            with pe.Fori(0, DEPTH) as l:
                for kind, i in SCHEDULE[TOP]:
                    step(l, kind, i)
                for u in range(NU):
                    if u in GROUPED:
                        group(l, u, GROUPED[u])
                    elif UNITS[u] and not any(u0 < u < u0 + GROUPED[u0] for u0 in GROUPED):
                        unit(l, u)
                    for kind, i in SCHEDULE.get(u, []):
                        step(l, kind, i)

            for k in range(6):
                half, t = k // 3, k % 3
                w = P if t < 2 else TS
                for c in range(4):
                    o = 4 * half + c
                    pe.wait_ge(x_split, DEPTH * 2 * KC + o + 1)
                    mm = turned(Y_BANKS[k][0:w, c * P:(c + 1) * P], xT[:, o, t * P:t * P + w])
                done(mm)

        @block.scalar
        def _(act):
            sc = nc.scalar
            chain = [0]

            def link(ins):
                chain[0] += 1
                ins.then_inc(act_chain, 1)
                act.wait_ge(act_chain, chain[0])

            def hi_part(l, u):
                kind, _, c = UNITS[u]
                slot = u % SLOTS
                act.wait_ge(landed[slot], n(l, landed_at[u], per_slot[slot]))
                act.wait_ge(unit_used, unit_n(l, u + 1))
                w = width(u)
                sc.copy(w_hi[:, slot, :, :].rearrange("p c e -> p (c e)")[:, 0:w],
                        raw[:, slot, 0:w]).then_inc(hi_made, credit(u))

            def tile_wait(l, tile):
                act.wait_ge(unit_used, SLOTS + unit_n(l, last_unit(tile) + 1))
                return bank[TILE[tile] % 4]

            def after(l, u):
                kind, i, c = UNITS[u]
                if kind == "forget":
                    b = tile_wait(l, ("forget", 0))
                    act.wait_ge(inputs_in, 16 * n(l, LANDED_INPUTS, LANDED_INPUTS))
                    sc.activation(fz[:], b[0:NH, 0:TOK], ACT.Identity, bias=b_f[:]).then_inc(copied, 1)
                elif kind in ("qa", "qb"):
                    b = tile_wait(l, (kind, i))
                    sc.activation(qT[:, i + (4 if kind == "qb" else 0), :], b[:, 0:TOK], ACT.Copy,
                                  scale=SCALE).then_inc(copied, 1)
                elif kind == "kb":
                    b = tile_wait(l, (kind, i))
                    sc.copy(kT[:, 1 + i, 0:TOK], b[:, 0:TOK]).then_inc(copied, 1)
                elif kind in ("ka", "va", "vb"):
                    b = tile_wait(l, (kind, i))
                    k = 0 if kind == "ka" else value_stage(1 if kind == "va" else 6 + i)
                    if kind == "vb":
                        back = ("kv", 6 + i - 2) if i >= 2 else ("kv", 1)
                        act.wait_ge(spare_done, spare(l, back)[1])
                        act.wait_ge(roped, n(l, 1, 5))
                    sc.copy(stage[:, k, :], b[:, 0:TOK]).then_inc(copied, 1)
                elif kind in ("ga", "gb"):
                    b = tile_wait(l, (kind, i))
                    sc.activation(gates[:, i + (KC if kind == "gb" else 0), :], b[:, 0:TOK], ACT.Tanh,
                                  scale=0.5).then_inc(copied, 1)
                elif kind == "gate":
                    b = tile_wait(l, ("gate", i))
                    e = a_ext[:, i % 2, :]
                    if i >= 2:
                        act.wait_ge(conv_done, n(l, i - 1, FT))
                    sc.copy(e[:, 2:2 + TP], b[:, 0:TP])
                    sc.copy(e[:, 4 + TP:4 + TOK], b[:, TP:TOK]).then_inc(copied, 1)
                    act.wait_ge(copied, n(l, COPIED[("gate", i)], N_COPIED))
                    act.wait_ge(history_set, n(l, i + 1, FT))
                    act.wait_ge(params_ready, n(l, 1, 1))
                    sc.activation(conv[:, i % 2, :], e[:, 2:4 + TOK], ACT.Identity,
                                  bias=par[:, P_CB + i:P_CB + i + 1],
                                  scale=par[:, P_CW + 2 * FT + i:P_CW + 2 * FT + i + 1]).then_inc(conv_begun, 1)
                    if i > 0:
                        h_part(l, i - 1)
                elif kind == "up":
                    act.wait_ge(conv_done, n(l, i + 1, FT))
                    sc.activation(conv[:, i % 2, :], conv[:, i % 2, :], ACT.Gelu_apprx_tanh).then_inc(gelu_done, 1)
                elif kind == "down" and i == 0 and c == 0:
                    h_part(l, FT - 1)
                elif u in NORM_UNITS:
                    square(l, NORM_UNITS.index(u), KC - 1)

            def merged_hi(l, i):
                act.wait_ge(m_ready, n(l, i + 1, KC))
                sc.activation(act_hi[:, i, :], merged_a[:, i % 2, :], ACT.Copy, scale=0.5).then_inc(m_hi_made, 1)

            def square(l, norm, o):
                for k in range(FROM_SHIFTED) if o == FROM_SHIFTED - 1 else (o,) if o >= FROM_SHIFTED else ():
                    if k < FROM_SHIFTED:
                        act.wait_ge(shifted, n(l, norm + 1, 2))
                    else:
                        act.wait_ge(r_ready, n(l, KC * norm + k + 1, 2 * KC))
                    sc.activation(gates[:, KC + k, :], gates[:, k, :], ACT.Square).then_inc(squared, 1)

            def h_part(l, j):
                act.wait_ge(h_ready, n(l, j + 1, FT))
                if j == 0:
                    act.wait_ge(kv_stored, 16 * n(l, STORES_KV, STORES_KV))
                sc.copy(h_hi[:, j, :], hf[:, j % 2, :]).then_inc(h_hi_made, 1)

            def step(l, kind, i):
                if kind == "logf":
                    act.wait_ge(copied, n(l, COPIED[("forget", 0)], N_COPIED))
                    link(sc.activation(fe[:], fz[:], ACT.Abs))
                    link(sc.activation(fe[:], fe[:], ACT.Exp, scale=-1.0))
                    sc.activation(fe[:], fe[:], ACT.Ln, bias=1.0).then_inc(log_ready, 1)
                elif kind == "scores":
                    pr = probs[:, i % 2, :]
                    for g, (key, c0, w) in enumerate(GROUPS):
                        b, v = spare(l, (f"s{key}", i))
                        src = b[:, c0:c0 + w]
                        if g == 0:
                            act.wait_ge(max_ready, n(l, i + 1, PAIRS))
                            if i >= 2:
                                act.wait_ge(spare_done, spare(l, ("t2", i - 2))[1])
                        at = 3 * P * key + c0
                        ins = sc.activation(pr[:, at:at + w], src, ACT.Exp, bias=nmax[:, i, g:g + 1],
                                            accum_out=den[:, i, g:g + 1])
                        if g in (1, 3, 4):
                            ins.then_inc(exp_done, 1)
                    if i < 4:
                        sc.activation(sink_e[:, i, :], sink_e[:, i, :], ACT.Exp).then_inc(sink_done, 1)
                elif kind == "turn":
                    if i > 0:
                        act.wait_ge(spare_done, spare(l, ("o", i - 1))[1])
                    b, v = spare(l, ("t0", i))
                    act.wait_ge(spare_done, v)
                    sc.copy(probs_t[:, 0, :], b[:, 0:3 * P]).then_inc(turned_act, 1)
                    b, v = spare(l, ("t2", i))
                    act.wait_ge(spare_done, v)
                    sc.copy(probs_t[:, 2, 0:P], b[:, 0:P])
                    sc.copy(probs_t[0:TS, 2, P:2 * P], b[0:TS, P:2 * P]).then_inc(turned_act, 1)
                elif kind == "values":
                    b, v = spare(l, ("o", i))
                    act.wait_ge(spare_done, v)
                    sc.copy(o_hi[:, i, :], b[:, 0:TOK]).then_inc(o_hi_made, 1)
                elif kind == "shift":
                    b, v = spare(l, ("shift", i))
                    act.wait_ge(spare_done, v)
                    sc.activation(shift, b[:, 0:TOK], ACT.Copy, scale=float(KC)).then_inc(shift_ready, 1)
                elif kind == "root":
                    sc.activation(warm[:], eps_t[:], ACT.Sqrt)
                elif kind == "norm":
                    b, v = spare(l, ("mean", i))
                    act.wait_ge(spare_done, v)
                    sc.activation(mean_sq, b[:, 0:TOK], ACT.Square).then_inc(mean_squared, 1)
                    sc.copy(mean_q, b[:, 0:TOK]).then_inc(mean_copied, 1)
                    act.wait_ge(var_ready, n(l, i + 1, 2) + 2)
                    sc.activation(spread, spread, ACT.Sqrt, bias=eps_t[:]).then_inc(spread_ready, 1)
                    g0, b0 = (P_LN1G, P_LN1B) if i == 0 else (P_LN2G, P_LN2B)
                    for o in range(KC):
                        act.wait_ge(scaled, n(l, KC * i + o + 1, 2 * KC))
                        for out in (xT[:, o, :], act_hi[:, o, :])[o == 0:]:
                            ins = sc.activation(out, gates[:, KC + o, :], ACT.Identity,
                                                bias=par[:, b0 + o:b0 + o + 1], scale=par[:, g0 + o:g0 + o + 1])
                        ins.then_inc(x_hi_made, 1)

            act.wait_ge(set_once, 4)
            for o in range(KC):
                act.wait_ge(x_copied, o + 1)
                sc.copy(act_hi[:, o, :], xT[:, o, :]).then_inc(x_hi_made, 1)
            for u in range(AHEAD):
                hi_part(0, u)
            with act.Fori(0, DEPTH) as l:
                act.wait_ge(x_hi_made, KC * (2 * l + 1))
                act.sem_inc(gate_pass, 1)
                act.sem_clear(act_chain)
                chain[0] = 0
                for kind, i in SCHEDULE[TOP]:
                    step(l, kind, i)
                for u in range(NU):
                    if u + AHEAD >= NU:
                        with act.If(l < DEPTH - 1):
                            hi_part(l + 1, u + AHEAD - NU)
                    elif UNITS[u + AHEAD]:
                        hi_part(l, u + AHEAD)
                    if AT[("pab", 0)] < u <= AT[("wo", 0)]:
                        merged_hi(l, u - 1 - AT[("pab", 0)])
                    if u in SQUARES_AT:
                        square(l, *SQUARES_AT[u])
                    if UNITS[u]:
                        after(l, u)
                    for kind, i in SCHEDULE.get(u, []):
                        step(l, kind, i)

        @block.vector
        def _(dve):
            ve = nc.vector
            chain = [0]

            def link(ins):
                chain[0] += 1
                ins.then_inc(dve_chain, 1)
                dve.wait_ge(dve_chain, chain[0])

            def lo_part(l, u):
                slot = u % SLOTS
                dve.wait_ge(hi_made, unit_n(l, u + credit(u)))
                w = width(u)
                hi = w_hi[:, slot, :, :].rearrange("p c e -> p (c e)")[:, 0:w]
                ve.tensor_tensor(w_lo[:, slot, :, :].rearrange("p c e -> p (c e)")[:, 0:w], raw[:, slot, 0:w],
                                 hi.bitcast(F32), ALU.subtract).then_inc(lo_made, credit(u))

            def tile_wait(l, tile):
                dve.wait_ge(unit_used, SLOTS + unit_n(l, last_unit(tile) + 1))
                return bank[TILE[tile] % 4]

            def after(l, u):
                kind, i, c = UNITS[u]
                if kind == "pab":
                    b = tile_wait(l, ("pa", i))
                    dve.wait_ge(copied, n(l, COPIED[("gb", i)], N_COPIED))
                    ma, g = merged_a[:, i % 2, :], gates[:, i, :]
                    if i >= 2:
                        dve.wait_ge(m_split, n(l, i - 1, KC))
                    ve.scalar_tensor_tensor(ma, g, 1.0, b[:, 0:TOK], ALU.add, ALU.mult).then_inc(a_gated, 1)
                    b = tile_wait(l, ("pb", i))
                    gb = gates[:, KC + i, :]
                    ve.scalar_tensor_tensor(gb, gb, 1.0, b[:, 0:TOK], ALU.add, ALU.mult).then_inc(b_gated, 1)
                    dve.wait_ge(b_gated, n(l, i + 1, KC))
                    ve.tensor_tensor(ma, ma, gb, ALU.add).then_inc(m_ready, 1)
                    if i > 0:
                        merged_lo(l, i - 1)
                elif kind == "wo" or (kind == "down" and c == 2):
                    norm_tile(l, kind, 0 if kind == "wo" else 1, i)
                elif kind == "gate":
                    e, cv = a_ext[:, i % 2, :], conv[:, i % 2, :]
                    if i == 0:
                        history(l, 0)
                    if i + 1 < FT:
                        history(l, i + 1)
                    dve.wait_ge(conv_begun, n(l, i + 1, FT))
                    for s, last in ((0, TP), (1, TOK + 2)):
                        ve.tensor_copy(tails[:].rearrange("p (s r j) -> p s r j", s=2, r=2)[:, s, :, i],
                                       e[:, last:last + 2]).then_inc(tail_copied, 1)
                    link(ve.scalar_tensor_tensor(cv, e[:, 1:3 + TOK], par[:, P_CW + FT + i:P_CW + FT + i + 1], cv,
                                                 ALU.mult, ALU.add))
                    ve.scalar_tensor_tensor(cv, e[:, 0:2 + TOK], par[:, P_CW + i:P_CW + i + 1], cv, ALU.mult,
                                            ALU.add).then_inc(conv_done, 1)
                    if i > 0:
                        h_part(l, i - 1)
                elif kind == "up":
                    b = tile_wait(l, ("up", i))
                    dve.wait_ge(gelu_done, n(l, i + 1, FT))
                    cv, h = conv[:, i % 2, :], hf[:, i % 2, :]
                    if i >= 2:
                        dve.wait_ge(h_split, n(l, i - 1, FT))
                    ve.tensor_tensor(h[:, 0:TP], cv[:, 0:TP], b[:, 0:TP], ALU.mult)
                    ve.tensor_tensor(h[:, TP:TOK], cv[:, TP + 2:TOK + 2], b[:, TP:TOK],
                                     ALU.mult).then_inc(h_ready, 1)
                elif kind == "down" and i == 0 and c == 0:
                    h_part(l, FT - 1)

            def merged_lo(l, i):
                dve.wait_ge(m_hi_made, n(l, i + 1, KC))
                ve.scalar_tensor_tensor(act_lo[:, i, :], merged_a[:, i % 2, :], 0.5, act_hi[:, i, :].bitcast(F32),
                                        ALU.mult, ALU.subtract).then_inc(m_split, 1)

            def norm_tile(l, kind, norm, o):
                for k in {3: (1,), 4: (2, 3)}.get(o, (o - 1,) if o > 4 else ()):
                    dve.wait_ge(squared, n(l, KC * norm + k + 1, 2 * KC))
                    if k >= FROM_SHIFTED:
                        dve.wait_ge(r_ready, n(l, KC * norm + k + 1, 2 * KC))
                    ve.tensor_tensor(sum_q, gates[:, 0, :] if k == 1 else sum_q, gates[:, k, :], ALU.add)
                    ins = ve.tensor_tensor(sum_sq, gates[:, KC, :] if k == 1 else sum_sq, gates[:, KC + k, :], ALU.add)
                    if k < KC - 2:
                        link(ins)
                    else:
                        ins.then_inc(summed, 1)
                b = tile_wait(l, (kind, o))
                if o < FROM_SHIFTED:
                    ve.scalar_tensor_tensor(gates[:, o, :], xT[:, o, :], ALPHA, b[:, 0:TOK], ALU.mult,
                                            ALU.add).then_inc(r_ready, 1)
                else:
                    ve.tensor_tensor(gates[:, o, :], gates[:, o, :], b[:, 0:TOK], ALU.add).then_inc(r_ready, 1)
                if o == FROM_SHIFTED - 1:
                    dve.wait_ge(shift_ready, n(l, norm + 1, 2))
                    dve.wait_ge(r_ready, n(l, KC * norm + o + 1, 2 * KC))
                    first = gates[:, 0:FROM_SHIFTED, :]
                    ve.tensor_tensor(first, first, shift.unsqueeze(1).to_broadcast([P, FROM_SHIFTED, TOK]),
                                     ALU.subtract).then_inc(shifted, 1)
                if FROM_SHIFTED - 1 <= o < KC - 1:
                    link(ve.scalar_tensor_tensor(gates[:, o + 1, :], xT[:, o + 1, :], ALPHA, shift, ALU.mult,
                                                 ALU.subtract))

            def history(l, j):
                if j >= 2:
                    dve.wait_ge(conv_done, n(l, j - 1, FT))
                ve.tensor_copy(a_ext[:, j % 2, TP + 2:TP + 4],
                               par[:, P_STATE:P_STATE + 2 * FT].rearrange("p (r j) -> p r j", r=2)[:, :, j])\
                    .then_inc(history_set, 1)

            def h_part(l, j):
                dve.wait_ge(h_hi_made, n(l, j + 1, FT))
                ve.tensor_tensor(h_lo[:, j, :], hf[:, j % 2, :], h_hi[:, j, :].bitcast(F32),
                                 ALU.subtract).then_inc(h_split, 1)

            def step(l, kind, i):
                if kind == "params":
                    b, v = spare(l, ("params", 0))
                    dve.wait_ge(spare_done, v)
                    ve.tensor_copy(par[:], b[:, 0:P_ALL]).then_inc(params_ready, 1)
                    for g in range(4):
                        ve.tensor_copy(sink5[:, :, g], sinks[:, 4 * (g // 2):4 * (g // 2) + 4])
                    ve.tensor_copy(sink5[0:64, :, 4], sinks[0:64, 0:4])
                    link(ve.tensor_copy(sink5[64:P, :, 4], sinks[64:P, 4:8]))
                    dve.wait_ge(params_ready, n(l, 1, 1))
                elif kind == "cache" and i == 0:
                    b, v = spare(l, ("cache", 0))
                    dve.wait_ge(spare_done, v)
                    ve.tensor_copy(kT[:, 1:5, TOK:KEYS],
                                   b[:, 0:4 * P].rearrange("p (t c) -> p t c", t=4)).then_inc(cache_turned, 1)
                elif kind == "cache":
                    b, v = spare(l, ("cache", 1))
                    dve.wait_ge(spare_done, v)
                    ve.tensor_copy(kT[:, 0, TOK:KEYS], b[:, 0:P])
                    ve.tensor_copy(logf_c[:], b[0:NH, P:2 * P]).then_inc(cache_turned, 1)
                    dve.wait_ge(cache_turned, n(l, 2, 2))
                elif kind == "logf":
                    dve.wait_ge(log_ready, n(l, 1, 1))
                    ve.scalar_tensor_tensor(logf[:], fz[:], 0.0, fe[:], ALU.min, ALU.subtract).then_inc(logf_ready, 1)
                elif kind == "sums" and i == 0:
                    dve.wait_ge(logf_ready, n(l, 1, 1))
                    cache0 = P + TOK
                    link(ve.tensor_tensor_scan(fsum[:, P:P + TP], ones8[:], logf[:, 0:TP], 0.0, ALU.mult, ALU.add))
                    link(ve.tensor_tensor_scan(fsum[:, cache0:NF], ones8[:, 0:PAST], logf_c[:], 0.0, ALU.mult,
                                               ALU.add))
                elif kind == "sums" and i == 1:
                    cache0 = P + TOK
                    link(ve.tensor_tensor_scan(fsum[:, P + TP:cache0], ones8[:, 0:TS], logf[:, TP:TOK],
                                               fsum[:, NF - 1:NF], ALU.mult, ALU.add))
                    link(ve.tensor_copy(fsum[:, 0:P], fsum[:, P:2 * P]))
                elif kind == "sums" and i == 2:
                    link(ve.tensor_scalar(fparts[0:NH, :], fsum[:], -1.0, None, ALU.mult))
                    link(ve.scalar_tensor_tensor(fres[:], fsum[:], -1.0, fparts[0:NH, :], ALU.mult, ALU.subtract))
                elif kind == "sums":
                    link(ve.tensor_copy(fmid[:], fres[:]))
                    ve.tensor_copy(fparts[32:32 + NH, :], fmid[:])
                    link(ve.tensor_tensor(fres[:], fres[:], fmid[:], ALU.subtract))
                    ve.tensor_copy(fparts[64:64 + NH, :], fres[:]).then_inc(f_ready, 1)
                elif kind == "logft":
                    b, v = spare(l, ("logft", 0))
                    dve.wait_ge(spare_done, v)
                    dve.wait_ge(rows_free, n(l, 1, 1))
                    ve.tensor_copy(logf_t[:, 0:2, :], b[:, 0:2 * NH].rearrange("p (t h) -> p t h", t=2))
                    ve.tensor_copy(logf_t[0:TS, 2, :], b[0:TS, 2 * NH:3 * NH]).then_inc(logf_turned, 1)
                elif kind == "rope":
                    x = stage[:, 0, :] if i == 0 else qT[:, i - 1, :]
                    out = kT[:, 0, 0:TOK] if i == 0 else qT[:, i - 1, :]
                    b, v = spare(l, ("rope", i))
                    dve.wait_ge(spare_done, v)
                    if i > 0:
                        dve.wait_ge(roped, n(l, i, 5))
                    dve.wait_ge(tables_in, 16)
                    ve.tensor_tensor(roped_b[:], sin, b[:, 0:TOK], ALU.mult)
                    link(ve.tensor_tensor(roped_a[:], x, cos, ALU.mult))
                    ve.tensor_tensor(out, roped_a[:], roped_b[:], ALU.add).then_inc(roped, 1)
                elif kind == "kv":
                    b, v = spare(l, ("kv", i))
                    dve.wait_ge(spare_done, v)
                    if i == 0:
                        dve.wait_ge(masks_ready, 1)
                    ve.tensor_copy(kv[:, 0:2, i * P:(i + 1) * P], b[:, 0:2 * P].rearrange("p (t c) -> p t c", t=2))
                    ve.tensor_copy(kv[0:TS, 2, i * P:(i + 1) * P], b[0:TS, 2 * P:3 * P]).then_inc(kv_turned, 1)
                elif kind == "scores":
                    for g, (key, c0, w) in enumerate(GROUPS):
                        b, v = spare(l, (f"s{key}", i))
                        if g in (0, 2, 4):
                            dve.wait_ge(spare_done, v)
                        ins = ve.tensor_reduce(nmax[:, i, g:g + 1], b[:, c0:c0 + w], AX.X, ALU.max, negate=True)
                    if i < 4:
                        link(ins)
                        link(ve.scalar_tensor_tensor(nmax[:, i, :], sink5[:, i, :], -1.0, nmax[:, i, :], ALU.mult,
                                                     ALU.min))
                        ins = ve.tensor_tensor(sink_e[:, i, :], sink5[:, i, :], nmax[:, i, :], ALU.add)
                    ins.then_inc(max_ready, 1)
                elif kind == "soften":
                    dve.wait_ge(exp_done, n(l, 3 * i + 3, 3 * PAIRS))
                    if i < 4:
                        dve.wait_ge(sink_done, n(l, i + 1, 4))
                        link(ve.tensor_tensor(den[:, i, :], den[:, i, :], sink_e[:, i, :], ALU.add))
                    link(ve.reciprocal(rden[:, i, :], den[:, i, :]))
                    for g, (key, c0, w) in enumerate(GROUPS):
                        pr = probs[:, i % 2, 3 * P * key + c0:3 * P * key + c0 + w]
                        ins = ve.tensor_scalar(pr, pr, rden[:, i, g:g + 1], None, ALU.mult)
                    ins.then_inc(probs_ready, 1)
                elif kind == "turn":
                    if i > 0:
                        dve.wait_ge(spare_done, spare(l, ("o", i - 1))[1])
                    b, v = spare(l, ("t1", i))
                    dve.wait_ge(spare_done, v)
                    ve.tensor_copy(probs_t[:, 1, :], b[:, 0:3 * P]).then_inc(turned_dve, 1)
                elif kind == "values":
                    b, v = spare(l, ("o", i))
                    dve.wait_ge(o_hi_made, n(l, i + 1, PAIRS))
                    ve.tensor_tensor(o_lo[:, i, :], b[:, 0:TOK], o_hi[:, i, :].bitcast(F32),
                                     ALU.subtract).then_inc(o_split, 1)
                elif kind == "norm":
                    dve.wait_ge(mean_squared, n(l, i + 1, 2))
                    b, v = spare(l, ("square", i))
                    dve.wait_ge(spare_done, v)
                    ve.tensor_tensor(spread, b[:, 0:TOK], mean_sq, ALU.subtract).then_inc(var_ready, 1)

                    def centre(o):
                        ve.tensor_tensor(gates[:, o, :], gates[:, o, :], mean_q, ALU.subtract).then_inc(centred, 1)

                    dve.wait_ge(mean_copied, n(l, i + 1, 2))
                    centre(0)
                    dve.wait_ge(spread_ready, n(l, i + 1, 2))
                    link(ve.reciprocal(rstd[:], spread))

                    g0, b0 = (P_LN1G, P_LN1B) if i == 0 else (P_LN2G, P_LN2B)

                    def lo(o):
                        dve.wait_ge(x_hi_made, KC + n(l, KC * i + o + 1, 2 * KC))
                        ve.tensor_tensor(act_lo[:, o, :], xT[:, o, :], act_hi[:, o, :].bitcast(F32),
                                         ALU.subtract).then_inc(x_split, 1)

                    for o in range(KC):
                        dve.wait_ge(centred, n(l, KC * i + o + 1, 2 * KC))
                        ve.tensor_tensor(gates[:, KC + o, :], gates[:, o, :], rstd[:], ALU.mult).then_inc(scaled, 1)
                        if o == 0:
                            dve.wait_ge(scaled, n(l, KC * i + 1, 2 * KC))
                            link(ve.tensor_scalar(xT[:, 0, :], gates[:, KC, :], par[:, g0:g0 + 1], par[:, b0:b0 + 1],
                                                  ALU.mult, ALU.add))
                            lo(0)
                        if o + 1 < KC:
                            centre(o + 1)
                        if o > 1:
                            lo(o - 1)
                    lo(KC - 1)
                elif kind == "tails":
                    b, v = spare(l, ("tails", 0))
                    dve.wait_ge(spare_done, v)
                    dve.wait_ge(rows_free, n(l, 1, 1))
                    ve.tensor_copy(tails_t[:], b[0:4 * FT, 0:P]).then_inc(tails_turned, 1)

            dve.sem_inc(lo_made, SLOTS)
            dve.sem_inc(unit_used, SLOTS)
            dve.sem_inc(o_split, 1)
            dve.sem_inc(rows_free, 1)
            ve.memset(a_ext[:, :, 0:2], 0.0).then_inc(set_once, 1)
            ve.memset(ones8[:], 1.0).then_inc(set_once, 1)
            ve.memset(fparts[:], 0.0).then_inc(set_once, 1)
            ve.memset(eps_t[:], EPS).then_inc(set_once, 1)
            for o in range(KC):
                dve.wait_ge(spare_done, o + 1)
                ve.tensor_copy(xT[:, o, :], bank[4 + o % 4][:, 0:TOK]).then_inc(x_copied, 1)
            dve.wait_ge(x_copied, KC)
            dve.sem_inc(var_ready, 2)
            for o in range(KC):
                dve.wait_ge(x_hi_made, o + 1)
                ve.tensor_tensor(act_lo[:, o, :], xT[:, o, :], act_hi[:, o, :].bitcast(F32),
                                 ALU.subtract).then_inc(x_split, 1)

            for u in range(AHEAD):
                lo_part(0, u)
            with dve.Fori(0, DEPTH) as l:
                dve.wait_ge(x_split, KC * (2 * l + 1))
                dve.sem_inc(gate_pass, 1)
                dve.sem_clear(dve_chain)
                chain[0] = 0
                for kind, i in SCHEDULE[TOP]:
                    step(l, kind, i)
                for u in range(NU):
                    if u == AT[("wo", 0)]:
                        merged_lo(l, KC - 1)
                    if u == NORM_UNITS[1]:
                        after(l, u)
                    if u + AHEAD >= NU:
                        with dve.If(l < DEPTH - 1):
                            lo_part(l + 1, u + AHEAD - NU)
                    elif UNITS[u + AHEAD] and u not in NORM_UNITS:
                        lo_part(l, u + AHEAD)
                    if UNITS[u] and u != NORM_UNITS[1]:
                        after(l, u)
                    if u == NORM_UNITS[0]:
                        lo_part(l, u + AHEAD)
                    for kind, i in SCHEDULE.get(u, []):
                        step(l, kind, i)

            for k in range(6):
                half, t = k // 3, k % 3
                w = P if t < 2 else TS
                dve.wait_ge(spare_done, FIRST + DEPTH * N_USES + k + 1)
                ve.tensor_copy(xin[0:w, t, half * DM // 2:(half + 1) * DM // 2], Y_BANKS[k][0:w, :]).then_inc(y_copied, 1)


OUTS = [(1, TP, DM), (1, TS, DM),
        (DEPTH, 1, 128, 2, HD), (DEPTH, 1, 128, 2, HD), (DEPTH, 1, TP, NH, HD), (DEPTH, 1, TP, NH, HD),
        (DEPTH, 1, TP, NH), (DEPTH, 1, CONV - 1, DFF),
        (DEPTH, 1, PAST, 2, HD), (DEPTH, 1, PAST, 2, HD), (DEPTH, 1, TS, NH, HD), (DEPTH, 1, TS, NH, HD),
        (DEPTH, 1, TS, NH), (DEPTH, 1, CONV - 1, DFF)]


def kernel(**inputs):
    import concourse.bacc as bacc
    from concourse.bass_utils import run_bass_kernel_spmd

    nc = bacc.Bacc("TRN2", target_bir_lowering=False, num_devices=1)
    const_f, const_b = constants()
    arrays, A, O = {}, {}, []
    for name, value in {**inputs, "const_f": const_f, "const_b": const_b}.items():
        a = np.ascontiguousarray(value)
        arrays["in_" + name] = a
        A[name] = nc.dram_tensor("in_" + name, a.shape, mybir.dt.from_np(a.dtype), kind="ExternalInput").ap()
    for k, shape in enumerate(OUTS):
        O.append(nc.dram_tensor(f"out_{k}", shape, F32, kind="ExternalOutput").ap())
    build(nc, A, O)
    r = run_bass_kernel_spmd(nc, [arrays], core_ids=[0])
    return tuple(r.results[0][f"out_{k}"] for k in range(len(OUTS)))
```

```python
from contextlib import ExitStack

import numpy as np

import concourse.bass as bass
from concourse import mybir

P = 128
F32, F32R, BF16 = mybir.dt.float32, mybir.dt.float32r, mybir.dt.bfloat16
ALU = mybir.AluOpType
ACT = mybir.ActivationFunctionType
AX = mybir.AxisListType

DM, TP, TS, DEPTH, PAST = 1024, 256, 64, 2, 128
HD, DFF, CONV = 64, 2816, 3
CHUNK = 64
ALPHA = (2.0 * DEPTH) ** 0.25
SCALE = HD ** -0.5
EPS = 1e-5
NEG = -1e30
THETA = 10000.0
TOK = TP + TS
KC = DM // P
FT = DFF // P
KEYS = TOK + PAST
KV = 10
NH = 8
PAIRS = 8

C_QA, C_KA, C_VA, C_QB, C_KB, C_VB, C_F, C_GA, C_GB = 0, 512, 640, 768, 1280, 1792, 2304, 2312, 3336

P_STATE, P_CW, P_CB = 0, 2 * FT, 5 * FT
P_LN1G = 6 * FT
P_LN1B, P_LN2G, P_LN2B = P_LN1G + KC, P_LN1G + 2 * KC, P_LN1G + 3 * KC
P_ALL = P_LN1G + 4 * KC
ROWS_A = 5 * FT
ROWS_B = P_ALL - ROWS_A

CF_ID, CF_MEAN, CF_COS, CF_SIN = 0, 128, 256, 256 + TOK
CF_ALL = CF_SIN + TOK
CB_ID, CB_FOX, CB_SWA, CB_SMP, CB_SEL, CB_SELS = 0, 128, 512, 896, 1088, 1088 + NH * P
CB_ALL = CB_SELS + 4 * P

SLOTS = 4
F_LO = 32


def unit_list():
    units = [("forget", 0, KC), ("ka", 0, KC), ("va", 0, KC)]
    units += [("qa", t, KC) for t in range(4)]
    units += [("kb", t, KC) for t in range(4)] + [None]
    units += [("vb", t, KC) for t in range(4)] + [("qb", t, KC) for t in range(4)]
    for o in range(KC):
        units += [("ga", o, KC), ("gb", o, KC)]
    units += [("pab", o, KC) for o in range(KC)] + [("wo", o, KC) for o in range(KC)]
    for j in range(FT):
        units += [("gate", j, KC), ("up", j, KC)]
    for o in range(KC):
        units += [("down", o, 0), ("down", o, 1), ("down", o, 2)]
    assert len(units) % SLOTS == 0
    return units


UNITS = unit_list()
NU = len(UNITS)
AHEAD = 3
DOWN_CHUNKS = [(0, 8), (8, 15), (15, FT)]
AT = {u[:2] + ((u[2],) if u[0] == "down" else ()): n for n, u in enumerate(UNITS) if u}


GROUP = 3


def unit_dmas(u):
    return {"qa": 2, "pab": 3}.get(UNITS[u][0], 1)


def credit(u):
    n = 1
    while u + n < NU and UNITS[u + n] is None:
        n += 1
    return n


TILES = []
for _u in UNITS:
    if _u is None:
        continue
    if _u[0] == "pab":
        TILES += [("pa", _u[1]), ("pb", _u[1])]
    elif _u[0] != "down" or _u[2] == 0:
        TILES.append(_u[:2])
TILE = {t: n for n, t in enumerate(TILES)}
BY_SCALAR = ("forget", "ka", "va", "qa", "kb", "vb", "qb", "ga", "gb", "gate")
COPIED = {t: n + 1 for n, t in enumerate([t for t in TILES if t[0] in BY_SCALAR])}
N_COPIED = len(COPIED)


def last_unit(tile):
    kind, i = tile
    return AT[("pab", i)] if kind in ("pa", "pb") else AT[("down", i, 2)] if kind == "down" else AT[tile]


SCHEDULE = {}


def at_unit(u, *step):
    SCHEDULE.setdefault(u, []).append(step)


KEY_TILES = [0, 2, 3, 4, 5]
TOP = -1
at_unit(TOP, "cache", 0)
at_unit(TOP, "cache", 1)
at_unit(TOP, "params", 0)
at_unit(7, "logf", 0)
at_unit(3, "rope", 0)
at_unit(4, "rope", 1)
at_unit(5, "rope", 2)
at_unit(9, "logft", 0)
at_unit(5, "kv", 1)
at_unit(6, "rope", 3)
at_unit(7, "rope", 4)
for _t in range(4):
    at_unit(14 + _t, "kv", 6 + _t)
for _p in range(PAIRS):
    _a = 8 + 3 * _p
    at_unit(_a, "scores", _p)
    at_unit(_a, "soften", _p)
    at_unit(_a + 2, "turn", _p)
    at_unit(_a + 4, "values", _p)
for _k in range(4):
    at_unit(10 + 3 * _k, "sums", _k)
at_unit(AT[("pab", 2)], "root", 0)
at_unit(AT[("down", 0, 2)], "root", 1)
at_unit(AT[("wo", 1)], "shift", 0)
at_unit(AT[("down", 1, 2)], "shift", 1)
NORM_UNITS = [AT[("wo", KC - 1)], AT[("down", KC - 1, 2)]]
SQUARES_AT = {AT[("wo", o)] + 1: (0, o) for o in range(KC - 1)}
SQUARES_AT.update({AT[("down", o, 2)] + 1: (1, o) for o in range(KC - 1)})
at_unit(NORM_UNITS[0], "norm", 0)
at_unit(NORM_UNITS[0], "keys", 0)
at_unit(NORM_UNITS[1], "norm", 1)
at_unit(AT[("down", 0, 1)], "tails", 0)

USES = []
for _u in range(TOP, NU):
    for _s, _i in SCHEDULE.get(_u, []):
        if (_s, _i) == ("norm", 1):
            while len(USES) % 4 != 3:
                USES.append(None)
        if _s == "keys":
            USES += [("kv", t) for t in KEY_TILES]
            continue
        USES += [(k, _i) for k in {"logf": (), "rope": (), "sums": (), "root": (), "soften": (), "scores": ("s0", "s1", "s2"), "turn": ("t0", "t1", "t2"),
                                   "values": ("o",), "norm": ("mean", "square")}.get(_s, (_s,))]
FROM_SHIFTED = 3
FIRST = KC
while len(USES) % 4:
    USES.append(None)
USE = {u: n for n, u in enumerate(USES) if u}
USED = {u: n + 1 for n, u in enumerate(USE)}
N_USES = len(USED)

KV_TILES = [("ka", 0), ("va", 0)] + [("kb", t) for t in range(4)] + [("vb", t) for t in range(4)]
LANDED_INPUTS = 12
STORES_KV = 8


def constants():
    f = np.zeros((P, CF_ALL), np.float32)
    f[:, CF_ID:CF_ID + P] = np.eye(P)
    f[:, CF_MEAN:CF_MEAN + P] = 1.0 / DM
    half = HD // 2
    inv = (1.0 / (np.float32(THETA) ** (np.arange(half, dtype=np.float32) / np.float32(half)))).astype(np.float32)
    pos = np.concatenate([np.arange(TP), PAST + np.arange(TS)]).astype(np.float32)
    ang = (pos[None, :] * inv[np.arange(P) % half][:, None]).astype(np.float32)
    f[:, CF_COS:CF_COS + TOK] = np.cos(ang)
    f[:, CF_SIN:CF_SIN + TOK] = np.sin(ang) * np.where(np.arange(P) % HD < half, -1, 1)[:, None]

    b = np.zeros((P, CB_ALL), np.float32)
    b[:, CB_ID:CB_ID + P] = np.eye(P)
    t, s = np.arange(P)[:, None], np.arange(2 * P)[None, :]
    b[:, CB_FOX:CB_FOX + P] = np.where(s[:, :P] <= t, 0, NEG)
    b[:, CB_FOX + P:CB_FOX + 3 * P] = np.where(s <= P + t, 0, NEG)
    back = 2 * CHUNK

    def window(q, k):
        c = q // CHUNK
        return (k // CHUNK <= c) & (k // CHUNK >= c - back // CHUNK)

    b[:, CB_SWA:CB_SWA + P] = np.where(window(t, s[:, :P]), 0, NEG)
    b[:, CB_SWA + P:CB_SWA + 3 * P] = np.where(window(t + P, s), 0, NEG)
    b[:, CB_SMP:CB_SMP + TS] = np.where(s[:, :TS] <= t % TS, 0, NEG)
    for part in range(3):
        for h in range(NH):
            b[32 * part + h, CB_SEL + h * P:CB_SEL + (h + 1) * P] = 1
        for j in range(4):
            b[32 * part + 2 * j, CB_SELS + j * P:CB_SELS + j * P + 64] = 1
            b[32 * part + 2 * j + 1, CB_SELS + j * P + 64:CB_SELS + (j + 1) * P] = 1
    return f, b


def build(nc, A, O):
    (y_prompt, y_sample, p_swa_k, p_swa_v, p_fox_k, p_fox_v, p_logf, p_conv,
     s_swa_k, s_swa_v, s_fox_k, s_fox_v, s_logf, s_conv) = O
    with ExitStack() as ctx:
        def sb(name, shape, dt=F32):
            return ctx.enter_context(nc.sbuf_tensor(name, shape, dt))

        def sem(name):
            return ctx.enter_context(nc.semaphore(name))

        raw = sb("raw", [P, SLOTS, KC * P])
        w_hi = sb("w_hi", [P, SLOTS, KC, P], F32R)
        w_lo = sb("w_lo", [P, SLOTS, KC, P], F32R)
        xT = sb("xT", [P, KC, TOK])
        act_hi = sb("act_hi", [P, KC, TOK], F32R)
        act_lo = sb("act_lo", [P, KC, TOK], F32R)
        arena0 = (nc.sbuf_base + 31) // 32 * 32
        sb("arena", [P, 2 * FT * TOK])

        def within(name, first, shape, dt=F32):
            return nc.alloc_sbuf_tensor_at(name, shape, dt, offset=arena0 + 4 * first)

        h_hi = within("h_hi", 0, [P, FT, TOK], F32R)
        h_lo = within("h_lo", FT * TOK, [P, FT, TOK], F32R)
        o_hi = within("o_hi", 0, [P, PAIRS, TOK], F32R)
        o_lo = within("o_lo", PAIRS * TOK, [P, PAIRS, TOK], F32R)
        qT = within("qT", 2 * PAIRS * TOK, [P, PAIRS, TOK])
        kT = within("kT", 3 * PAIRS * TOK, [P, 5, KEYS])
        kv = within("kv", 3 * PAIRS * TOK + 5 * KEYS, [P, 3, KV * P])
        assert 3 * PAIRS * TOK + 5 * KEYS + 3 * KV * P <= 2 * FT * TOK
        gates = sb("gates", [P, 2 * KC, TOK])
        kcache = sb("kcache", [P, 5 * P])
        vcache = sb("vcache", [P, 5 * P])
        cf = sb("cf", [P, CF_ALL])
        cb = sb("cb", [P, CB_ALL], BF16)
        rows_a = sb("rows_a", [ROWS_A, P])
        rows_b = sb("rows_b", [ROWS_B, P])
        par = sb("par", [P, P_ALL])
        lf_cache = sb("lf_cache", [P, NH])
        b_f = sb("b_f", [NH, 1])
        sinks = sb("sinks", [P, NH])
        sink5 = sb("sink5", [P, 4, 5])
        fz = sb("fz", [NH, TOK])
        fe = sb("fe", [NH, TOK])
        logf = sb("logf", [NH, TOK])
        logf_c = sb("logf_c", [NH, PAST])
        ones8 = sb("ones8", [NH, TP])
        NF = P + KEYS
        fsum = sb("fsum", [NH, NF])
        fres = sb("fres", [NH, NF])
        fmid = sb("fmid", [NH, NF], BF16)
        fparts = sb("fparts", [72, NF], BF16)
        logf_t = sb("logf_t", [P, 3, NH])
        stage = sb("stage", [P, 2, TOK])
        roped_a = sb("roped_a", [P, TOK])
        roped_b = sb("roped_b", [P, TOK])
        probs = sb("probs", [P, 2, 960])
        probs_t = sb("probs_t", [P, 3, 3 * P])
        nmax = sb("nmax", [P, PAIRS, 5])
        den = sb("den", [P, PAIRS, 5])
        sink_e = sb("sink_e", [P, 4, 5])
        rden = sb("rden", [P, PAIRS, 5])
        EXT = TOK + 4
        a_ext = sb("a_ext", [P, 2, EXT])
        conv = sb("conv", [P, 2, EXT - 2])
        hf = stage
        tails = sb("tails", [P, 4 * FT])
        tails_t = sb("tails_t", [4 * FT, P])
        merged_a = probs_t[:].rearrange("p a b -> p (a b)")[:, 0:2 * TOK].rearrange("p (a b) -> p a b", a=2)
        swapped = probs[:, 1, :].rearrange("p (k t) -> p k t", t=TOK)
        vectors = probs[:].rearrange("p a b -> p (a b)").rearrange("p (k t) -> p k t", t=TOK)
        shift, sum_q, sum_sq, mean_q, mean_sq, spread = [vectors[:, k, :] for k in range(6)]
        rstd = roped_b
        eps_t, warm = sb("eps_t", [P, 1]), sb("warm", [P, 1])

        xin = gates[:].rearrange("p a b -> p (a b)")[:, 0:3 * DM].rearrange("p (t d) -> p t d", t=3)
        y_rows = raw
        bank = [ctx.enter_context(nc.psum_tensor(f"bank{i}", [P, 512], F32)) for i in range(8)]

        id32 = cf[:, CF_ID:CF_ID + P]
        mean_w = cf[:, CF_MEAN:CF_MEAN + P]
        cos, sin = cf[:, CF_COS:CF_COS + TOK], cf[:, CF_SIN:CF_SIN + TOK]
        id16 = cb[:, CB_ID:CB_ID + P]

        cb_wide = kv[:].rearrange("p a b -> p (a b)")[:, 0:CB_ALL]
        masks_in, masks_ready = sem("masks_in"), sem("masks_ready")
        tables_in = sem("tables_in")
        matrices_in = sem("matrices_in")
        x_in = [sem("x_in0"), sem("x_in1")]
        landed = [sem(f"landed{i}") for i in range(SLOTS)]
        inputs_in, vcache_in = sem("inputs_in"), sem("vcache_in")
        hi_made, lo_made = sem("hi_made"), sem("lo_made")
        unit_used = sem("unit_used")
        copied = sem("copied")
        a_gated, b_gated = sem("a_gated"), sem("b_gated")
        spare_done = sem("spare_done")
        cache_turned, logf_turned = sem("cache_turned"), sem("logf_turned")
        params_ready = sem("params_ready")
        x_copied = [sem("x_copied_even"), sem("x_copied_odd")]
        x_hi_made, x_split = sem("x_hi_made"), sem("x_split")
        z_ready, log_ready, logf_ready, f_ready = sem("z_ready"), sem("log_ready"), sem("logf_ready"), sem("f_ready")
        roped = sem("roped")
        kv_turned, keys_turned = sem("kv_turned"), sem("keys_turned")
        max_ready, exp_done, sink_done, probs_ready = (sem("max_ready"), sem("exp_done"), sem("sink_done"),
                                                       sem("probs_ready"))
        turned_act, turned_dve = sem("turned_act"), sem("turned_dve")
        o_hi_made, o_split = sem("o_hi_made"), sem("o_split")
        m_ready, m_hi_made, m_split = sem("m_ready"), sem("m_hi_made"), sem("m_split")
        r_ready, shift_ready, shifted, squared = sem("r_ready"), sem("shift_ready"), sem("shifted"), sem("squared")
        prepared, added, mean_copied, var_ready = sem("prepared"), sem("added"), sem("mean_copied"), sem("var_ready")
        mean_squared = sem("mean_squared")
        centred = sem("centred")
        spread_ready, scaled = sem("spread_ready"), sem("scaled")
        history_set, conv_begun, conv_done = sem("history_set"), sem("conv_begun"), sem("conv_done")
        gelu_done, h_ready, h_hi_made, h_split = sem("gelu_done"), sem("h_ready"), sem("h_hi_made"), sem("h_split")
        tail_copied, tails_turned = sem("tail_copied"), sem("tails_turned")
        y_ready, y_turned, y_copied = sem("y_ready"), sem("y_turned"), sem("y_copied")
        y_copied_act, y_stored = sem("y_copied_act"), sem("y_stored")
        rows_free = sem("rows_free")
        kv_stored, logf_stored, conv_stored, stored = (sem("kv_stored"), sem("logf_stored"), sem("conv_stored"),
                                                       sem("stored"))
        set_once = sem("set_once")
        act_chain, dve_chain = sem("act_chain"), sem("dve_chain")
        gate_pass = sem("gate_pass")

        def n(l, k, per):
            return l * per + k

        def unit_n(l, u):
            return l * NU + u

        def values_count(i):
            return 1 if i == 1 else i - 4

        def released(l, key):
            kind, i = key
            return {"params": (params_ready, n(l, 1, 1)), "cache": (cache_turned, n(l, i + 1, 2)),
                    "logft": (logf_turned, n(l, 1, 1)),
                    "kv": (keys_turned, n(l, KEY_TILES.index(i) + 1, 5)) if i in KEY_TILES
                    else (kv_turned, n(l, values_count(i), 5)), "tails": (tails_turned, n(l, 1, 1)),
                    "s0": (exp_done, n(l, 3 * i + 1, 3 * PAIRS)), "s1": (exp_done, n(l, 3 * i + 2, 3 * PAIRS)),
                    "s2": (exp_done, n(l, 3 * i + 3, 3 * PAIRS)), "t0": (turned_act, n(l, 2 * i + 1, 2 * PAIRS)),
                    "t1": (turned_dve, n(l, i + 1, PAIRS)), "t2": (turned_act, n(l, 2 * i + 2, 2 * PAIRS)),
                    "o": (o_split, n(l, i + 1, PAIRS) + 1), "shift": (shift_ready, n(l, i + 1, 2)),
                    "mean": (mean_copied, n(l, i + 1, 2)), "square": (var_ready, n(l, i + 1, 2) + 2)}[kind]

        def tile_released(l, tile):
            kind, i = tile
            if kind in BY_SCALAR:
                return copied, n(l, COPIED[tile], N_COPIED)
            return {"pa": (a_gated, n(l, i + 1, KC)), "pb": (b_gated, n(l, i + 1, KC)),
                    "wo": (r_ready, n(l, i + 1, 2 * KC)), "down": (r_ready, n(l, KC + i + 1, 2 * KC)),
                    "up": (h_ready, n(l, i + 1, FT))}[kind]

        per_slot = [0] * SLOTS
        landed_at = []
        for u in range(NU):
            if UNITS[u]:
                per_slot[u % SLOTS] += 16 * unit_dmas(u)
            landed_at.append(per_slot[u % SLOTS])

        Y_BANKS = bank[4:7] + bank[0:3]

        block = ctx.enter_context(nc.Block())

        def value_stage(i):
            return 1 if i == 1 else i % 2

        def spare(l, key):
            return bank[4 + USE[key] % 4], FIRST + n(l, USED[key], N_USES)

        def width(u):
            kind, _, c = UNITS[u]
            return (DOWN_CHUNKS[c][1] - DOWN_CHUNKS[c][0] if kind == "down" else KC) * P

        GROUPS = [(0, 0, P), (0, P, TP), (1, 0, P), (1, P, TP), (2, 0, TS + PAST)]

        @block.sync
        def _(sp):
            sp.dma_start(cf[:, 0:CF_COS], A["const_f"][:, 0:CF_COS]).then_inc(matrices_in, 16)
            for half in range(2):
                cols = slice(half * DM // 2, (half + 1) * DM // 2)
                sp.dma_start(xin[:, 0:2, cols],
                             A["x_prompt"][0].rearrange("(t p) d -> p t d", p=P)[:, :, cols]).then_inc(x_in[half], 16)
                sp.dma_start(xin[0:TS, 2, cols], A["x_sample"][0][:, cols]).then_inc(x_in[half], 16)

            def columns(w, l, c0, width=P):
                return w[l].rearrange("(c p) e -> p c e", p=P)[:, :, c0:c0 + width]

            def small_inputs(l):
                def load(dst, src):
                    sp.dma_start(dst, src).then_inc(inputs_in, 16)

                sp.wait_ge(o_split, n(l, 1, PAIRS))
                sp.sem_inc(gate_pass, 1)
                load(rows_a[0:2 * FT, :], A["state_conv"][l, 0].rearrange("r (j p) -> (r j) p", p=P))
                load(rows_a[2 * FT:5 * FT, :], A["conv_w"][l].rearrange("r (j p) -> (r j) p", p=P))
                load(rows_b[0:FT, :], A["conv_b"][l].rearrange("(j p) -> j p", p=P))
                for k, name in enumerate(("ln1_g", "ln1_b", "ln2_g", "ln2_b")):
                    load(rows_b[FT + k * KC:FT + (k + 1) * KC, :], A[name][l].rearrange("(j p) -> j p", p=P))
                load(lf_cache[:], A["cache_fox_logf"][l, 0])
                load(b_f[:], A["b_f"][l].rearrange("(h a) -> h a", a=1))
                load(sinks[:], A["attn_sink"][l].rearrange("(a h) -> a h", a=1).to_broadcast([P, NH]))
                load(kcache[:, 0:P], A["cache_swa_k"][l, 0].rearrange("t h d -> t (h d)"))
                load(kcache[:, P:5 * P], A["cache_fox_k"][l, 0].rearrange("t h d -> t (h d)"))

            def cached_values(l):
                for cols, name in ((slice(0, P), "cache_swa_v"), (slice(P, 5 * P), "cache_fox_v")):
                    sp.dma_start(vcache[:, cols], A[name][l, 0].rearrange("t h d -> t (h d)")).then_inc(vcache_in, 16)

            with sp.Fori(0, DEPTH) as l:
                for u in range(NU):
                    if u == AHEAD:
                        small_inputs(l)
                    if u == AHEAD + 2:
                        cached_values(l)
                    if UNITS[u] is None:
                        continue
                    kind, i, c = UNITS[u]
                    slot = u % SLOTS
                    sp.wait_ge(lo_made, unit_n(l, u + 1))
                    sp.sem_inc(gate_pass, 1)
                    flat = raw[:, slot, :]
                    dst = flat.rearrange("p (c e) -> p c e", e=P)
                    if kind == "qa":
                        for g in range(2):
                            sp.dma_start(dst[:, :, g * HD:(g + 1) * HD],
                                         columns(A["w_in"], l, C_QA + (i + 4 * g) * HD, HD)).then_inc(landed[slot], 16)
                    elif kind == "pab":
                        wa = A["w_pa"][l].rearrange("(g t p) e -> g p t e", g=2, p=HD)
                        for g in range(2):
                            sp.dma_start(dst[g * HD:(g + 1) * HD, 0:4, :],
                                         wa[g, :, :, i * P:(i + 1) * P]).then_inc(landed[slot], 16)
                        sp.dma_start(dst[:, 4:8, :], columns(A["w_pb"], l, i * P)).then_inc(landed[slot], 16)
                    elif kind == "down":
                        k0, k1 = DOWN_CHUNKS[c]
                        sp.dma_start(dst[:, 0:k1 - k0, :],
                                     columns(A["w_down"], l, i * P)[:, k0:k1, :]).then_inc(landed[slot], 16)
                    else:
                        w, c0 = {"ka": ("w_in", C_KA), "va": ("w_in", C_VA), "kb": ("w_in", C_KB),
                                 "vb": ("w_in", C_VB), "qb": ("w_in", C_QB), "ga": ("w_in", C_GA), "forget": ("w_in", C_F),
                                 "gb": ("w_in", C_GB), "wo": ("w_o", 0), "gate": ("w_gate", 0),
                                 "up": ("w_up", 0)}[kind]
                        sp.dma_start(dst, columns(A[w], l, c0 + i * P)).then_inc(landed[slot], 16)

            for half in range(2):
                cols = slice(half * DM // 2, (half + 1) * DM // 2)
                sp.wait_ge(y_copied, 2 * half + 1)
                sp.dma_start(y_prompt[0, 0:P, cols], y_rows[:, 0, cols]).then_inc(y_stored, 16)
                sp.wait_ge(y_copied_act, half + 1)
                sp.dma_start(y_prompt[0, P:TP, cols], y_rows[:, 1, cols]).then_inc(y_stored, 16)
                sp.wait_ge(y_copied, 2 * half + 2)
                sp.dma_start(y_sample[0][:, cols], y_rows[0:TS, 2, cols]).then_inc(y_stored, 16)
            sp.wait_ge(y_stored, 96)

        @block.gpsimd
        def _(pool):
            def passed(wait_sem, value):
                pool.wait_ge(wait_sem, value)
                pool.sem_inc(gate_pass, 1)

            pool.wait_ge(x_in[1], 32)
            pool.dma_start(cf[:, CF_COS:CF_ALL], A["const_f"][:, CF_COS:CF_ALL]).then_inc(tables_in, 16)
            pool.dma_start(cb_wide, A["const_b"]).then_inc(masks_in, 16)
            pool.wait_ge(masks_in, 16)
            nc.gpsimd.tensor_copy(cb[:], cb_wide).then_inc(masks_ready, 1)

            with pool.Fori(0, DEPTH) as l:
                keep = PAST - TS
                pool.dma_start(s_swa_k[l, 0, 0:keep], A["cache_swa_k"][l, 0, TS:PAST]).then_inc(stored, 16)
                pool.dma_start(s_swa_v[l, 0, 0:keep], A["cache_swa_v"][l, 0, TS:PAST]).then_inc(stored, 16)

                passed(logf_turned, n(l, 1, 1))
                pool.dma_start(p_logf[l, 0].rearrange("(t p) h -> p t h", p=P), logf_t[:, 0:2, :]).then_inc(logf_stored, 16)
                pool.dma_start(s_logf[l, 0], logf_t[0:TS, 2, :]).then_inc(logf_stored, 16)

                def store_kv(dst_p, dst_s, f0, nf, window_only):
                    cols = slice(f0 * P, (f0 + nf) * P)
                    if window_only:
                        pool.dma_start(dst_p[l, 0].rearrange("t h d -> t (h d)"), kv[:, 1, cols]).then_inc(kv_stored, 16)
                        pool.dma_start(dst_s[l, 0, keep:PAST].rearrange("t h d -> t (h d)"),
                                       kv[0:TS, 2, cols]).then_inc(kv_stored, 16)
                    else:
                        pool.dma_start(dst_p[l, 0].rearrange("(t p) h d -> p t (h d)", p=P),
                                       kv[:, 0:2, cols]).then_inc(kv_stored, 16)
                        pool.dma_start(dst_s[l, 0].rearrange("t h d -> t (h d)"),
                                       kv[0:TS, 2, cols]).then_inc(kv_stored, 16)

                passed(kv_turned, n(l, 5, 5))
                store_kv(p_swa_v, s_swa_v, 1, 1, True)
                store_kv(p_fox_v, s_fox_v, 6, 4, False)
                passed(keys_turned, n(l, 5, 5))
                store_kv(p_swa_k, s_swa_k, 0, 1, True)
                store_kv(p_fox_k, s_fox_k, 2, 4, False)

                passed(tails_turned, n(l, 1, 1))
                pool.dma_start(p_conv[l, 0].rearrange("r (j p) -> (r j) p", p=P), tails_t[0:2 * FT, :]).then_inc(conv_stored, 16)
                pool.dma_start(s_conv[l, 0].rearrange("r (j p) -> (r j) p", p=P),
                               tails_t[2 * FT:4 * FT, :]).then_inc(conv_stored, 16)
                passed(logf_stored, 32 * n(l, 1, 1))
                passed(conv_stored, 32 * n(l, 1, 1))
                pool.sem_inc(rows_free, 1)

            pool.wait_ge(kv_stored, 16 * STORES_KV * DEPTH)
            pool.wait_ge(logf_stored, 32 * DEPTH)
            pool.wait_ge(conv_stored, 32 * DEPTH)
            pool.wait_ge(stored, 32 * DEPTH)

        @block.tensor
        def _(pe):
            def claim(l, key):
                at = USE[key]
                back = at - 4
                while back >= 0 and USES[back] is None:
                    back -= 4
                if back >= 0:
                    pe.wait_ge(*released(l, USES[back]))
                elif at < 3:
                    pe.wait_ge(var_ready, n(l, 2, 2))
                return bank[4 + at % 4]

            def claim_tile(l, tile):
                at = TILE[tile]
                if at >= 4:
                    pe.wait_ge(*tile_released(l, TILES[at - 4]))
                return bank[at % 4]

            def products(out, slot, n_chunks, hi, lo, k0, begin, end, ready=None, c0=0):
                for c in range(n_chunks):
                    if ready:
                        ready(k0 + c)
                    wh, wl = w_hi[:, slot, c0 + c, :], w_lo[:, slot, c0 + c, :]
                    pe.matmul(out, wh, hi[:, k0 + c, :], start=begin and c == 0, stop=False)
                    pe.matmul(out, wh, lo[:, k0 + c, :], start=False, stop=False)
                    mm = pe.matmul(out, wl, hi[:, k0 + c, :], start=False, stop=end and c == n_chunks - 1)
                return mm

            def group(l, u0, count):
                pe.wait_ge(lo_made, unit_n(l, u0 + count) + SLOTS)
                split_n = KC if UNITS[u0][0] == "gate" else 0
                outs = [bank[TILE[UNITS[u][:2]] % 4][:, 0:TOK] for u in range(u0, u0 + count)]
                for c in range(KC):
                    pe.wait_ge(x_hi_made, n(l, split_n + c + 1, 2 * KC))
                    for k, out in enumerate(outs):
                        slot = (u0 + k) % SLOTS
                        pe.matmul(out, w_hi[:, slot, c, :], act_hi[:, c, :], start=c == 0, stop=False)
                        if UNITS[u0 + k][0] == "forget":
                            continue
                        pe.matmul(out, w_lo[:, slot, c, :], act_hi[:, c, :], start=False, stop=False)
                    pe.wait_ge(x_split, n(l, split_n + c + 1, 2 * KC))
                    for k, out in enumerate(outs):
                        mm = pe.matmul(out, w_hi[:, (u0 + k) % SLOTS, c, :], act_lo[:, c, :], start=False,
                                       stop=c == KC - 1)
                        if c == KC - 1:
                            mm.then_inc(unit_used, 1)

            def unit(l, u):
                kind, i, c = UNITS[u]
                slot = u % SLOTS
                pe.wait_ge(lo_made, unit_n(l, u + 1) + SLOTS)
                fresh = {("forget", 0): (x_split, lambda k: n(l, k + 1, 2 * KC)),
                         ("pab", 0): (o_split, lambda k: n(l, k + 1, PAIRS) + 1),
                         ("wo", 0): (m_split, lambda k: n(l, k + 1, KC)),
                         ("down", 0): (h_split, lambda k: n(l, k + 1, FT))}.get((kind, i))

                def ready(k):
                    if fresh:
                        pe.wait_ge(fresh[0], fresh[1](k))

                if kind == "pab":
                    for part, k0 in (("pa", 0), ("pb", 4)):
                        out = claim_tile(l, (part, i))
                        mm = products(out[:, 0:TOK], slot, 4, o_hi, o_lo, k0, True, True, ready, c0=k0)
                elif kind == "down":
                    k0, k1 = DOWN_CHUNKS[c]
                    out = claim_tile(l, ("down", i)) if c == 0 else bank[TILE[("down", i)] % 4]
                    mm = products(out[:, 0:TOK], slot, k1 - k0, h_hi, h_lo, k0, c == 0, c == 2, ready)
                elif kind == "forget":
                    out = claim_tile(l, (kind, i))[:, 0:TOK]
                    for c in range(KC):
                        ready(c)
                        pe.matmul(out, w_hi[:, slot, c, :], act_hi[:, c, :], start=c == 0, stop=False)
                        mm = pe.matmul(out, w_hi[:, slot, c, :], act_lo[:, c, :], start=False, stop=c == KC - 1)
                else:
                    out = claim_tile(l, (kind, i))
                    mm = products(out[:, 0:TOK], slot, KC, act_hi, act_lo, 0, True, True, ready)
                mm.then_inc(unit_used, credit(u))

            def done(mm):
                mm.then_inc(spare_done, 1)

            def turned(out, src):
                rows, cols = src.shape
                if cols == P:
                    return pe.transpose(out, src, id32[0:rows, 0:rows])
                return pe.matmul(out, src, id32[0:rows, 0:rows], start=True, stop=True)

            def settled():
                pe.sem_inc(gate_pass, 1)

            def step(l, kind, i):
                if kind == "params":
                    b = claim(l, ("params", 0))
                    turned(b[:, 0:ROWS_A], rows_a[:])
                    done(turned(b[:, ROWS_A:P_ALL], rows_b[:]))
                elif kind == "cache" and i == 0:
                    pe.wait_ge(inputs_in, 16 * n(l, LANDED_INPUTS, LANDED_INPUTS))
                    b = claim(l, ("cache", 0))
                    for t in range(4):
                        mm = turned(b[:, t * P:(t + 1) * P], kcache[:, (t + 1) * P:(t + 2) * P])
                    done(mm)
                elif kind == "cache":
                    b = claim(l, ("cache", 1))
                    turned(b[:, 0:P], kcache[:, 0:P])
                    done(turned(b[0:NH, P:2 * P], lf_cache[:]))
                elif kind == "logft":
                    pe.wait_ge(logf_ready, n(l, 1, 1))
                    b = claim(l, ("logft", 0))
                    settled()
                    for t in range(3):
                        w = P if t < 2 else TS
                        mm = turned(b[0:w, t * NH:(t + 1) * NH], logf[:, t * P:t * P + w])
                    done(mm)
                elif kind == "keys":
                    for t in KEY_TILES:
                        step(l, "kv", t)
                elif kind == "kv":
                    b = claim(l, ("kv", i))
                    if i == 0:
                        pe.wait_ge(roped, n(l, 1, 5))
                        src = kT[:, 0, :]
                    else:
                        pe.wait_ge(copied, n(l, COPIED[KV_TILES[i]], N_COPIED))
                        src = kT[:, i - 1, :] if 2 <= i < 6 else stage[:, value_stage(i), :]
                    for t in range(3):
                        w = P if t < 2 else TS
                        mm = turned(b[0:w, t * P:(t + 1) * P], src[:, t * P:t * P + w])
                    done(mm)
                elif kind == "scores":
                    scores(l, i)
                elif kind == "turn":
                    pe.wait_ge(probs_ready, n(l, i + 1, PAIRS))
                    pr = probs[:, i % 2, :]
                    for hd in range(2):
                        b = claim(l, (f"t{hd}", i))
                        for k in range(3):
                            c0 = 3 * P * hd + k * P
                            mm = turned(b[:, k * P:(k + 1) * P], pr[:, c0:c0 + P])
                        done(mm)
                    b = claim(l, ("t2", i))
                    turned(b[:, 0:P], pr[:, 6 * P + TS:6 * P + TS + PAST])
                    done(turned(b[0:TS, P:2 * P], pr[:, 6 * P:6 * P + TS]))
                elif kind == "values":
                    values(l, i)
                elif kind == "shift":
                    pe.wait_ge(r_ready, n(l, KC * i + 1, 2 * KC))
                    b = claim(l, ("shift", i))
                    done(pe.matmul(b[:, 0:TOK], mean_w, gates[:, 0, :], start=True, stop=True))
                elif kind == "norm":
                    pe.wait_ge(added, n(l, (KC - 2) * (i + 1), 2 * (KC - 2)))
                    mean = claim(l, ("mean", i))[:, 0:TOK]
                    settled()
                    square = claim(l, ("square", i))[:, 0:TOK]
                    pe.matmul(mean, mean_w, sum_q, start=True, stop=False)
                    pe.matmul(square, mean_w, sum_sq, start=True, stop=False)
                    pe.wait_ge(r_ready, n(l, KC * i + KC, 2 * KC))
                    done(pe.matmul(mean, mean_w, gates[:, KC - 1, :], start=False, stop=True))
                    pe.wait_ge(squared, n(l, KC * i + KC, 2 * KC))
                    done(pe.matmul(square, mean_w, gates[:, 2 * KC - 1, :], start=False, stop=True))
                elif kind == "tails":
                    pe.wait_ge(tail_copied, n(l, 2 * FT, 2 * FT))
                    b = claim(l, ("tails", 0))
                    done(turned(b[0:4 * FT, 0:P], tails[:]))

            def scores(l, p):
                fox = p >= 4
                pe.wait_ge(masks_ready, 1)
                if fox:
                    pe.wait_ge(f_ready, n(l, 1, 1))
                    pe.wait_ge(copied, n(l, COPIED[("qb", p - 4)], N_COPIED))
                else:
                    pe.wait_ge(roped, n(l, p + 2, 5))
                k = kT[:, p - 3, :] if fox else kT[:, 0, :]
                mask = CB_FOX if fox else CB_SWA
                outs = []
                for hd in range(2):
                    outs.append(claim(l, (f"s{hd}", p)))
                    settled()
                for hd, b in enumerate(outs):
                    rows = slice(hd * HD, (hd + 1) * HD)
                    pe.matmul(b[:, 0:P], qT[rows, p, 0:P], k[rows, 0:P], start=True, stop=False)
                for hd, b in enumerate(outs):
                    rows = slice(hd * HD, (hd + 1) * HD)
                    pe.matmul(b[:, P:3 * P], qT[rows, p, P:TP], k[rows, 0:TP], start=False, stop=False)
                for hd, b in enumerate(outs):
                    if fox:
                        h = 2 * (p - 4) + hd
                        pe.matmul(b[:, 0:3 * P], cb[0:72, CB_SEL + h * P:CB_SEL + (h + 1) * P], fparts[:, 0:3 * P],
                                  start=False, stop=False)
                    done(pe.matmul(b[:, 0:3 * P], id16, cb[:, mask:mask + 3 * P], start=False, stop=True))
                b = claim(l, ("s2", p))
                settled()
                for hd in range(2):
                    rows = slice(hd * HD, (hd + 1) * HD)
                    mm = pe.matmul(b[rows, 0:TS + PAST], qT[rows, p, TP:TOK], k[rows, TP:KEYS],
                                   start=True, stop=not fox)
                if fox:
                    pe.matmul(b[:, 0:TS + PAST], cb[0:72, CB_SELS + (p - 4) * P:CB_SELS + (p - 3) * P],
                              fparts[:, 3 * P:3 * P + TS + PAST], start=False, stop=False)
                    mm = pe.matmul(b[:, 0:TS + PAST], id16, cb[:, CB_SMP:CB_SMP + TS + PAST], start=False, stop=True)
                done(mm)

            def values(l, p):
                fox = p >= 4
                pe.wait_ge(vcache_in, 32 * n(l, 1, 1))
                pe.wait_ge(kv_turned, n(l, values_count(6 + p - 4) if fox else 1, 5))
                pe.wait_ge(turned_act, n(l, 2 * p + 2, 2 * PAIRS))
                pe.wait_ge(turned_dve, n(l, p + 1, PAIRS))
                b = claim(l, ("o", p))
                settled()
                f = 6 + p - 4 if fox else 1
                sample = P
                steps = [(lambda v, vc: kv[:, 0, v], lambda hd: probs_t[:, hd, 0:P], 0, P, True, True),
                         (lambda v, vc: kv[:, 0, v], lambda hd: probs_t[:, hd, P:2 * P], P, TP, False, False),
                         (lambda v, vc: kv[:, 1, v], lambda hd: probs_t[:, hd, 2 * P:3 * P], P, TP, False, True),
                         (lambda v, vc: vcache[:, vc], lambda hd: probs_t[:, 2, hd * TS:(hd + 1) * TS], TP, TOK, False,
                          False),
                         (lambda v, vc: kv[0:TS, 2, v],
                          lambda hd: probs_t[0:TS, 2, sample + hd * TS:sample + (hd + 1) * TS], TP, TOK, False, True)]
                for values_of, probs_of, c0, c1, start, stop in steps:
                    for hd in range(2):
                        v = slice(f * P + hd * HD, f * P + (hd + 1) * HD)
                        rows = slice(hd * HD, (hd + 1) * HD)
                        vc = slice((p - 3) * P + hd * HD, (p - 3) * P + (hd + 1) * HD) if fox else rows
                        mm = pe.matmul(b[rows, c0:c1], values_of(v, vc), probs_of(hd), start=start, stop=stop,
                                       skip_group_check=True)
                done(mm)

            pe.wait_ge(matrices_in, 16)
            for o in range(KC):
                if o % (KC // 2) == 0:
                    pe.wait_ge(x_in[2 * o // KC], 32)
                if o >= 4:
                    pe.wait_ge(x_copied[o % 2], o // 2 - 1)
                for t in range(3):
                    w = P if t < 2 else TS
                    mm = turned(bank[4 + o % 4][:, t * P:t * P + w], xin[0:w, t, o * P:(o + 1) * P])
                done(mm)

            with pe.Fori(0, DEPTH) as l:
                with pe.If(l > 0):
                    for kind, i in SCHEDULE[TOP]:
                        step(l, kind, i)
                    group(l, 0, GROUP)
                with pe.Else():
                    for u in range(GROUP):
                        unit(l, u)
                    for kind, i in SCHEDULE[TOP]:
                        step(l, kind, i)
                for u in range(NU):
                    if u == AT[("gate", 0)]:
                        group(l, u, GROUP)
                    elif UNITS[u] and u >= GROUP and not 0 < u - AT[("gate", 0)] < GROUP:
                        unit(l, u)
                    for kind, i in SCHEDULE.get(u, []):
                        step(l, kind, i)

            for o in range(KC):
                pe.wait_ge(y_ready, o + 1)
                for t in range(3):
                    w, c = P if t < 2 else TS, o % (KC // 2)
                    mm = turned(Y_BANKS[3 * (o // (KC // 2)) + t][0:w, c * P:(c + 1) * P], xT[:, o, t * P:t * P + w])
                    if c == KC // 2 - 1:
                        mm.then_inc(y_turned, 1)

        @block.scalar
        def _(act):
            sc = nc.scalar
            chain = [0]

            def link(ins):
                chain[0] += 1
                ins.then_inc(act_chain, 1)
                act.wait_ge(act_chain, chain[0])

            def hi_part(l, u):
                kind, _, c = UNITS[u]
                slot = u % SLOTS
                act.wait_ge(landed[slot], n(l, landed_at[u], per_slot[slot]))
                act.wait_ge(unit_used, unit_n(l, u + 1))
                if UNITS[u][0] == "forget":
                    sc.copy(w_hi[:, slot, :, 0:NH],
                            raw[:, slot, :].rearrange("p (c e) -> p c e", e=P)[:, :, 0:NH]).then_inc(hi_made, credit(u))
                    return
                w = width(u)
                sc.copy(w_hi[:, slot, :, :].rearrange("p c e -> p (c e)")[:, 0:w],
                        raw[:, slot, 0:w]).then_inc(hi_made, credit(u))

            def tile_wait(l, tile):
                act.wait_ge(unit_used, SLOTS + unit_n(l, last_unit(tile) + 1))
                return bank[TILE[tile] % 4]

            def after(l, u):
                kind, i, c = UNITS[u]
                if kind == "forget":
                    b = tile_wait(l, ("forget", 0))
                    act.wait_ge(inputs_in, 16 * n(l, LANDED_INPUTS, LANDED_INPUTS))
                    sc.activation(fz[:], b[0:NH, 0:TOK], ACT.Identity, bias=b_f[:])
                    sc.copy(fe[:], b[F_LO:F_LO + NH, 0:TOK]).then_inc(copied, 1)
                elif kind in ("qa", "qb"):
                    b = tile_wait(l, (kind, i))
                    if kind == "qa":
                        swap(l, i + 1, b, SCALE)
                    sc.activation(qT[:, i + (4 if kind == "qb" else 0), :], b[:, 0:TOK], ACT.Copy,
                                  scale=SCALE).then_inc(copied, 1)
                elif kind == "kb":
                    b = tile_wait(l, (kind, i))
                    sc.copy(kT[:, 1 + i, 0:TOK], b[:, 0:TOK]).then_inc(copied, 1)
                elif kind in ("ka", "va", "vb"):
                    b = tile_wait(l, (kind, i))
                    k = 0 if kind == "ka" else value_stage(1 if kind == "va" else 6 + i)
                    if kind == "vb":
                        back = ("kv", 6 + i - 2) if i >= 2 else ("kv", 1)
                        act.wait_ge(spare_done, spare(l, back)[1])
                        act.wait_ge(roped, n(l, 1, 5))
                    if kind == "ka":
                        swap(l, 0, b, 1.0)
                    sc.copy(stage[:, k, :], b[:, 0:TOK]).then_inc(copied, 1)
                elif kind in ("ga", "gb"):
                    b = tile_wait(l, (kind, i))
                    sc.activation(gates[:, i + (KC if kind == "gb" else 0), :], b[:, 0:TOK], ACT.Tanh,
                                  scale=0.5).then_inc(copied, 1)
                elif kind == "gate":
                    b = tile_wait(l, ("gate", i))
                    e = a_ext[:, i % 2, :]
                    if i >= 2:
                        act.wait_ge(conv_done, n(l, i - 1, FT))
                    sc.copy(e[:, 2:2 + TP], b[:, 0:TP])
                    sc.copy(e[:, 4 + TP:4 + TOK], b[:, TP:TOK]).then_inc(copied, 1)
                    act.wait_ge(copied, n(l, COPIED[("gate", i)], N_COPIED))
                    act.wait_ge(history_set, n(l, i + 1, FT))
                    act.wait_ge(params_ready, n(l, 1, 1))
                    sc.activation(conv[:, i % 2, :], e[:, 2:4 + TOK], ACT.Identity,
                                  bias=par[:, P_CB + i:P_CB + i + 1],
                                  scale=par[:, P_CW + 2 * FT + i:P_CW + 2 * FT + i + 1]).then_inc(conv_begun, 1)
                    if i > 0:
                        h_part(l, i - 1)
                elif kind == "up":
                    act.wait_ge(conv_done, n(l, i + 1, FT))
                    sc.activation(conv[:, i % 2, :], conv[:, i % 2, :], ACT.Gelu_apprx_tanh).then_inc(gelu_done, 1)
                elif kind == "down" and i == 0 and c == 0:
                    h_part(l, FT - 1)
                elif u in NORM_UNITS:
                    square(l, NORM_UNITS.index(u), KC - 1)

            def swap(l, i, b, scale):
                if i >= 3:
                    act.wait_ge(roped, n(l, i - 2, 5))
                for p0 in range(0, P, HD // 2):
                    other = p0 + HD // 2 if p0 % HD == 0 else p0 - HD // 2
                    sc.activation(swapped[p0:p0 + HD // 2, i % 3, :], b[other:other + HD // 2, 0:TOK], ACT.Copy,
                                  scale=scale)

            def merged_hi(l, i):
                act.wait_ge(m_ready, n(l, i + 1, KC))
                sc.activation(act_hi[:, i, :], merged_a[:, i % 2, :], ACT.Copy, scale=0.5).then_inc(m_hi_made, 1)

            def square(l, norm, o):
                for k in range(FROM_SHIFTED) if o == FROM_SHIFTED - 1 else (o,) if o >= FROM_SHIFTED else ():
                    if k < FROM_SHIFTED:
                        act.wait_ge(shifted, n(l, norm + 1, 2))
                    else:
                        act.wait_ge(r_ready, n(l, KC * norm + k + 1, 2 * KC))
                    sc.activation(gates[:, KC + k, :], gates[:, k, :], ACT.Square).then_inc(squared, 1)

            def h_part(l, j):
                act.wait_ge(h_ready, n(l, j + 1, FT))
                if j == 8:
                    act.wait_ge(kv_stored, 16 * n(l, STORES_KV, STORES_KV))
                sc.copy(h_hi[:, j, :], hf[:, j % 2, :]).then_inc(h_hi_made, 1)

            def keys_out(l, t):
                b, v = spare(l, ("kv", t))
                act.wait_ge(spare_done, v)
                sc.copy(kv[:, 0:2, t * P:(t + 1) * P], b[:, 0:2 * P].rearrange("p (t c) -> p t c", t=2))
                sc.copy(kv[0:TS, 2, t * P:(t + 1) * P], b[0:TS, 2 * P:3 * P]).then_inc(keys_turned, 1)

            def step(l, kind, i):
                if kind == "logf":
                    act.wait_ge(z_ready, n(l, 1, 1))
                    link(sc.activation(fe[:], fz[:], ACT.Abs))
                    link(sc.activation(fe[:], fe[:], ACT.Exp, scale=-1.0))
                    sc.activation(fe[:], fe[:], ACT.Ln, bias=1.0).then_inc(log_ready, 1)
                elif kind == "scores":
                    pr = probs[:, i % 2, :]
                    for g, (key, c0, w) in enumerate(GROUPS):
                        b, v = spare(l, (f"s{key}", i))
                        src = b[:, c0:c0 + w]
                        if g == 0:
                            act.wait_ge(max_ready, n(l, i + 1, PAIRS))
                            if i >= 2:
                                act.wait_ge(spare_done, spare(l, ("t2", i - 2))[1])
                        at = 3 * P * key + c0
                        ins = sc.activation(pr[:, at:at + w], src, ACT.Exp, bias=nmax[:, i, g:g + 1],
                                            accum_out=den[:, i, g:g + 1])
                        if g in (1, 3, 4):
                            ins.then_inc(exp_done, 1)
                    if i < 4:
                        sc.activation(sink_e[:, i, :], sink_e[:, i, :], ACT.Exp).then_inc(sink_done, 1)
                elif kind == "turn":
                    if i > 0:
                        act.wait_ge(spare_done, spare(l, ("o", i - 1))[1])
                    b, v = spare(l, ("t0", i))
                    act.wait_ge(spare_done, v)
                    sc.copy(probs_t[:, 0, :], b[:, 0:3 * P]).then_inc(turned_act, 1)
                    b, v = spare(l, ("t2", i))
                    act.wait_ge(spare_done, v)
                    sc.copy(probs_t[:, 2, 0:P], b[:, 0:P])
                    sc.copy(probs_t[0:TS, 2, P:2 * P], b[0:TS, P:2 * P]).then_inc(turned_act, 1)
                elif kind == "values":
                    b, v = spare(l, ("o", i))
                    act.wait_ge(spare_done, v)
                    sc.copy(o_hi[:, i, :], b[:, 0:TOK]).then_inc(o_hi_made, 1)
                elif kind == "shift":
                    b, v = spare(l, ("shift", i))
                    act.wait_ge(spare_done, v)
                    sc.activation(shift, b[:, 0:TOK], ACT.Copy, scale=float(KC)).then_inc(shift_ready, 1)
                elif kind == "root":
                    sc.activation(warm[:], eps_t[:], ACT.Sqrt)
                elif kind == "norm":
                    b, v = spare(l, ("mean", i))
                    act.wait_ge(spare_done, v)
                    sc.activation(mean_sq, b[:, 0:TOK], ACT.Square).then_inc(mean_squared, 1)
                    sc.copy(mean_q, b[:, 0:TOK]).then_inc(mean_copied, 1)
                    act.wait_ge(var_ready, n(l, i + 1, 2) + 2)
                    sc.activation(spread, spread, ACT.Sqrt, bias=eps_t[:]).then_inc(spread_ready, 1)
                    g0, b0 = (P_LN1G, P_LN1B) if i == 0 else (P_LN2G, P_LN2B)

                    def affine(out, o):
                        return sc.activation(out, gates[:, KC + o, :], ACT.Identity, bias=par[:, b0 + o:b0 + o + 1],
                                             scale=par[:, g0 + o:g0 + o + 1])

                    def split_tiles():
                        for o in range(KC):
                            act.wait_ge(scaled, n(l, KC * i + o + 1, 2 * KC))
                            if o > 0:
                                affine(xT[:, o, :], o)
                            affine(act_hi[:, o, :], o).then_inc(x_hi_made, 1)

                    def output_tiles():
                        for o in range(KC):
                            act.wait_ge(scaled, n(l, KC * i + o + 1, 2 * KC))
                            affine(xT[:, o, :], o).then_inc(y_ready, 1)

                    if i == 0:
                        hi_part(l, NORM_UNITS[0] + 4)
                        for t in KEY_TILES[0:3]:
                            keys_out(l, t)
                        split_tiles()
                        for t in KEY_TILES[3:]:
                            keys_out(l, t)
                    else:
                        with act.If(l < DEPTH - 1):
                            hi_part(l + 1, 3)
                            split_tiles()
                        with act.Else():
                            output_tiles()

            act.wait_ge(set_once, 5)
            sc.copy(warm[:], eps_t[:])
            for o in range(1, KC, 2):
                act.wait_ge(spare_done, o + 1)
                sc.copy(xT[:, o, :], bank[4 + o % 4][:, 0:TOK]).then_inc(x_copied[1], 1)
                for k in (o - 1, o):
                    act.wait_ge(x_copied[k % 2], k // 2 + 1)
                    sc.copy(act_hi[:, k, :], xT[:, k, :]).then_inc(x_hi_made, 1)
                if o == 5:
                    hi_part(0, 0)
            for u in range(1, SLOTS):
                hi_part(0, u)
            with act.Fori(0, DEPTH) as l:
                act.wait_ge(x_hi_made, KC * (2 * l + 1))
                act.sem_inc(gate_pass, 1)
                act.sem_clear(act_chain)
                chain[0] = 0
                sc.activation(warm[:], eps_t[:], ACT.Exp)
                for kind, i in SCHEDULE[TOP]:
                    step(l, kind, i)
                for u in range(NU):
                    if u + AHEAD >= NU:
                        with act.If(l < DEPTH - 1):
                            hi_part(l + 1, u + AHEAD - NU)
                    elif UNITS[u + AHEAD] and u not in (0, NORM_UNITS[0] + 1):
                        hi_part(l, u + AHEAD)
                    if AT[("pab", 0)] < u <= AT[("wo", 0)]:
                        merged_hi(l, u - 1 - AT[("pab", 0)])
                    if u in SQUARES_AT:
                        square(l, *SQUARES_AT[u])
                    if UNITS[u]:
                        after(l, u)
                    for kind, i in SCHEDULE.get(u, []):
                        step(l, kind, i)

            for half in range(2):
                act.wait_ge(y_turned, 3 * half + 2)
                sc.copy(y_rows[:, 1, half * DM // 2:(half + 1) * DM // 2],
                        Y_BANKS[3 * half + 1][:]).then_inc(y_copied_act, 1)

        @block.vector
        def _(dve):
            ve = nc.vector
            chain = [0]

            def link(ins):
                chain[0] += 1
                ins.then_inc(dve_chain, 1)
                dve.wait_ge(dve_chain, chain[0])

            def lo_part(l, u):
                slot = u % SLOTS
                dve.wait_ge(hi_made, unit_n(l, u + credit(u)))
                if UNITS[u][0] == "forget":
                    chunks = w_hi[:, slot, :, :]
                    ve.tensor_tensor(chunks[:, :, F_LO:F_LO + NH],
                                     raw[:, slot, :].rearrange("p (c e) -> p c e", e=P)[:, :, 0:NH],
                                     chunks[:, :, 0:NH].bitcast(F32), ALU.subtract).then_inc(lo_made, credit(u))
                    return
                w = width(u)
                hi = w_hi[:, slot, :, :].rearrange("p c e -> p (c e)")[:, 0:w]
                ve.tensor_tensor(w_lo[:, slot, :, :].rearrange("p c e -> p (c e)")[:, 0:w], raw[:, slot, 0:w],
                                 hi.bitcast(F32), ALU.subtract).then_inc(lo_made, credit(u))

            def tile_wait(l, tile):
                dve.wait_ge(unit_used, SLOTS + unit_n(l, last_unit(tile) + 1))
                return bank[TILE[tile] % 4]

            def after(l, u):
                kind, i, c = UNITS[u]
                if kind == "forget":
                    dve.wait_ge(copied, n(l, COPIED[("forget", 0)], N_COPIED))
                    ve.tensor_tensor(fz[:], fz[:], fe[:], ALU.add).then_inc(z_ready, 1)
                elif kind == "pab":
                    b = tile_wait(l, ("pa", i))
                    dve.wait_ge(copied, n(l, COPIED[("gb", i)], N_COPIED))
                    ma, g = merged_a[:, i % 2, :], gates[:, i, :]
                    if i >= 2:
                        dve.wait_ge(m_split, n(l, i - 1, KC))
                    ve.scalar_tensor_tensor(ma, g, 1.0, b[:, 0:TOK], ALU.add, ALU.mult).then_inc(a_gated, 1)
                    b = tile_wait(l, ("pb", i))
                    gb = gates[:, KC + i, :]
                    ve.scalar_tensor_tensor(gb, gb, 1.0, b[:, 0:TOK], ALU.add, ALU.mult).then_inc(b_gated, 1)
                    dve.wait_ge(b_gated, n(l, i + 1, KC))
                    ve.tensor_tensor(ma, ma, gb, ALU.add).then_inc(m_ready, 1)
                    if i > 0:
                        merged_lo(l, i - 1)
                elif kind == "wo" or (kind == "down" and c == 2):
                    norm_tile(l, kind, 0 if kind == "wo" else 1, i)
                elif kind == "gate":
                    e, cv = a_ext[:, i % 2, :], conv[:, i % 2, :]
                    if i == 0:
                        history(l, 0)
                    if i + 1 < FT:
                        history(l, i + 1)
                    dve.wait_ge(conv_begun, n(l, i + 1, FT))
                    for s, last in ((0, TP), (1, TOK + 2)):
                        ve.tensor_copy(tails[:].rearrange("p (s r j) -> p s r j", s=2, r=2)[:, s, :, i],
                                       e[:, last:last + 2]).then_inc(tail_copied, 1)
                    link(ve.scalar_tensor_tensor(cv, e[:, 1:3 + TOK], par[:, P_CW + FT + i:P_CW + FT + i + 1], cv,
                                                 ALU.mult, ALU.add))
                    ve.scalar_tensor_tensor(cv, e[:, 0:2 + TOK], par[:, P_CW + i:P_CW + i + 1], cv, ALU.mult,
                                            ALU.add).then_inc(conv_done, 1)
                    if i > 0:
                        h_part(l, i - 1)
                elif kind == "up":
                    b = tile_wait(l, ("up", i))
                    dve.wait_ge(gelu_done, n(l, i + 1, FT))
                    cv, h = conv[:, i % 2, :], hf[:, i % 2, :]
                    if i >= 2:
                        dve.wait_ge(h_split, n(l, i - 1, FT))
                    ve.tensor_tensor(h[:, 0:TP], cv[:, 0:TP], b[:, 0:TP], ALU.mult)
                    ve.tensor_tensor(h[:, TP:TOK], cv[:, TP + 2:TOK + 2], b[:, TP:TOK],
                                     ALU.mult).then_inc(h_ready, 1)
                elif kind == "down" and i == 0 and c == 0:
                    h_part(l, FT - 1)

            def merged_lo(l, i):
                dve.wait_ge(m_hi_made, n(l, i + 1, KC))
                ve.scalar_tensor_tensor(act_lo[:, i, :], merged_a[:, i % 2, :], 0.5, act_hi[:, i, :].bitcast(F32),
                                        ALU.mult, ALU.subtract).then_inc(m_split, 1)

            def norm_tile(l, kind, norm, o):
                for k in {3: (1,), 4: (2, 3)}.get(o, (o - 1,) if o > 4 else ()):
                    dve.wait_ge(squared, n(l, KC * norm + k + 1, 2 * KC))
                    if k >= FROM_SHIFTED:
                        dve.wait_ge(r_ready, n(l, KC * norm + k + 1, 2 * KC))
                    if k > 1:
                        dve.wait_ge(added, n(l, (KC - 2) * norm + k - 1, 2 * (KC - 2)))
                    ve.tensor_tensor(sum_q, gates[:, 0, :] if k == 1 else sum_q, gates[:, k, :], ALU.add)
                    ve.tensor_tensor(sum_sq, gates[:, KC, :] if k == 1 else sum_sq, gates[:, KC + k, :],
                                     ALU.add).then_inc(added, 1)
                b = tile_wait(l, (kind, o))
                if o < FROM_SHIFTED:
                    ve.scalar_tensor_tensor(gates[:, o, :], xT[:, o, :], ALPHA, b[:, 0:TOK], ALU.mult,
                                            ALU.add).then_inc(r_ready, 1)
                else:
                    dve.wait_ge(prepared, n(l, (KC - FROM_SHIFTED) * (norm + 1) - (KC - 1 - o),
                                            2 * (KC - FROM_SHIFTED)))
                    ve.tensor_tensor(gates[:, o, :], gates[:, o, :], b[:, 0:TOK], ALU.add).then_inc(r_ready, 1)
                if o == FROM_SHIFTED - 1:
                    dve.wait_ge(shift_ready, n(l, norm + 1, 2))
                    dve.wait_ge(r_ready, n(l, KC * norm + o + 1, 2 * KC))
                    first = gates[:, 0:FROM_SHIFTED, :]
                    ve.tensor_tensor(first, first, shift.unsqueeze(1).to_broadcast([P, FROM_SHIFTED, TOK]),
                                     ALU.subtract).then_inc(shifted, 1)
                if FROM_SHIFTED - 1 <= o < KC - 1:
                    ve.scalar_tensor_tensor(gates[:, o + 1, :], xT[:, o + 1, :], ALPHA, shift, ALU.mult,
                                            ALU.subtract).then_inc(prepared, 1)

            def history(l, j):
                if j >= 2:
                    dve.wait_ge(conv_done, n(l, j - 1, FT))
                ve.tensor_copy(a_ext[:, j % 2, TP + 2:TP + 4],
                               par[:, P_STATE:P_STATE + 2 * FT].rearrange("p (r j) -> p r j", r=2)[:, :, j])\
                    .then_inc(history_set, 1)

            def h_part(l, j):
                dve.wait_ge(h_hi_made, n(l, j + 1, FT))
                ve.tensor_tensor(h_lo[:, j, :], hf[:, j % 2, :], h_hi[:, j, :].bitcast(F32),
                                 ALU.subtract).then_inc(h_split, 1)

            def step(l, kind, i):
                if kind == "params":
                    b, v = spare(l, ("params", 0))
                    dve.wait_ge(spare_done, v)
                    ve.tensor_copy(par[:], b[:, 0:P_ALL]).then_inc(params_ready, 1)
                    for g in range(4):
                        ve.tensor_copy(sink5[:, :, g], sinks[:, 4 * (g // 2):4 * (g // 2) + 4])
                    ve.tensor_copy(sink5[0:64, :, 4], sinks[0:64, 0:4])
                    link(ve.tensor_copy(sink5[64:P, :, 4], sinks[64:P, 4:8]))
                    dve.wait_ge(params_ready, n(l, 1, 1))
                elif kind == "cache" and i == 0:
                    b, v = spare(l, ("cache", 0))
                    dve.wait_ge(spare_done, v)
                    ve.tensor_copy(kT[:, 1:5, TOK:KEYS],
                                   b[:, 0:4 * P].rearrange("p (t c) -> p t c", t=4)).then_inc(cache_turned, 1)
                elif kind == "cache":
                    b, v = spare(l, ("cache", 1))
                    dve.wait_ge(spare_done, v)
                    ve.tensor_copy(kT[:, 0, TOK:KEYS], b[:, 0:P])
                    ve.tensor_copy(logf_c[:], b[0:NH, P:2 * P]).then_inc(cache_turned, 1)
                    dve.wait_ge(cache_turned, n(l, 2, 2))
                elif kind == "logf":
                    dve.wait_ge(log_ready, n(l, 1, 1))
                    ve.scalar_tensor_tensor(logf[:], fz[:], 0.0, fe[:], ALU.min, ALU.subtract).then_inc(logf_ready, 1)
                elif kind == "sums" and i == 0:
                    dve.wait_ge(logf_ready, n(l, 1, 1))
                    cache0 = P + TOK
                    link(ve.tensor_tensor_scan(fsum[:, P:P + TP], ones8[:], logf[:, 0:TP], 0.0, ALU.mult, ALU.add))
                    link(ve.tensor_tensor_scan(fsum[:, cache0:NF], ones8[:, 0:PAST], logf_c[:], 0.0, ALU.mult,
                                               ALU.add))
                elif kind == "sums" and i == 1:
                    cache0 = P + TOK
                    link(ve.tensor_tensor_scan(fsum[:, P + TP:cache0], ones8[:, 0:TS], logf[:, TP:TOK],
                                               fsum[:, NF - 1:NF], ALU.mult, ALU.add))
                    link(ve.tensor_copy(fsum[:, 0:P], fsum[:, P:2 * P]))
                elif kind == "sums" and i == 2:
                    link(ve.tensor_scalar(fparts[0:NH, :], fsum[:], -1.0, None, ALU.mult))
                    link(ve.scalar_tensor_tensor(fres[:], fsum[:], -1.0, fparts[0:NH, :], ALU.mult, ALU.subtract))
                elif kind == "sums":
                    link(ve.tensor_copy(fmid[:], fres[:]))
                    ve.tensor_copy(fparts[32:32 + NH, :], fmid[:])
                    link(ve.tensor_tensor(fres[:], fres[:], fmid[:], ALU.subtract))
                    ve.tensor_copy(fparts[64:64 + NH, :], fres[:]).then_inc(f_ready, 1)
                elif kind == "logft":
                    b, v = spare(l, ("logft", 0))
                    dve.wait_ge(spare_done, v)
                    dve.wait_ge(rows_free, n(l, 1, 1))
                    ve.tensor_copy(logf_t[:, 0:2, :], b[:, 0:2 * NH].rearrange("p (t h) -> p t h", t=2))
                    ve.tensor_copy(logf_t[0:TS, 2, :], b[0:TS, 2 * NH:3 * NH]).then_inc(logf_turned, 1)
                elif kind == "rope":
                    x = stage[:, 0, :] if i == 0 else qT[:, i - 1, :]
                    out = kT[:, 0, 0:TOK] if i == 0 else qT[:, i - 1, :]
                    dve.wait_ge(copied, n(l, COPIED[("ka", 0) if i == 0 else ("qa", i - 1)], N_COPIED))
                    if i > 0:
                        dve.wait_ge(roped, n(l, i, 5))
                    dve.wait_ge(tables_in, 16)
                    ve.tensor_tensor(roped_b[:], sin, swapped[:, i % 3, :], ALU.mult)
                    link(ve.tensor_tensor(roped_a[:], x, cos, ALU.mult))
                    ve.tensor_tensor(out, roped_a[:], roped_b[:], ALU.add).then_inc(roped, 1)
                elif kind == "kv":
                    b, v = spare(l, ("kv", i))
                    dve.wait_ge(spare_done, v)
                    if i == 1:
                        dve.wait_ge(masks_ready, 1)
                    ve.tensor_copy(kv[:, 0:2, i * P:(i + 1) * P], b[:, 0:2 * P].rearrange("p (t c) -> p t c", t=2))
                    ve.tensor_copy(kv[0:TS, 2, i * P:(i + 1) * P], b[0:TS, 2 * P:3 * P]).then_inc(kv_turned, 1)
                elif kind == "scores":
                    for g, (key, c0, w) in enumerate(GROUPS):
                        b, v = spare(l, (f"s{key}", i))
                        if g in (0, 2, 4):
                            dve.wait_ge(spare_done, v)
                        ins = ve.tensor_reduce(nmax[:, i, g:g + 1], b[:, c0:c0 + w], AX.X, ALU.max, negate=True)
                    if i < 4:
                        link(ins)
                        link(ve.scalar_tensor_tensor(nmax[:, i, :], sink5[:, i, :], -1.0, nmax[:, i, :], ALU.mult,
                                                     ALU.min))
                        ins = ve.tensor_tensor(sink_e[:, i, :], sink5[:, i, :], nmax[:, i, :], ALU.add)
                    ins.then_inc(max_ready, 1)
                elif kind == "soften":
                    dve.wait_ge(exp_done, n(l, 3 * i + 3, 3 * PAIRS))
                    if i < 4:
                        dve.wait_ge(sink_done, n(l, i + 1, 4))
                        link(ve.tensor_tensor(den[:, i, :], den[:, i, :], sink_e[:, i, :], ALU.add))
                    link(ve.reciprocal(rden[:, i, :], den[:, i, :]))
                    for g, (key, c0, w) in enumerate(GROUPS):
                        pr = probs[:, i % 2, 3 * P * key + c0:3 * P * key + c0 + w]
                        ins = ve.tensor_scalar(pr, pr, rden[:, i, g:g + 1], None, ALU.mult)
                    ins.then_inc(probs_ready, 1)
                elif kind == "turn":
                    if i > 0:
                        dve.wait_ge(spare_done, spare(l, ("o", i - 1))[1])
                    b, v = spare(l, ("t1", i))
                    dve.wait_ge(spare_done, v)
                    ve.tensor_copy(probs_t[:, 1, :], b[:, 0:3 * P]).then_inc(turned_dve, 1)
                elif kind == "values":
                    b, v = spare(l, ("o", i))
                    dve.wait_ge(o_hi_made, n(l, i + 1, PAIRS))
                    ve.tensor_tensor(o_lo[:, i, :], b[:, 0:TOK], o_hi[:, i, :].bitcast(F32),
                                     ALU.subtract).then_inc(o_split, 1)
                elif kind == "norm":
                    dve.wait_ge(mean_squared, n(l, i + 1, 2))
                    b, v = spare(l, ("square", i))
                    dve.wait_ge(spare_done, v)
                    ve.tensor_tensor(spread, b[:, 0:TOK], mean_sq, ALU.subtract).then_inc(var_ready, 1)

                    def centre(o):
                        ve.tensor_tensor(gates[:, o, :], gates[:, o, :], mean_q, ALU.subtract).then_inc(centred, 1)

                    dve.wait_ge(mean_copied, n(l, i + 1, 2))
                    centre(0)
                    centre(1)
                    dve.wait_ge(spread_ready, n(l, i + 1, 2))
                    link(ve.reciprocal(rstd[:], spread))
                    g0, b0 = (P_LN1G, P_LN1B) if i == 0 else (P_LN2G, P_LN2B)

                    def scale(o):
                        dve.wait_ge(centred, n(l, KC * i + o + 1, 2 * KC))
                        ve.tensor_tensor(gates[:, KC + o, :], gates[:, o, :], rstd[:], ALU.mult).then_inc(scaled, 1)

                    def lo(o):
                        dve.wait_ge(x_hi_made, KC + n(l, KC * i + o + 1, 2 * KC))
                        ve.tensor_tensor(act_lo[:, o, :], xT[:, o, :], act_hi[:, o, :].bitcast(F32),
                                         ALU.subtract).then_inc(x_split, 1)

                    def split_tiles():
                        scale(0)
                        scale(1)
                        dve.wait_ge(scaled, n(l, KC * i + 1, 2 * KC))
                        link(ve.tensor_scalar(xT[:, 0, :], gates[:, KC, :], par[:, g0:g0 + 1], par[:, b0:b0 + 1],
                                              ALU.mult, ALU.add))
                        centre(2)
                        for o in range(KC):
                            lo(o)
                            if o + 2 < KC:
                                scale(o + 2)
                            if o + 3 < KC:
                                centre(o + 3)

                    def output_tiles():
                        for o in range(KC):
                            scale(o)
                            if o + 2 < KC:
                                centre(o + 2)

                    if i == 0:
                        split_tiles()
                        lo_part(l, NORM_UNITS[0] + 4)
                    else:
                        with dve.If(l < DEPTH - 1):
                            split_tiles()
                            lo_part(l + 1, 3)
                        with dve.Else():
                            output_tiles()
                elif kind == "tails":
                    b, v = spare(l, ("tails", 0))
                    dve.wait_ge(spare_done, v)
                    dve.wait_ge(rows_free, n(l, 1, 1))
                    ve.tensor_copy(tails_t[:], b[0:4 * FT, 0:P]).then_inc(tails_turned, 1)

            dve.sem_inc(lo_made, SLOTS)
            dve.sem_inc(unit_used, SLOTS)
            dve.sem_inc(o_split, 1)
            dve.sem_inc(rows_free, 1)
            ve.memset(a_ext[:, :, 0:2], 0.0).then_inc(set_once, 1)
            ve.memset(ones8[:], 1.0).then_inc(set_once, 1)
            ve.memset(fparts[:], 0.0).then_inc(set_once, 1)
            ve.memset(eps_t[:], EPS).then_inc(set_once, 1)
            ve.memset(w_hi[:, 0, :, :].bitcast(F32), 0.0).then_inc(set_once, 1)
            for o in range(0, KC + 2, 2):
                if o < KC:
                    dve.wait_ge(spare_done, o + 1)
                    ve.tensor_copy(xT[:, o, :], bank[4 + o % 4][:, 0:TOK]).then_inc(x_copied[0], 1)
                if o == KC:
                    for copied_by in x_copied:
                        dve.wait_ge(copied_by, KC // 2)
                    dve.sem_inc(var_ready, 2)
                for k in (o - 2, o - 1) if o > 0 else ():
                    dve.wait_ge(x_hi_made, k + 1)
                    ve.tensor_tensor(act_lo[:, k, :], xT[:, k, :], act_hi[:, k, :].bitcast(F32),
                                     ALU.subtract).then_inc(x_split, 1)
                if o == KC - 2:
                    lo_part(0, 0)
            for u in range(1, SLOTS):
                lo_part(0, u)
            with dve.Fori(0, DEPTH) as l:
                dve.wait_ge(x_split, KC * (2 * l + 1))
                dve.sem_inc(gate_pass, 1)
                dve.sem_clear(dve_chain)
                chain[0] = 0
                for kind, i in SCHEDULE[TOP]:
                    step(l, kind, i)
                for u in range(NU):
                    if u == AT[("wo", 0)]:
                        merged_lo(l, KC - 1)
                    if u == NORM_UNITS[1]:
                        after(l, u)
                    if u + AHEAD >= NU:
                        with dve.If(l < DEPTH - 1):
                            lo_part(l + 1, u + AHEAD - NU)
                    elif UNITS[u + AHEAD] and u not in (0, NORM_UNITS[0], NORM_UNITS[0] + 1):
                        lo_part(l, u + AHEAD)
                    if UNITS[u] and u != NORM_UNITS[1]:
                        after(l, u)
                    if u == NORM_UNITS[0]:
                        lo_part(l, u + AHEAD)
                    for kind, i in SCHEDULE.get(u, []):
                        step(l, kind, i)

            for half in range(2):
                for t in (0, 2):
                    w = P if t < 2 else TS
                    dve.wait_ge(y_turned, 3 * half + t + 1)
                    ve.tensor_copy(y_rows[0:w, t, half * DM // 2:(half + 1) * DM // 2],
                                   Y_BANKS[3 * half + t][0:w, :]).then_inc(y_copied, 1)


OUTS = [(1, TP, DM), (1, TS, DM),
        (DEPTH, 1, 128, 2, HD), (DEPTH, 1, 128, 2, HD), (DEPTH, 1, TP, NH, HD), (DEPTH, 1, TP, NH, HD),
        (DEPTH, 1, TP, NH), (DEPTH, 1, CONV - 1, DFF),
        (DEPTH, 1, PAST, 2, HD), (DEPTH, 1, PAST, 2, HD), (DEPTH, 1, TS, NH, HD), (DEPTH, 1, TS, NH, HD),
        (DEPTH, 1, TS, NH), (DEPTH, 1, CONV - 1, DFF)]


def kernel(**inputs):
    import concourse.bacc as bacc
    from concourse.bass_utils import run_bass_kernel_spmd

    nc = bacc.Bacc("TRN2", target_bir_lowering=False, num_devices=1)
    const_f, const_b = constants()
    arrays, A, O = {}, {}, []
    for name, value in {**inputs, "const_f": const_f, "const_b": const_b}.items():
        a = np.ascontiguousarray(value)
        arrays["in_" + name] = a
        A[name] = nc.dram_tensor("in_" + name, a.shape, mybir.dt.from_np(a.dtype), kind="ExternalInput").ap()
    for k, shape in enumerate(OUTS):
        O.append(nc.dram_tensor(f"out_{k}", shape, F32, kind="ExternalOutput").ap())
    build(nc, A, O)
    r = run_bass_kernel_spmd(nc, [arrays], core_ids=[0])
    return tuple(r.results[0][f"out_{k}"] for k in range(len(OUTS)))
```
